# Optimizing a Trainium2 kernel written in Bass

```python
import jax
import jax.numpy as jnp
from jax import lax
import numpy as np

D_MODEL = 1024
BATCH = 1
SEQ = 1024
DEPTH = 2

N_EVEN = (DEPTH + 1) // 2
N_ODD = DEPTH // 2

MLA_HEADS = 8
MLA_NOPE = 64
MLA_ROPE = 32
MLA_V = 64
MLA_Q_RANK = 256
MLA_KV_RANK = 128
MLA_COLS = MLA_Q_RANK + MLA_KV_RANK + MLA_ROPE
MLA_SCALE = (MLA_NOPE + MLA_ROPE) ** -0.5
Q_BLOCK = 128

GDN_HEADS = 8
GDN_DK = 64
GDN_DV = 64
GDN_CONV = 4
GDN_CHUNK = 64
GDN_QKV = GDN_HEADS * (2 * GDN_DK + GDN_DV)
GDN_COLS = GDN_QKV + 2 * GDN_HEADS + GDN_HEADS * GDN_DV

HY_IN = MLA_COLS + GDN_COLS
HY_MIX = MLA_HEADS * MLA_V + GDN_HEADS * GDN_DV

RET_HEADS = 8
RET_DK = D_MODEL // RET_HEADS
RET_DV = 2 * D_MODEL // RET_HEADS
RET_CHUNK = 128
RET_IN = RET_HEADS * (2 * RET_DK + 2 * RET_DV)
RET_MIX = RET_HEADS * RET_DV

N_GROUPS = 4
EXPERTS_PER_GROUP = 8
N_EXPERTS = N_GROUPS * EXPERTS_PER_GROUP
TOP_K_IN_GROUP = 2
EXPERT_FF = 512
MOE_BLOCK = 128

ROPE_BASE = 10000.0
LN_EPS = 1e-5
RMS_EPS = 1e-6
DEEPNORM_ALPHA = (2.0 * DEPTH) ** 0.25
DEEPNORM_BETA = (8.0 * DEPTH) ** -0.25
N_MOD = 6

kernel_name = 'hybrid_mla_gdn_retention_hmoe_deepnorm'

def layer_norm(x, g, b):
    xf = x.astype(jnp.float32)
    mu = jnp.mean(xf, -1, keepdims=True)
    var = jnp.mean(jnp.square(xf - mu), -1, keepdims=True)
    return ((xf - mu) * lax.rsqrt(var + LN_EPS)).astype(x.dtype) * g + b

def rms_norm(x, g):
    xf = x.astype(jnp.float32)
    return (xf * lax.rsqrt(jnp.mean(xf * xf, -1, keepdims=True) + RMS_EPS)).astype(x.dtype) * g

def l2_normalize(x):
    xf = x.astype(jnp.float32)
    return (xf * lax.rsqrt(jnp.sum(xf * xf, -1, keepdims=True) + RMS_EPS)).astype(x.dtype)

def rope_tables(positions, dim):
    inv_freq = ROPE_BASE ** (-jnp.arange(0, dim, 2, dtype=jnp.float32) / dim)
    ang = positions.astype(jnp.float32)[..., None] * inv_freq
    return jnp.cos(ang), jnp.sin(ang)

def apply_rope(x, cos, sin):
    x1, x2 = jnp.split(x, 2, axis=-1)
    c = cos[:, :, None, :].astype(x.dtype)
    s = sin[:, :, None, :].astype(x.dtype)
    return jnp.concatenate([x1 * c - x2 * s, x1 * s + x2 * c], axis=-1)

def to_chunks(x, chunk):
    B, S, H, d = x.shape
    return x.reshape(B, S // chunk, chunk, H, d).transpose(0, 3, 1, 2, 4).astype(jnp.float32)

def from_chunks(x):
    B, H, N, C, d = x.shape
    return x.transpose(0, 2, 3, 1, 4).reshape(B, N * C, H, d)

def causal_attention_blocks(q, k, v):
    B, S, H, Dq = q.shape
    Dv = v.shape[-1]
    nb = S // Q_BLOCK
    qb = jnp.moveaxis(q.reshape(B, nb, Q_BLOCK, H, Dq), 1, 0)
    kpos = jnp.arange(S)

    def one_block(args):
        q_blk, blk = args
        s = jnp.einsum('bqhd,bkhd->bhqk', q_blk, k).astype(jnp.float32)
        qpos = blk * Q_BLOCK + jnp.arange(Q_BLOCK)
        s = jnp.where(kpos[None, :] <= qpos[:, None], s, -jnp.inf)
        p = jax.nn.softmax(s, axis=-1).astype(v.dtype)
        return jnp.einsum('bhqk,bkhd->bqhd', p, v)

    out = lax.map(one_block, (qb, jnp.arange(nb)))
    return jnp.moveaxis(out, 0, 1).reshape(B, S, H, Dv)

def latent_attention(h_mla, positions, q_norm, w_uq, kv_norm, w_ukv):
    B, S, _ = h_mla.shape
    q_lat, kv_lat, k_rope = jnp.split(h_mla, [MLA_Q_RANK, MLA_Q_RANK + MLA_KV_RANK], axis=-1)
    q = (rms_norm(q_lat, q_norm) @ w_uq).reshape(B, S, MLA_HEADS, MLA_NOPE + MLA_ROPE)
    kv = (rms_norm(kv_lat, kv_norm) @ w_ukv).reshape(B, S, MLA_HEADS, MLA_NOPE + MLA_V)
    q_nope, q_rope = jnp.split(q, [MLA_NOPE], axis=-1)
    k_nope, v = jnp.split(kv, [MLA_NOPE], axis=-1)
    cos, sin = rope_tables(positions, MLA_ROPE)
    q_rope = apply_rope(q_rope, cos, sin)
    k_rope = jnp.broadcast_to(apply_rope(k_rope[:, :, None, :], cos, sin), (B, S, MLA_HEADS, MLA_ROPE))
    q = jnp.concatenate([q_nope, q_rope], axis=-1) * MLA_SCALE
    k = jnp.concatenate([k_nope, k_rope], axis=-1)
    o = causal_attention_blocks(q, k, v)
    return o.reshape(B, S, MLA_HEADS * MLA_V)

def causal_depthwise_conv(x, w):
    K = w.shape[0]
    return lax.conv_general_dilated(x, w[:, None, :].astype(x.dtype), window_strides=(1,), padding=[(K - 1, 0)],
                                    dimension_numbers=('NWC', 'WIO', 'NWC'), feature_group_count=x.shape[-1])

def chunk_gated_delta_rule(q, k, v, log_alpha, beta):
    B, S, H, DK = q.shape
    DV = v.shape[-1]
    C = GDN_CHUNK
    N = S // C
    qc, kc, vc = (to_chunks(t, C) for t in (q, k, v))
    bc = beta.reshape(B, N, C, H).transpose(0, 3, 1, 2).astype(jnp.float32)
    g = jnp.cumsum(log_alpha.reshape(B, N, C, H).transpose(0, 3, 1, 2), axis=-1)
    tril = jnp.tril(jnp.ones((C, C), bool))
    strict = jnp.tril(jnp.ones((C, C), bool), -1)
    gdiff = g[..., :, None] - g[..., None, :]
    decay = jnp.where(tril, jnp.exp(jnp.where(tril, gdiff, 0.0)), 0.0)
    kb = kc * bc[..., None]
    L = jnp.where(strict, jnp.einsum('bhnid,bhnjd->bhnij', kb, kc) * decay, 0.0)
    eye = jnp.eye(C, dtype=jnp.float32)
    T = lax.linalg.triangular_solve(eye + L, jnp.broadcast_to(eye, L.shape), left_side=True, lower=True)
    u = jnp.einsum('bhnij,bhnje->bhnie', T, vc * bc[..., None])
    w = jnp.einsum('bhnij,bhnjd->bhnid', T, kb * jnp.exp(g)[..., None])
    a_intra = jnp.where(tril, jnp.einsum('bhnid,bhnjd->bhnij', qc, kc) * decay, 0.0)

    def step(state, xs):
        q_i, k_i, u_i, w_i, g_i, a_i = xs
        v_new = u_i - jnp.einsum('bhcd,bhde->bhce', w_i, state)
        o_i = jnp.einsum('bhcd,bhde->bhce', q_i * jnp.exp(g_i)[..., None], state) + jnp.einsum('bhij,bhje->bhie', a_i, v_new)
        g_last = g_i[..., -1]
        k_dec = k_i * jnp.exp(g_last[..., None] - g_i)[..., None]
        state = state * jnp.exp(g_last)[..., None, None] + jnp.einsum('bhcd,bhce->bhde', k_dec, v_new)
        return state, o_i

    state0 = jnp.zeros((B, H, DK, DV), jnp.float32)
    xs = tuple(jnp.moveaxis(t, 2, 0) for t in (qc, kc, u, w, g, a_intra))
    _, o = lax.scan(step, state0, xs)
    return from_chunks(jnp.moveaxis(o, 0, 2)).astype(v.dtype)

def gated_deltanet(h_gdn, conv_w, a_log, dt_bias, o_norm):
    B, S, _ = h_gdn.shape
    qkv, a, b, gate = jnp.split(h_gdn, [GDN_QKV, GDN_QKV + GDN_HEADS, GDN_QKV + 2 * GDN_HEADS], axis=-1)
    qkv = jax.nn.silu(causal_depthwise_conv(qkv, conv_w))
    q, k, v = jnp.split(qkv, [GDN_HEADS * GDN_DK, 2 * GDN_HEADS * GDN_DK], axis=-1)
    q = l2_normalize(q.reshape(B, S, GDN_HEADS, GDN_DK)) * (GDN_DK ** -0.5)
    k = l2_normalize(k.reshape(B, S, GDN_HEADS, GDN_DK))
    v = v.reshape(B, S, GDN_HEADS, GDN_DV)
    beta = jax.nn.sigmoid(b.astype(jnp.float32))
    log_alpha = -jnp.exp(a_log.astype(jnp.float32)) * jax.nn.softplus(a.astype(jnp.float32) + dt_bias.astype(jnp.float32))
    o = chunk_gated_delta_rule(q, k, v, log_alpha, beta)
    o = rms_norm(o, o_norm) * jax.nn.silu(gate.reshape(B, S, GDN_HEADS, GDN_DV))
    return o.reshape(B, S, GDN_HEADS * GDN_DV)

def mla_gdn_mixer(h, positions, w_in, q_norm, w_uq, kv_norm, w_ukv, conv_w, a_log, dt_bias, o_norm, w_out):
    proj = h @ w_in
    h_mla, h_gdn = jnp.split(proj, [MLA_COLS], axis=-1)
    y_mla = latent_attention(h_mla, positions, q_norm, w_uq, kv_norm, w_ukv)
    y_gdn = gated_deltanet(h_gdn, conv_w, a_log, dt_bias, o_norm)
    return jnp.concatenate([y_mla, y_gdn], axis=-1) @ w_out

def chunkwise_retention(q, k, v):
    B, S, H, DK = q.shape
    DV = v.shape[-1]
    C = RET_CHUNK
    log_gamma = jnp.log(1.0 - 2.0 ** (-5.0 - jnp.arange(H, dtype=jnp.float32)))
    idx = jnp.arange(C, dtype=jnp.float32)
    diff = idx[:, None] - idx[None, :]
    causal = diff >= 0
    decay = jnp.where(causal, jnp.exp(jnp.where(causal, diff, 0.0) * log_gamma[:, None, None]), 0.0)
    cross_decay = jnp.exp((idx + 1.0) * log_gamma[:, None])
    key_decay = jnp.exp((C - 1.0 - idx) * log_gamma[:, None])
    chunk_decay = jnp.exp(C * log_gamma)
    qc, kc, vc = (to_chunks(t, C) for t in (q, k, v))
    scores = jnp.einsum('bhnid,bhnjd->bhnij', qc, kc) * decay[None, :, None]
    inner = jnp.einsum('bhnij,bhnje->bhnie', scores, vc)

    def step(state, xs):
        q_i, k_i, v_i = xs
        o_cross = jnp.einsum('bhcd,bhde->bhce', q_i, state) * cross_decay[None, :, :, None]
        state = state * chunk_decay[None, :, None, None] + jnp.einsum('bhcd,bhce->bhde', k_i * key_decay[None, :, :, None], v_i)
        return state, o_cross

    state0 = jnp.zeros((B, H, DK, DV), jnp.float32)
    xs = tuple(jnp.moveaxis(t, 2, 0) for t in (qc, kc, vc))
    _, cross = lax.scan(step, state0, xs)
    return from_chunks(inner + jnp.moveaxis(cross, 0, 2)).astype(v.dtype)

def retention_mixer(h, positions, w_in, gn_g, gn_b, w_out):
    B, S, _ = h.shape
    proj = h @ w_in
    q, k, v, gate = jnp.split(proj, [RET_HEADS * RET_DK, 2 * RET_HEADS * RET_DK, 2 * RET_HEADS * RET_DK + RET_MIX], axis=-1)
    cos, sin = rope_tables(positions, RET_DK)
    q = apply_rope(q.reshape(B, S, RET_HEADS, RET_DK), cos, sin) * (RET_DK ** -0.5)
    k = apply_rope(k.reshape(B, S, RET_HEADS, RET_DK), cos, sin)
    v = v.reshape(B, S, RET_HEADS, RET_DV)
    o = chunkwise_retention(q, k, v)
    o = layer_norm(o, gn_g.reshape(RET_HEADS, RET_DV), gn_b.reshape(RET_HEADS, RET_DV))
    return (jax.nn.silu(gate) * o.reshape(B, S, RET_MIX)) @ w_out

def routed_experts(xt, expert_id, weights, w_gate, w_up, w_down):
    T, D = xt.shape
    K = expert_id.shape[1]
    n = T * K
    flat_e = expert_id.reshape(n).astype(jnp.int32)
    flat_tok = jnp.repeat(jnp.arange(T, dtype=jnp.int32), K)
    flat_w = weights.reshape(n)
    order = jnp.argsort(flat_e)
    e_sorted = flat_e[order]
    tok_sorted = flat_tok[order]
    w_sorted = flat_w[order]
    counts = jnp.zeros((N_EXPERTS,), jnp.int32).at[flat_e].add(1)
    padded = (counts + MOE_BLOCK - 1) // MOE_BLOCK * MOE_BLOCK
    start = jnp.cumsum(counts) - counts
    pstart = jnp.cumsum(padded) - padded
    slot = pstart[e_sorted] + (jnp.arange(n, dtype=jnp.int32) - start[e_sorted])
    n_blocks = n // MOE_BLOCK + N_EXPERTS
    n_slots = n_blocks * MOE_BLOCK
    slot_tok = jnp.zeros((n_slots,), jnp.int32).at[slot].set(tok_sorted)
    block_start = jnp.arange(n_blocks, dtype=jnp.int32) * MOE_BLOCK
    block_expert = jnp.minimum(jnp.searchsorted(jnp.cumsum(padded), block_start, side='right'), N_EXPERTS - 1)
    xb = xt[slot_tok].reshape(n_blocks, MOE_BLOCK, D)

    def expert_block(args):
        xs, e = args
        hid = jax.nn.silu(xs @ w_gate[e]) * (xs @ w_up[e])
        return hid @ w_down[e]

    yb = lax.map(expert_block, (xb, block_expert)).reshape(n_slots, D)
    contrib = yb[slot] * w_sorted[:, None].astype(yb.dtype)
    return jax.ops.segment_sum(contrib, tok_sorted, num_segments=T)

def hierarchical_moe(h, w_group, b_group, w_expert, b_expert, w_gate, w_up, w_down):
    B, S, D = h.shape
    T = B * S
    xt = h.reshape(T, D)
    g_prob = jax.nn.softmax((xt @ w_group + b_group).astype(jnp.float32), axis=-1)
    g_top, g_idx = lax.top_k(g_prob, 1)
    e_logits_all = (xt @ w_expert + b_expert).astype(jnp.float32).reshape(T, N_GROUPS, EXPERTS_PER_GROUP)
    e_logits = jnp.take_along_axis(e_logits_all, g_idx[:, :, None], axis=1)[:, 0]
    e_top, e_idx = lax.top_k(e_logits, TOP_K_IN_GROUP)
    e_w = jax.nn.softmax(e_top, axis=-1)
    weights = g_top * e_w
    expert_id = g_idx * EXPERTS_PER_GROUP + e_idx
    y = routed_experts(xt, expert_id, weights, w_gate, w_up, w_down)
    return y.reshape(B, S, D)

def setup_inputs(seed: int = 0) -> dict:
    key = jax.random.key(seed)
    ks = iter(jax.random.split(key, 40))
    f32 = jnp.float32

    def nrm(shape, scale):
        return scale * jax.random.normal(next(ks), shape, f32)

    def gain(shape):
        return 1.0 + 0.01 * jax.random.normal(next(ks), shape, f32)

    x = nrm((BATCH, SEQ, D_MODEL), 1.0)
    c = nrm((BATCH, D_MODEL), 1.0)
    positions = jax.random.randint(next(ks), (BATCH, 1), 0, 1024, jnp.int32) + jnp.arange(SEQ, dtype=jnp.int32)[None, :]
    ada_w = nrm((DEPTH, D_MODEL, N_MOD * D_MODEL), 0.1 * D_MODEL ** -0.5)
    ada_b = nrm((DEPTH, N_MOD * D_MODEL), 0.01)
    ln_mix_g = gain((DEPTH, D_MODEL))
    ln_mix_b = nrm((DEPTH, D_MODEL), 0.01)
    ln_ffn_g = gain((DEPTH, D_MODEL))
    ln_ffn_b = nrm((DEPTH, D_MODEL), 0.01)
    hy_w_in = nrm((N_EVEN, D_MODEL, HY_IN), D_MODEL ** -0.5)
    mla_q_norm = gain((N_EVEN, MLA_Q_RANK))
    mla_w_uq = nrm((N_EVEN, MLA_Q_RANK, MLA_HEADS * (MLA_NOPE + MLA_ROPE)), MLA_Q_RANK ** -0.5)
    mla_kv_norm = gain((N_EVEN, MLA_KV_RANK))
    mla_w_ukv = nrm((N_EVEN, MLA_KV_RANK, MLA_HEADS * (MLA_NOPE + MLA_V)), MLA_KV_RANK ** -0.5)
    gdn_conv_w = nrm((N_EVEN, GDN_CONV, GDN_QKV), GDN_CONV ** -0.5)
    gdn_a_log = jnp.log(jax.random.uniform(next(ks), (N_EVEN, GDN_HEADS), f32, 1.0, 16.0))
    dt = jnp.exp(jnp.log(1e-3) + jax.random.uniform(next(ks), (N_EVEN, GDN_HEADS), f32) * (jnp.log(1e-1) - jnp.log(1e-3)))
    gdn_dt_bias = dt + jnp.log(-jnp.expm1(-dt))
    gdn_norm = gain((N_EVEN, GDN_DV))
    hy_w_out = nrm((N_EVEN, HY_MIX, D_MODEL), DEEPNORM_BETA * HY_MIX ** -0.5)
    ret_w_in = nrm((N_ODD, D_MODEL, RET_IN), D_MODEL ** -0.5)
    ret_gn_g = gain((N_ODD, RET_MIX))
    ret_gn_b = nrm((N_ODD, RET_MIX), 0.01)
    ret_w_out = nrm((N_ODD, RET_MIX, D_MODEL), DEEPNORM_BETA * RET_MIX ** -0.5)
    moe_w_group = nrm((DEPTH, D_MODEL, N_GROUPS), D_MODEL ** -0.5)
    moe_b_group = nrm((DEPTH, N_GROUPS), 0.01)
    moe_w_expert = nrm((DEPTH, D_MODEL, N_EXPERTS), D_MODEL ** -0.5)
    moe_b_expert = nrm((DEPTH, N_EXPERTS), 0.01)
    moe_w_gate = nrm((DEPTH, N_EXPERTS, D_MODEL, EXPERT_FF), D_MODEL ** -0.5)
    moe_w_up = nrm((DEPTH, N_EXPERTS, D_MODEL, EXPERT_FF), D_MODEL ** -0.5)
    moe_w_down = nrm((DEPTH, N_EXPERTS, EXPERT_FF, D_MODEL), DEEPNORM_BETA * EXPERT_FF ** -0.5)
    return {'x': x, 'c': c, 'positions': positions, 'ada_w': ada_w, 'ada_b': ada_b,
            'ln_mix_g': ln_mix_g, 'ln_mix_b': ln_mix_b, 'ln_ffn_g': ln_ffn_g, 'ln_ffn_b': ln_ffn_b,
            'hy_w_in': hy_w_in, 'mla_q_norm': mla_q_norm, 'mla_w_uq': mla_w_uq, 'mla_kv_norm': mla_kv_norm,
            'mla_w_ukv': mla_w_ukv, 'gdn_conv_w': gdn_conv_w, 'gdn_a_log': gdn_a_log, 'gdn_dt_bias': gdn_dt_bias,
            'gdn_norm': gdn_norm, 'hy_w_out': hy_w_out, 'ret_w_in': ret_w_in, 'ret_gn_g': ret_gn_g,
            'ret_gn_b': ret_gn_b, 'ret_w_out': ret_w_out, 'moe_w_group': moe_w_group, 'moe_b_group': moe_b_group,
            'moe_w_expert': moe_w_expert, 'moe_b_expert': moe_b_expert, 'moe_w_gate': moe_w_gate,
            'moe_w_up': moe_w_up, 'moe_w_down': moe_w_down}

def reference(x, c, positions, ada_w, ada_b, ln_mix_g, ln_mix_b, ln_ffn_g, ln_ffn_b,
              hy_w_in, mla_q_norm, mla_w_uq, mla_kv_norm, mla_w_ukv, gdn_conv_w, gdn_a_log, gdn_dt_bias,
              gdn_norm, hy_w_out, ret_w_in, ret_gn_g, ret_gn_b, ret_w_out, moe_w_group, moe_b_group,
              moe_w_expert, moe_b_expert, moe_w_gate, moe_w_up, moe_w_down):
    c_act = jax.nn.silu(c)
    for layer in range(DEPTH):
        mod = (c_act @ ada_w[layer] + ada_b[layer])[:, None, :]
        sh_m, sc_m, gt_m, sh_f, sc_f, gt_f = jnp.split(mod, N_MOD, axis=-1)
        h = x * (1.0 + sc_m) + sh_m
        i = layer // 2
        if layer % 2 == 0:
            y = mla_gdn_mixer(h, positions, hy_w_in[i], mla_q_norm[i], mla_w_uq[i], mla_kv_norm[i], mla_w_ukv[i],
                              gdn_conv_w[i], gdn_a_log[i], gdn_dt_bias[i], gdn_norm[i], hy_w_out[i])
        else:
            y = retention_mixer(h, positions, ret_w_in[i], ret_gn_g[i], ret_gn_b[i], ret_w_out[i])
        x = layer_norm(DEEPNORM_ALPHA * x + (1.0 + gt_m) * y, ln_mix_g[layer], ln_mix_b[layer])
        h = x * (1.0 + sc_f) + sh_f
        y = hierarchical_moe(h, moe_w_group[layer], moe_b_group[layer], moe_w_expert[layer], moe_b_expert[layer],
                             moe_w_gate[layer], moe_w_up[layer], moe_w_down[layer])
        x = layer_norm(DEEPNORM_ALPHA * x + (1.0 + gt_f) * y, ln_ffn_g[layer], ln_ffn_b[layer])
    return x


_drawn_inputs = setup_inputs


def setup_inputs(seed=0):
    import zlib

    import numpy as np

    out = dict(_drawn_inputs(seed))
    spreads = {}
    factors = {'ada_b': 3.415,
     'ln_mix_g': 2.709,
     'ln_mix_b': 2.81,
     'ln_ffn_g': 3.516,
     'ln_ffn_b': 3.518,
     'mla_q_norm': 8.0,
     'mla_kv_norm': 8.0,
     'gdn_a_log': 2.795,
     'gdn_norm': 8.0,
     'ret_gn_g': 8.0,
     'ret_gn_b': 8.0,
     'moe_b_group': 8.0,
     'moe_b_expert': 8.0}
    for name, (base, spread) in spreads.items():
        noise = np.random.default_rng([zlib.crc32(name.encode()), seed]).standard_normal(out[name].shape)
        drawn = base * np.exp(spread * noise) if base else spread * noise
        out[name] = jnp.asarray(drawn.astype(out[name].dtype))
    for name, factor in factors.items():
        out[name] = (out[name] * factor).astype(out[name].dtype)
    return out
```

```python
import math
from contextlib import ExitStack

import numpy as np

import concourse.bass as bass
from concourse import mybir
from concourse.alu_op_type import AluOpType as ALU

P = 128
D = 1024
T = 1024
NT = T // P
KD = D // P
DEPTH = 2
NMOD = 6
ALPHA = (2.0 * DEPTH) ** 0.25
LN_EPS = 1e-5
RMS_EPS = 1e-6
NEG = -1.0e30

HEADS = 8
QR, KVR, ROPE, NOPE, VD = 256, 128, 32, 64, 64
QD = NOPE + ROPE
MLA_COLS = QR + KVR + ROPE
MLA_SCALE = QD ** -0.5
GD = 64
CONV = 4
QKV = HEADS * 3 * GD
CT = QKV // P
HY_IN = MLA_COLS + QKV + 2 * HEADS + HEADS * GD

RDK, RDV = 128, 256
RET_MIX = HEADS * RDV

NG, EPG = 4, 8
NE = NG * EPG
FF = 512
PAIRS = 2 * T
NBLK = PAIRS // P + NE
NFREQ = RDK // 2
PE_BANKS = 7
DVE_BANKS = NMOD * D // 512 - PE_BANKS
DVE_COLS = DVE_BANKS * 512

F32 = mybir.dt.float32
I32 = mybir.dt.int32
U32 = mybir.dt.uint32
ACT = mybir.ActivationFunctionType
AX = mybir.AxisListType


class Chain:

    def __init__(self, eng, sem, base=0):
        self.eng, self.sem, self.base, self.n = eng, sem, base, 0

    def mark(self, ins):
        ins.then_inc(self.sem, 1)
        self.n += 1

    def do(self, ins):
        self.mark(ins)
        self.eng.wait_ge(self.sem, self.base + self.n)


class Program:
    def __init__(self, nc, io):
        self.nc, self.io = nc, io
        self.keep = ExitStack()
        self.ns = 0

    def sb(self, ctx, name, shape, dt=F32):
        return ctx.enter_context(self.nc.sbuf_tensor(name, shape, dt))

    def ps(self, ctx, name, shape, dt=F32):
        return ctx.enter_context(self.nc.psum_tensor(name, shape, dt))

    def sems(self, ctx, tag, *names):
        got = [self.nc.alloc_semaphore(f"{tag}_{n}") for n in names]

        def release():
            self.nc.clear_and_free_semaphores(got)
            self.nc.all_engine_barrier()

        ctx.callback(release)
        return got


def constants(g):
    nc, io = g.nc, g.io
    k = g.keep
    g.ident = g.sb(k, "ident", [P, P])
    g.ones = g.sb(k, "ones", [P, P])
    g.upto = g.sb(k, "upto", [P, P])
    g.before = g.sb(k, "before", [P, P])
    g.future = g.sb(k, "future", [P, P])
    g.futureT = g.sb(k, "futureT", [P, P])
    g.cos = g.sb(k, "cos", [P, NT, NFREQ])
    g.sin = g.sb(k, "sin", [P, NT, NFREQ])
    g.cols = g.sb(k, "cols", [P, P])
    g.convw = g.sb(k, "convw", [P, CONV, CT])
    g.mod = g.sb(k, "mod", [P, DEPTH, NMOD, KD])
    NV = DEPTH * NMOD * KD
    with ExitStack() as ctx:
        rows = g.sb(ctx, "rows", [P, P])
        crow = g.sb(ctx, "crow", [CONV * CT, P])
        pos_i = g.sb(ctx, "pos_i", [P, NT], I32)
        pos = g.sb(ctx, "pos", [P, NT])
        freq = g.sb(ctx, "freq", [P, NFREQ])
        ang = g.sb(ctx, "ang", [P, NT, NFREQ])
        turn = g.sb(ctx, "turn", [P, NT, NFREQ])
        turn_i = g.sb(ctx, "turn_i", [P, NT, NFREQ], I32)
        cact = g.sb(ctx, "cact", [P, KD])
        wada = [g.sb(ctx, f"wada{i}", [P, NMOD * D]) for i in range(4)]
        modrow = g.sb(ctx, "modrow", [1, NMOD * D])
        modrows = g.sb(ctx, "modrows", [DEPTH * NMOD * KD, P])
        part = g.sb(ctx, "part", [P, DVE_COLS])
        pv = g.ps(ctx, "pv", [P, 512])
        pm = [g.ps(ctx, f"pm{i}", [1, 512]) for i in range(PE_BANKS)]
        (vec_in, pos_in, consts, posf, angs, rope_arg, ropes, turned, colsok, cactok, made, added,
         freqs, parts, summed, taken, mod_out, mod_in, modT) = g.sems(
            ctx, "c", "vec_in", "pos_in", "consts", "posf", "angs", "rope_arg", "ropes", "turned", "colsok", "cactok",
            "made", "added", "freqs", "parts", "summed", "taken", "mod_out", "mod_in", "modT")
        w_in = g.sems(ctx, "c", *[f"w_in{i}" for i in range(4)])
        mod_dram = nc.dram_tensor("mod_dram", [DEPTH * NMOD * KD, P], F32).ap()
        block = ctx.enter_context(nc.Block())
        ada_rows = io["ada_w"].rearrange("l (k p) n -> (l k) p n", p=P)

        @block.sync
        def _(sp):
            sp.dma_start(rows[0:NV, :], io["ada_b"].rearrange("l (n p) -> (l n) p", p=P)).then_inc(vec_in, 16)
            sp.dma_start(rows[NV:NV + KD, :], io["c"].rearrange("b (k p) -> (b k) p", p=P)).then_inc(vec_in, 16)
            sp.dma_start(rows[NV + KD:NV + KD + 2, :],
                         io["mla_q_norm"].rearrange("a (k p) -> (a k) p", p=P)).then_inc(vec_in, 16)
            sp.dma_start(rows[NV + KD + 2:NV + KD + 3, :], io["mla_kv_norm"]).then_inc(vec_in, 16)
            sp.dma_start(crow[:, :], io["gdn_conv_w"].rearrange("a j (m p) -> (a j m) p", p=P)).then_inc(vec_in, 16)
            for i in range(DEPTH * KD):
                if i >= 4:
                    sp.wait_ge(made, i - 3)
                    sp.wait_ge(parts, i - 3)
                sp.dma_start(wada[i % 4][:, :], ada_rows[i]).then_inc(w_in[i % 4], 16)

        @block.gpsimd
        def _(pool):
            with nc.allow_non_contiguous_dma(reason="1024 positions, once"):
                pool.dma_start(pos_i[:, :], io["positions"].rearrange("b (t p) -> p (b t)", p=P)).then_inc(pos_in, 16)
            ch = Chain(pool, consts)
            ch.mark(pool.memset(g.ident[:, :], 0.0))
            ch.mark(pool.memset(g.ones[:, :], 1.0))
            ch.mark(pool.memset(g.future[:, :], 0.0))
            ch.do(pool.memset(g.futureT[:, :], 0.0))
            ch.mark(pool.affine_select(out=g.ident[:, :], in_=g.ident[:, :], compare_op=ALU.not_equal, fill=1.0,
                                       base=0, pattern=[[-1, P]], channel_multiplier=1))
            ch.mark(pool.affine_select(out=g.upto[:, :], in_=g.ones[:, :], compare_op=ALU.is_ge, fill=0.0,
                                       base=0, pattern=[[1, P]], channel_multiplier=-1))
            ch.mark(pool.affine_select(out=g.before[:, :], in_=g.ones[:, :], compare_op=ALU.is_gt, fill=0.0,
                                       base=0, pattern=[[1, P]], channel_multiplier=-1))
            ch.mark(pool.affine_select(out=g.future[:, :], in_=g.future[:, :], compare_op=ALU.is_ge, fill=NEG,
                                       base=0, pattern=[[1, P]], channel_multiplier=-1))
            ch.do(pool.affine_select(out=g.futureT[:, :], in_=g.futureT[:, :], compare_op=ALU.is_ge, fill=NEG,
                                     base=0, pattern=[[-1, P]], channel_multiplier=1))
            inv = 1.0 / (np.float32(10000.0) ** (np.arange(NFREQ, dtype=np.float32) / np.float32(NFREQ)))
            for i in range(NFREQ):
                pool.memset(freq[:, i:i + 1], float(inv[i])).then_inc(freqs, 1)

        @block.tensor
        def _(pe):
            pe.wait_ge(consts, 9)
            pe.wait_ge(vec_in, 5 * 16)
            pe.transpose(pv[:, 0:NV + KD + 3], rows[0:NV + KD + 3, :], g.ident[0:NV + KD + 3, 0:NV + KD + 3])\
                .then_inc(turned, 1)
            pe.transpose(pv[:, P:P + CONV * CT], crow[:, :], g.ident[0:CONV * CT, 0:CONV * CT]).then_inc(turned, 1)
            pe.wait_ge(cactok, 1)
            for i in range(DEPTH * KD):
                layer, kk = i // KD, i % KD
                pe.wait_ge(w_in[i % 4], 16 * (i // 4 + 1))
                if i == KD:
                    pe.wait_ge(taken, PE_BANKS + DVE_BANKS)
                for n in range(PE_BANKS):
                    mm = pe.matmul(pm[n][:, :], cact[:, kk:kk + 1], wada[i % 4][:, n * 512:(n + 1) * 512],
                                   start=(kk == 0), stop=(kk == KD - 1))
                mm.then_inc(made, 1)
                if kk == KD - 1:
                    pe.wait_ge(parts, i + 1)
                    for n in range(DVE_BANKS):
                        pe.wait_ge(taken, layer * (PE_BANKS + DVE_BANKS) + PE_BANKS)
                        mm = pe.matmul(pm[n][:, :], g.ones[:, 0:1], part[:, n * 512:(n + 1) * 512],
                                       start=True, stop=True)
                    mm.then_inc(summed, 1)
            pe.wait_ge(mod_in, 16)
            pe.transpose(pv[:, 256:256 + NV], modrows[:, :], g.ident[0:NV, 0:NV]).then_inc(modT, 1)

        TWO_PI = 2.0 * math.pi
        C1 = 6.28125
        C2 = float(np.float32(TWO_PI - C1))
        C3 = float(TWO_PI - C1 - C2)

        @block.vector
        def _(dve):
            dve.wait_ge(turned, 2)
            dve.tensor_copy(g.cols[:, 0:NV + KD + 3], pv[:, 0:NV + KD + 3]).then_inc(colsok, 1)
            dve.tensor_copy(g.convw[:, :, :], pv[:, P:P + CONV * CT]).then_inc(colsok, 1)
            dve.wait_ge(pos_in, 16)
            ch = Chain(dve, angs)
            ch.do(dve.tensor_copy(pos[:, :], pos_i[:, :]))
            dve.wait_ge(freqs, NFREQ)
            for t in range(NT):
                ch.mark(dve.tensor_scalar(ang[:, t, :], freq[:, :], pos[:, t:t + 1], None, ALU.mult))
            dve.wait_ge(angs, ch.n)
            for out, quarter, n in ((g.sin, 0.0, 0), (g.cos, 0.25, 1)):
                ch.do(dve.tensor_scalar(turn[:, :, :], ang[:, :, :], 1.0 / TWO_PI, quarter, ALU.mult, ALU.add))
                ch.do(dve.tensor_copy(turn_i[:, :, :], turn[:, :, :]))
                ch.do(dve.tensor_copy(turn[:, :, :], turn_i[:, :, :]))
                ch.do(dve.scalar_tensor_tensor(out=out[:, :, :], in0=turn[:, :, :], scalar=-C1, in1=ang[:, :, :],
                                               op0=ALU.mult, op1=ALU.add))
                for less in (C2, C3):
                    ch.do(dve.scalar_tensor_tensor(out=out[:, :, :], in0=turn[:, :, :], scalar=-less,
                                                   in1=out[:, :, :], op0=ALU.mult, op1=ALU.add))
                ch.do(dve.tensor_scalar(out[:, :, :], out[:, :, :], math.pi / 2 * n, 3.1415925, ALU.add, ALU.min))
                dve.tensor_scalar(out[:, :, :], out[:, :, :], -3.1415925, None, ALU.max).then_inc(rope_arg, 1)
            ch = Chain(dve, parts)
            dve.wait_ge(cactok, 1)
            at = PE_BANKS * 512
            for i in range(DEPTH * KD):
                layer, kk = i // KD, i % KD
                dve.wait_ge(w_in[i % 4], 16 * (i // 4 + 1))
                if kk == 0:
                    if layer:
                        dve.wait_ge(summed, layer)
                    ch.do(dve.tensor_scalar(part[:, :], wada[i % 4][:, at:], cact[:, kk:kk + 1], None, ALU.mult))
                else:
                    ch.do(dve.scalar_tensor_tensor(out=part[:, :], in0=wada[i % 4][:, at:],
                                                   scalar=cact[:, kk:kk + 1], in1=part[:, :],
                                                   op0=ALU.mult, op1=ALU.add))
            dve.wait_ge(modT, 1)
            dve.wait_ge(colsok, 2)
            dve.tensor_tensor(g.mod[:, :, :, :].rearrange("p l m k -> p (l m k)"), pv[:, 256:256 + NV],
                              g.cols[:, 0:NV], ALU.add).then_inc(added, 1)
            dve.wait_ge(added, 1)
            for m in (1, 2, 4, 5):
                dve.tensor_scalar(g.mod[:, :, m, :], g.mod[:, :, m, :], 1.0, None, ALU.add).then_inc(added, 1)

        @block.scalar
        def _(act):
            act.wait_ge(colsok, 1)
            act.activation(cact[:, :], g.cols[:, NV:NV + KD], ACT.Silu).then_inc(cactok, 1)
            for n, table in enumerate((g.sin, g.cos)):
                act.wait_ge(rope_arg, n + 1)
                act.activation(table[:, :, :], table[:, :, :], ACT.Sin).then_inc(ropes, 1)
            for layer in range(DEPTH):
                act.wait_ge(made, KD * (layer + 1))
                if layer:
                    act.wait_ge(mod_out, 16 * layer)
                for n in range(PE_BANKS):
                    act.copy(modrow[:, n * 512:(n + 1) * 512], pm[n][:, :]).then_inc(taken, 1)
                act.wait_ge(summed, layer + 1)
                for n in range(DVE_BANKS):
                    m = PE_BANKS + n
                    act.copy(modrow[:, m * 512:(m + 1) * 512], pm[n][:, :]).then_inc(taken, 1)
                act.wait_ge(taken, (layer + 1) * (PE_BANKS + DVE_BANKS))
                act.dma_start(mod_dram[layer * NMOD * KD:(layer + 1) * NMOD * KD, :],
                              modrow[:, :].rearrange("a (n p) -> a n p", p=P)).then_inc(mod_out, 16)
            act.wait_ge(mod_out, 16 * DEPTH)
            act.dma_start(modrows[:, :], mod_dram).then_inc(mod_in, 16)
    g.qnorm = g.cols[:, NV + KD:NV + KD + 2]
    g.kvnorm = g.cols[:, NV + KD + 2:NV + KD + 3]


def modulate(g, tag, x_dram, layer, which):
    nc = g.nc
    with ExitStack() as ctx:
        xin = g.sb(ctx, f"{tag}_xin", [P, 4, D])
        pt = [g.ps(ctx, f"{tag}_pt{i}", [P, 512]) for i in range(4)]
        turned, *outs = g.sems(ctx, tag, "turned", "act_out", "dve_out")
        x_in = g.sems(ctx, tag, *[f"x_in{i}" for i in range(4)])
        block = ctx.enter_context(nc.Block())
        shift, scale = g.mod[:, layer, 3 * which, :], g.mod[:, layer, 3 * which + 1, :]

        @block.sync
        def _(sp):
            for t in range(NT):
                if t >= 4:
                    sp.wait_ge(turned, 2 * (t - 4) + 2)
                sp.dma_start(xin[:, t % 4, :], x_dram[t * P:(t + 1) * P, :]).then_inc(x_in[t % 4], 16)

        @block.tensor
        def _(pe):
            for t in range(NT):
                pe.wait_ge(x_in[t % 4], 16 * (t // 4 + 1))
                for half in range(2):
                    n = 2 * t + half
                    if n >= 4:
                        pe.wait_ge(outs[half], t - 1)
                    for j in range(4):
                        kk = 4 * half + j
                        mm = pe.transpose(pt[n % 4][:, j * P:(j + 1) * P], xin[:, t % 4, kk * P:(kk + 1) * P],
                                          g.ident[:, :])
                    mm.then_inc(turned, 1)

        def take(eng, half, out):
            for t in range(NT):
                n = 2 * t + half
                eng.wait_ge(turned, n + 1)
                for j in range(4):
                    kk = 4 * half + j
                    dst, src = g.hT[:, kk, t * P:(t + 1) * P], pt[n % 4][:, j * P:(j + 1) * P]
                    if half == 0:
                        ins = eng.activation(dst, src, ACT.Identity, bias=shift[:, kk:kk + 1],
                                             scale=scale[:, kk:kk + 1])
                    else:
                        ins = eng.tensor_scalar(dst, src, scale[:, kk:kk + 1], shift[:, kk:kk + 1],
                                                ALU.mult, ALU.add)
                ins.then_inc(out, 1)

        @block.scalar
        def _(act):
            take(nc.scalar, 0, outs[0])

        @block.vector
        def _(dve):
            take(nc.vector, 1, outs[1])



def bc(ap, shape):
    return ap.to_broadcast(list(shape))


def gdn_convolve(g, qkvT):
    nc, io = g.nc, g.io
    w_dram = io["hy_w_in"][0].rearrange("(k p) n -> p k n", p=P)
    with ExitStack() as ctx:
        w = [g.sb(ctx, f"gc_w{u}", [P, KD, P]) for u in range(2)]
        acc = [g.sb(ctx, f"gc_acc{u}", [P, T]) for u in range(2)]
        pq = [g.ps(ctx, f"gc_pq{u}", [P, T]) for u in range(2)]
        proj, taps = g.sems(ctx, "gc", "proj", "taps")
        convd = g.sems(ctx, "gc", "convd0", "convd1")
        silud = g.sems(ctx, "gc", "silud0", "silud1")
        w_in = g.sems(ctx, "gc", "w_in0", "w_in1")
        block = ctx.enter_context(nc.Block())

        @block.sync
        def _(sp):
            for u in range(2):
                sp.dma_start(w[u][:, :, :], w_dram[:, :, MLA_COLS + u * P:MLA_COLS + (u + 1) * P]).then_inc(w_in[u], 16)
            with sp.Fori(0, CT // 2 - 1) as i:
                for u in range(2):
                    sp.wait_ge(proj, i * 2 + (u + 1))
                    sp.dma_start(w[u][:, :, :], w_dram[:, :, bass.ds(i * (2 * P) + (MLA_COLS + (u + 2) * P), P)])\
                        .then_inc(w_in[u], 16)

        @block.tensor
        def _(pe):
            with pe.Fori(0, CT // 2) as i:
                for u in range(2):
                    pe.wait_ge(w_in[u], i * 16 + 16)
                    pe.wait_ge(convd[u], i)
                    for half in range(2):
                        for kk in range(KD):
                            mm = pe.matmul(pq[u][:, half * 512:(half + 1) * 512], w[u][:, kk, :],
                                           g.hT[:, kk, half * 512:(half + 1) * 512],
                                           start=(kk == 0), stop=(kk == KD - 1))
                    mm.then_inc(proj, 1)

        convw = g.convw[:, :, :].rearrange("p j (m u) -> p j m u", u=2)

        @block.vector
        def _(dve):
            with dve.Fori(0, CT // 2) as i:
                ch = Chain(dve, taps, i * (2 * (CONV - 1)))
                for u in range(2):
                    dve.wait_ge(proj, i * 2 + (u + 1))
                    dve.wait_ge(silud[u], i)
                    x, a = pq[u], acc[u]
                    ch.do(dve.tensor_scalar(a[:, :], x[:, :], convw[:, CONV - 1, bass.ds(i, 1), u], None, ALU.mult))
                    for back in range(1, CONV):
                        ins = dve.scalar_tensor_tensor(out=a[:, back:], in0=x[:, 0:T - back],
                                                       scalar=convw[:, CONV - 1 - back, bass.ds(i, 1), u],
                                                       in1=a[:, back:], op0=ALU.mult, op1=ALU.add)
                        if back < CONV - 1:
                            ch.do(ins)
                        else:
                            ins.then_inc(convd[u], 1)

        @block.scalar
        def _(act):
            with act.Fori(0, CT // 2) as i:
                for u in range(2):
                    act.wait_ge(convd[u], i + 1)
                    act.activation(qkvT[:, bass.ds(i * 2 + u, 1), :].rearrange("p a t -> p (a t)"), acc[u][:, :],
                                   ACT.Silu).then_inc(silud[u], 1)


def hybrid_inputs(g, o):
    nc, io = g.nc, g.io
    w_dram = io["hy_w_in"][0].rearrange("(k p) n -> p k n", p=P)
    ab0 = MLA_COLS + QKV
    gate0 = ab0 + 2 * HEADS
    NA = MLA_COLS + 2 * HEADS
    GW = HEADS * GD
    HR = ROPE // 2
    with ExitStack() as ctx:
        wa = g.sb(ctx, "hi_wa", [P, KD, NA])
        wg = g.sb(ctx, "hi_wg", [P, KD, GW])
        wq = g.sb(ctx, "hi_wq", [P, 2, HEADS * QD])
        wv = g.sb(ctx, "hi_wv", [P, HEADS, NOPE + VD])
        lat = g.sb(ctx, "hi_lat", [P, NT, NA])
        latT = o.latT
        junk = g.sb(ctx, "hi_junk", [P, QR])
        ss = g.sb(ctx, "hi_ss", [P, NT, 2])
        rs = g.sb(ctx, "hi_rs", [P, NT, 2])
        kr = g.sb(ctx, "hi_kr", [P, NT, ROPE])
        tmp = [g.sb(ctx, f"hi_tmp{i}", [P, NT, HR]) for i in range(2)]
        qt = [g.sb(ctx, f"hi_qt{i}", [P, HEADS, HR]) for i in range(2)]
        pa = [g.ps(ctx, f"hi_pa{i}", [P, 512]) for i in range(2)]
        pg = [g.ps(ctx, f"hi_pg{i}", [P, 512]) for i in range(2)]
        pq = [g.ps(ctx, f"hi_pq{i}", [P, 1024]) for i in range(2)]
        (w_in, w2_in, proj, gated, copied, squared, msd, rsd, lnd, scaled, roped, latTd, latTok, krTd, krTok, vd, vok,
         qd, qrope) = g.sems(
            ctx, "hi", "w_in", "w2_in", "proj", "gated", "copied", "squared", "msd", "rsd", "lnd", "scaled", "roped",
            "latTd", "latTok", "krTd", "krTok", "vd", "vok", "qd", "qrope")
        block = ctx.enter_context(nc.Block())
        GROUPS = [(part, half) for half in range(2) for part in range(3)]

        @block.sync
        def _(sp):
            sp.dma_start(wa[:, :, 0:MLA_COLS], w_dram[:, :, 0:MLA_COLS]).then_inc(w_in, 16)
            sp.dma_start(wa[:, :, MLA_COLS:NA], w_dram[:, :, ab0:gate0]).then_inc(w_in, 16)
            sp.dma_start(wg[:, :, :], w_dram[:, :, gate0:HY_IN]).then_inc(w_in, 16)
            sp.dma_start(wq[:, :, :], io["mla_w_uq"][0].rearrange("(k p) n -> p k n", p=P)).then_inc(w2_in, 16)
            sp.dma_start(wv[:, :, :], io["mla_w_ukv"][0].rearrange("p (h n) -> p h n", h=HEADS)).then_inc(w2_in, 16)

        @block.tensor
        def _(pe):
            pe.wait_ge(w_in, 3 * 16)
            for t in range(NT):
                b = t % 2
                if t >= 2:
                    pe.wait_ge(copied, t - 1)
                    pe.wait_ge(gated, t - 1)
                for kk in range(KD):
                    pe.matmul(pa[b][:, 0:NA], g.hT[:, kk, t * P:(t + 1) * P], wa[:, kk, :],
                              start=(kk == 0), stop=(kk == KD - 1))
                for kk in range(KD):
                    mm = pe.matmul(pg[b][:, :], g.hT[:, kk, t * P:(t + 1) * P], wg[:, kk, :],
                                   start=(kk == 0), stop=(kk == KD - 1))
                mm.then_inc(proj, 1)
            pe.wait_ge(copied, NT)
            pe.wait_ge(gated, NT)
            for n, (part, half) in enumerate(GROUPS):
                pe.wait_ge(scaled, 2 * NT)
                if n >= 2:
                    pe.wait_ge(latTok, n - 1)
                for j in range(4):
                    t = 4 * half + j
                    mm = pe.transpose(pa[n % 2][:, j * P:(j + 1) * P], lat[:, t, part * P:(part + 1) * P], g.ident[:, :])
                mm.then_inc(latTd, 1)
            pe.wait_ge(roped, 6)
            for half in range(2):
                for j in range(4):
                    t = 4 * half + j
                    mm = pe.transpose(pg[half][0:ROPE, j * P:(j + 1) * P], kr[:, t, :], g.ident[:, :])
                mm.then_inc(krTd, 1)
            pe.wait_ge(latTok, len(GROUPS))
            pe.wait_ge(krTok, 2)
            pe.wait_ge(w2_in, 2 * 16)
            for t in range(NT):
                b = t % 2
                if t >= 2:
                    pe.wait_ge(vok, t - 1)
                    pe.wait_ge(qrope, 14 * (t - 1))
                pe.matmul(pa[b][:, :], latT[:, 2, t * P:(t + 1) * P], wv[:, :, NOPE:NOPE + VD],
                          start=True, stop=True).then_inc(vd, 1)
                for c0, c1 in ((0, 480), (480, 768)):
                    at = 0 if c0 == 0 else 512
                    for kk in range(2):
                        mm = pe.matmul(pq[b][:, at:at + c1 - c0], latT[:, kk, t * P:(t + 1) * P], wq[:, kk, c0:c1],
                                       start=(kk == 0), stop=(kk == 1))
                mm.then_inc(qd, 1)

        @block.scalar
        def _(act):
            for t in range(NT):
                act.wait_ge(proj, t + 1)
                act.activation(o.gate[:, t, :], pg[t % 2][:, :], ACT.Silu).then_inc(gated, 1)
            for t in range(NT):
                act.wait_ge(copied, t + 1)
                for j, (a, b) in enumerate(((0, QR), (QR, QR + KVR))):
                    if j or t:
                        act.wait_ge(squared, 2 * t + j)
                    act.activation(junk[:, 0:b - a], lat[:, t, a:b], ACT.Square,
                                   accum_out=ss[:, t, j:j + 1]).then_inc(squared, 1)
            act.wait_ge(msd, 2)
            act.activation(rs[:, :, :], ss[:, :, :], ACT.Ln).then_inc(lnd, 1)
            act.wait_ge(lnd, 1)
            act.activation(rs[:, :, :], rs[:, :, :], ACT.Exp, scale=-0.5).then_inc(rsd, 1)
            for n, (part, half) in enumerate(GROUPS):
                act.wait_ge(latTd, n + 1)
                gain = g.qnorm[:, part:part + 1] if part < 2 else g.kvnorm
                act.activation(latT[:, part, half * 512:(half + 1) * 512], pa[n % 2][:, :], ACT.Copy,
                               scale=gain).then_inc(latTok, 1)
            for half in range(2):
                act.wait_ge(krTd, half + 1)
                act.copy(o.krT[:, half * 512:(half + 1) * 512], pg[half][0:ROPE, :]).then_inc(krTok, 1)
            for t in range(NT):
                act.wait_ge(vd, t + 1)
                act.copy(o.v[:, t, :], pa[t % 2][:, :]).then_inc(vok, 1)

        @block.vector
        def _(dve):
            for t in range(NT):
                dve.wait_ge(proj, t + 1)
                dve.tensor_copy(lat[:, t, :], pa[t % 2][:, 0:NA]).then_inc(copied, 1)
            dve.wait_ge(copied, NT)
            dve.tensor_copy(o.ab[:, :, :], lat[:, :, MLA_COLS:NA])
            dve.wait_ge(squared, 2 * NT)
            for j, n in enumerate((QR, KVR)):
                dve.tensor_scalar(ss[:, :, j], ss[:, :, j], 1.0 / n, RMS_EPS, ALU.mult, ALU.add).then_inc(msd, 1)

            def rope(ch, out1, out2, x1, x2, cos, sin, ta, tb):
                ch.mark(dve.tensor_tensor(ta, x1, cos, ALU.mult))
                ch.do(dve.tensor_tensor(tb, x2, sin, ALU.mult))
                ch.do(dve.tensor_tensor(out1, ta, tb, ALU.subtract))
                ch.mark(dve.tensor_tensor(ta, x1, sin, ALU.mult))
                ch.do(dve.tensor_tensor(tb, x2, cos, ALU.mult))
                ch.do(dve.tensor_tensor(out2, ta, tb, ALU.add))

            k0 = QR + KVR
            rope(Chain(dve, roped), kr[:, :, 0:HR], kr[:, :, HR:ROPE], lat[:, :, k0:k0 + HR],
                 lat[:, :, k0 + HR:k0 + ROPE], g.cos[:, :, 0:NFREQ:4], g.sin[:, :, 0:NFREQ:4],
                 tmp[0][:, :, :], tmp[1][:, :, :])
            dve.wait_ge(rsd, 1)
            for t in range(NT):
                for j, (a, b) in enumerate(((0, QR), (QR, QR + KVR))):
                    dve.tensor_scalar(lat[:, t, a:b], lat[:, t, a:b], rs[:, t, j:j + 1], None, ALU.mult)\
                        .then_inc(scaled, 1)
            ch = Chain(dve, qrope)
            for t in range(NT):
                dve.wait_ge(qd, t + 1)
                for c0, heads in ((0, range(0, 5)), (512, range(5, 8))):
                    n = len(heads)
                    src = pq[t % 2][:, c0:c0 + n * QD].rearrange("p (h d) -> p h d", d=QD)
                    dst = o.q[:, t, heads[0]:heads[0] + n, :]
                    cos = bc(g.cos[:, t, 0:NFREQ:4].unsqueeze(1), [P, n, HR])
                    sin = bc(g.sin[:, t, 0:NFREQ:4].unsqueeze(1), [P, n, HR])
                    last = Chain(dve, qrope, ch.n)
                    rope(last, dst[:, :, NOPE:NOPE + HR], dst[:, :, NOPE + HR:QD], src[:, :, NOPE:NOPE + HR],
                         src[:, :, NOPE + HR:QD], cos, sin, qt[0][:, 0:n, :], qt[1][:, 0:n, :])
                    ch.n += last.n
                    ch.do(dve.tensor_copy(dst[:, :, 0:NOPE], src[:, :, 0:NOPE]))


def attention(g, o):
    nc, io = g.nc, g.io
    NB = T // P
    ITEMS = [(u, i) for u in range(2) for i in range(NB)]
    HALVES = [(n, b) for n, (u, i) in enumerate(ITEMS) for b in range(i // 4 + 1)]
    NI, NH = len(ITEMS), len(HALVES)
    upto_item = [sum(1 for m, _ in HALVES if m <= n) for n in range(NI)]
    with ExitStack() as ctx:
        wk_all = g.sb(ctx, "at_wk_all", [P, HEADS, NOPE])
        wk = [g.sb(ctx, f"at_wk{u}", [P, NOPE]) for u in range(2)]
        qs = [g.sb(ctx, f"at_qs{u}", [P, NT, QD]) for u in range(2)]
        qT = [g.sb(ctx, f"at_qT{u}", [QD, T]) for u in range(2)]
        kT = [g.sb(ctx, f"at_kT{u}", [QD, T]) for u in range(2)]
        p = [g.sb(ctx, f"at_p{u}", [P, T]) for u in range(2)]
        pT = [g.sb(ctx, f"at_pT{u}", [P, NB, P]) for u in range(2)]
        otok = g.sb(ctx, "at_o", [P, NT, 2 * VD])
        nmax = g.sb(ctx, "at_nmax", [P, NI])
        tot = g.sb(ctx, "at_tot", [P, NI])
        inv = g.sb(ctx, "at_inv", [P, NI])
        sc = [g.ps(ctx, f"at_s{u}", [P, T]) for u in range(2)]
        pt = [g.ps(ctx, f"at_pt{u}", [P, 512]) for u in range(2)]
        po = [g.ps(ctx, f"at_po{u}", [P, 512]) for u in range(2)]
        (w_in, krok, staged, kd, qd, kok, qok, scored, maxed, probs, turned, pTok, pv, topd, invd, normed, oTd, oTok) = g.sems(
            ctx, "at", "w_in", "krok", "staged", "kd", "qd", "kok", "qok", "scored", "maxed", "probs", "turned", "pTok",
            "pv", "topd", "invd", "normed", "oTd", "oTok")
        block = ctx.enter_context(nc.Block())
        PAIR = HEADS // 2

        @block.sync
        def _(sp):
            sp.dma_start(wk_all[:, :, :], io["mla_w_ukv"][0].rearrange("p (h n) -> p h n", h=HEADS)[:, :, 0:NOPE])\
                .then_inc(w_in, 16)

        @block.gpsimd
        def _(pool):
            pool.wait_ge(w_in, 16)
            with pool.Fori(0, PAIR) as m:
                for u in range(2):
                    pool.wait_ge(kd, m * 2)
                    pool.wait_ge(qd, m * 2)
                    qp = o.q[:, :, :, :].rearrange("p t (m u) d -> p t m u d", u=2)
                    wp = wk_all[:, :, :].rearrange("p (m u) d -> p m u d", u=2)
                    pool.tensor_copy(qs[u][:, :, :], qp[:, :, bass.ds(m, 1), u, :].rearrange("p t a d -> p t (a d)"))\
                        .then_inc(staged, 1)
                    pool.tensor_copy(wk[u][:, :], wp[:, bass.ds(m, 1), u, :].rearrange("p a d -> p (a d)"))\
                        .then_inc(staged, 1)

        @block.tensor
        def _(pe):
            def scores(m, n):
                u, i = ITEMS[n]
                s = sc[n % 2]
                pe.wait_ge(probs, m * NI + max(n - 1, 0))
                end = (i + 1) * P
                for c0 in range(0, end, 512):
                    c1 = min(c0 + 512, end)
                    pe.matmul(s[:, c0:c1], qT[u][:, i * P:end], kT[u][:, c0:c1], start=True, stop=(c1 < end))
                pe.matmul(s[:, i * P:end], g.ident[:, :], g.futureT[:, :], start=False, stop=True).then_inc(scored, 1)

            def values(m, n):
                u, i = ITEMS[n]
                for b in range(i // 4 + 1):
                    h = HALVES.index((n, b))
                    pe.wait_ge(probs, m * NI + n + 1)
                    pe.wait_ge(pTok, m * NH + max(h - 1, 0))
                    for j in range(4 * b, min(4 * b + 4, i + 1)):
                        mm = pe.transpose(pt[h % 2][:, (j - 4 * b) * P:(j - 4 * b + 1) * P],
                                          p[n % 2][:, j * P:(j + 1) * P], g.ident[:, :])
                    mm.then_inc(turned, 1)
                pe.wait_ge(normed, m * NI + max(n - 1, 0))
                pe.wait_ge(pTok, m * NH + upto_item[n])
                for j in range(i + 1):
                    mm = pe.matmul(po[n % 2][:, 0:VD], pT[n % 2][:, j, :], o.v[:, j, bass.ds(m * (2 * VD) + u * VD, VD)],
                                   start=(j == 0), stop=(j == i))
                mm.then_inc(pv, 1)

            pe.wait_ge(krok, 2)
            with pe.Fori(0, PAIR) as m:
                for u in range(2):
                    pe.wait_ge(staged, m * 4 + (2 * u + 2))
                    pe.wait_ge(probs, m * NI)
                    pe.wait_ge(oTok, m)
                    pe.wait_ge(kok, m * 2 + u)
                    for c in range(2):
                        mm = pe.matmul(sc[0][0:NOPE, c * 512:(c + 1) * 512], wk[u][:, :],
                                       o.latT[:, 2, c * 512:(c + 1) * 512], start=True, stop=True)
                    mm.then_inc(kd, 1)
                    pe.wait_ge(qok, m * 2 + u)
                    for t in range(NT):
                        mm = pe.transpose(sc[1][0:QD, t * P:(t + 1) * P], qs[u][:, t, :], g.ident[:, :])
                    mm.then_inc(qd, 1)
                pe.wait_ge(kok, m * 2 + 2)
                pe.wait_ge(qok, m * 2 + 2)
                scores(m, 0)
                for n in range(NI):
                    if n + 1 < NI:
                        scores(m, n + 1)
                    values(m, n)
                pe.wait_ge(normed, m * NI + NI)
                for t in range(NT):
                    mm = pe.transpose(sc[0][:, t * P:(t + 1) * P], otok[:, t, :], g.ident[:, :])
                mm.then_inc(oTd, 1)

        @block.scalar
        def _(act):
            for u in range(2):
                act.copy(kT[u][NOPE:QD, :], o.krT[:, :]).then_inc(krok, 1)
            with act.Fori(0, PAIR) as m:
                for u in range(2):
                    act.wait_ge(kd, m * 2 + (u + 1))
                    act.copy(kT[u][0:NOPE, :], sc[0][0:NOPE, :]).then_inc(kok, 1)
                for n, (u, i) in enumerate(ITEMS):
                    act.wait_ge(maxed, m * NI + n + 1)
                    act.wait_ge(turned, m * NH + (upto_item[n - 2] if n >= 2 else 0))
                    act.activation(p[n % 2][:, 0:(i + 1) * P], sc[n % 2][:, 0:(i + 1) * P], ACT.Exp,
                                   bias=nmax[:, n:n + 1], scale=MLA_SCALE, accum_out=tot[:, n:n + 1]).then_inc(probs, 1)
                act.wait_ge(oTd, m + 1)
                act.copy(o.mixT[:, bass.ds(m, 1), :].rearrange("p a t -> p (a t)"), sc[0][:, :]).then_inc(oTok, 1)

        @block.vector
        def _(dve):
            def top(m, n):
                u, i = ITEMS[n]
                dve.wait_ge(scored, m * NI + n + 1)
                dve.tensor_reduce(tot[:, n:n + 1], sc[n % 2][:, 0:(i + 1) * P], AX.X, ALU.max).then_inc(topd, 1)
                dve.wait_ge(topd, m * NI + n + 1)
                dve.tensor_scalar(nmax[:, n:n + 1], tot[:, n:n + 1], -MLA_SCALE, None, ALU.mult).then_inc(maxed, 1)

            with dve.Fori(0, PAIR) as m:
                for u in range(2):
                    dve.wait_ge(qd, m * 2 + (u + 1))
                    dve.tensor_copy(qT[u][:, :], sc[1][0:QD, :]).then_inc(qok, 1)
                top(m, 0)
                for n, (u, i) in enumerate(ITEMS):
                    for b in range(i // 4 + 1):
                        h = HALVES.index((n, b))
                        nb = min(4, i + 1 - 4 * b)
                        dve.wait_ge(turned, m * NH + h + 1)
                        dve.wait_ge(pv, m * NI + max(n - 1, 0))
                        dve.tensor_copy(pT[n % 2][:, 4 * b:4 * b + nb, :].rearrange("p j q -> p (j q)"),
                                        pt[h % 2][:, 0:nb * P]).then_inc(pTok, 1)
                    if n + 1 < NI:
                        top(m, n + 1)
                    dve.wait_ge(probs, m * NI + n + 1)
                    dve.reciprocal(inv[:, n:n + 1], tot[:, n:n + 1]).then_inc(invd, 1)
                    dve.wait_ge(invd, m * NI + n + 1)
                    dve.wait_ge(pv, m * NI + n + 1)
                    dve.wait_ge(oTd, m)
                    dve.tensor_scalar(otok[:, i, u * VD:(u + 1) * VD], po[n % 2][:, 0:VD], inv[:, n:n + 1], None,
                                      ALU.mult).then_inc(normed, 1)


def delta_rule(g, o, qkvT):
    nc, io = g.nc, g.io
    H, C = HEADS, P
    LEVELS = 7
    W = H * GD
    with ExitStack() as ctx:
        sb = lambda name, shape, dt=F32: g.sb(ctx, "dr_" + name, shape, dt)
        dtb = sb("dtb", [P, H])
        alog = sb("alog", [P, H])
        onorm = sb("onorm", [P, GD])
        sp1 = sb("sp1", [P, NT, H])
        sp2 = sb("sp2", [P, NT, H])
        sp3 = sb("sp3", [P, NT, H])
        la = sb("la", [P, NT, H])
        beta = sb("beta", [P, NT, H])
        level = sb("level", [P, LEVELS, C])
        raw = sb("raw", [P, CT, C])
        lac = sb("lac", [P, H])
        sq = sb("sq", [P, 2 * W])
        ssq = sb("ssq", [P, 2 * H])
        rn = sb("rn", [P, 2 * H])
        qn, kn, kb, kbg, kdec, vb = (sb(n, [P, H, GD]) for n in ("qn", "kn", "kb", "kbg", "kdec", "vb"))
        qT, kT, kbT = (sb(n, [P, H // 2, C]) for n in ("qT", "kT", "kbT"))
        dec = [sb(f"dec{i}", [P, 4, C]) for i in range(2)]
        gtmp = [sb(f"gtmp{i}", [P, 4, C]) for i in range(2)]
        gcol = sb("gcol", [P, H])
        eg = sb("eg", [P, H])
        egl = sb("egl", [P, H // 2])
        LT = [sb(f"LT{i}", [P, 4, C]) for i in range(2)]
        AT = [sb(f"AT{i}", [P, 4, C]) for i in range(2)]
        LM = [[sb(f"LM{i}_{b}", [P, 4, C]) for b in range(2)] for i in range(2)]
        Pm = [sb(f"Pm{i}", [P, 4, C]) for i in range(2)]
        Tm = [sb(f"Tm{i}", [P, 4, C]) for i in range(2)]
        Sm = [sb(f"Sm{i}", [P, 4, C]) for i in range(2)]
        wT = sb("wT", [P, H // 2, C])
        vn = sb("vn", [P, H, GD])
        state = sb("state", [P, H // 2, GD])
        osb = sb("osb", [P, H, GD])
        oss = sb("oss", [P, H])
        ors = sb("ors", [P, H])
        bank = [g.ps(ctx, f"dr_b{i}", [P, 512]) for i in range(8)]
        names = ("vec_in masks pre_a pre_b pre_c pre_d ones_state rawc rawT sqd ssqd lnr rnd qnd knd kbd kbgd kdecd vbd lacd gb gdiag "
                 "gcold gsub decd egd egld tT qTd kTd kbTd ltm ltd atm atd lmd pm pd wm tmd smd um wTm wTd vnm vn0 vnd "
                 "om tmp1 oq od kvm std osq ossd ors1 ors2 yd yT mixd").split()
        S = dict(zip(names, g.sems(ctx, "dr", *names)))
        block = ctx.enter_context(nc.Block())

        def w4(ap):
            return ap.rearrange("p (h d) -> p h d", d=GD)

        def m4(ap):
            return ap.rearrange("p (h c) -> p h c", c=C)

        def col(ap, n, d):
            return bc(ap.unsqueeze(2), [P, n, d])

        @block.sync
        def _(sp):
            sp.dma_start(dtb[:, :], io["gdn_dt_bias"].partition_broadcast(P)).then_inc(S["vec_in"], 16)
            sp.dma_start(alog[:, :], io["gdn_a_log"].partition_broadcast(P)).then_inc(S["vec_in"], 16)
            sp.dma_start(onorm[:, :], io["gdn_norm"].partition_broadcast(P)).then_inc(S["vec_in"], 16)

        @block.gpsimd
        def _(pool):
            ch = Chain(pool, S["masks"])
            for s_ in range(LEVELS):
                n = 2 ** s_
                m = level[:, s_, :].rearrange("p (b e i) -> p b e i", e=2, i=n)
                ch.do(pool.memset(level[:, s_, :], 0.0))
                ch.do(pool.memset(m[:, :, 1, :], 1.0))
                odd = m[:, :, 1, :]
                ch.do(pool.affine_select(out=odd, in_=odd, compare_op=ALU.is_ge, fill=0.0, base=0,
                                         pattern=[[-2 * n, C // (2 * n)], [0, n]], channel_multiplier=1))
                ch.do(pool.affine_select(out=odd, in_=odd, compare_op=ALU.is_gt, fill=0.0, base=n,
                                         pattern=[[2 * n, C // (2 * n)], [0, n]], channel_multiplier=-1))
            ch.do(pool.memset(state[:, :, :], 0.0))
            pool.wait_ge(S["vec_in"], 48)
            for t in range(NT):
                gt = w4(o.gate[:, t, :])
                ch.do(pool.tensor_tensor(gt, gt, bc(onorm[:, :].unsqueeze(1), [P, H, GD]), ALU.mult))
            pool.wait_ge(S["pre_d"], 1)
            with pool.Fori(0, NT) as n:
                pool.wait_ge(S["rawT"], n * 3)
                pool.tensor_copy(raw[:, :, :], qkvT[:, :, bass.ds(n * C, C)]).then_inc(S["rawc"], 1)
                pool.wait_ge(S["gb"], n * 2)
                pool.tensor_copy(lac[:, :], la[:, bass.ds(n, 1), :].rearrange("p a h -> p (a h)"))\
                    .then_inc(S["lacd"], 1)
                pool.wait_ge(S["kbd"], n + 1)
                pool.wait_ge(S["egd"], n + 1)
                pool.wait_ge(S["wTm"], n)
                pool.tensor_tensor(kbg[:, :, :], kb[:, :, :], col(eg[:, :], H, GD), ALU.mult).then_inc(S["kbgd"], 1)
                pool.wait_ge(S["decd"], n * 2 + 2)
                pool.wait_ge(S["kvm"], n)
                for i in range(2):
                    pool.tensor_tensor(kdec[:, i::2, :], kn[:, i::2, :],
                                       bc(dec[i][:, :, C - 1:C], [P, 4, GD]), ALU.mult).then_inc(S["kdecd"], 1)
                for s_ in range(LEVELS):
                    for i in range(2):
                        pool.wait_ge(S["ltd"], n * 2 + i + 1)
                        if s_ >= 2:
                            pool.wait_ge(S["pm"], n * (2 * LEVELS) + 2 * (s_ - 2) + i + 1)
                            if s_ == 2:
                                pool.wait_ge(S["smd"], n * (2 * LEVELS) + i + 1)
                        else:
                            pool.wait_ge(S["pm"], n * (2 * LEVELS))
                        pool.tensor_tensor(LM[i][s_ % 2][:, :, :], LT[i][:, :, :],
                                           bc(level[:, s_, :].unsqueeze(1), [P, 4, C]), ALU.mult).then_inc(S["lmd"], 1)
                pool.wait_ge(S["vnm"], n + 1)
                pool.wait_ge(S["om"], n + 1)
                pool.wait_ge(S["egld"], n * 2 + 2)
                pool.wait_ge(S["std"], n)
                pool.tensor_tensor(state[:, :, :], state[:, :, :], col(egl[:, :], H // 2, GD), ALU.mult)\
                    .then_inc(S["ones_state"], 1)

        @block.tensor
        def _(pe):
            wait = lambda name, v: pe.wait_ge(S[name], v)

            def part(h):
                return slice(64 * (h % 2), 64 * (h % 2) + 64)

            wait("masks", 4 * LEVELS + 1 + NT)
            wait("pre_d", 1)
            with pe.Fori(0, NT) as n:
                wait("rawc", n + 1)
                wait("mixd", n)
                wait("std", n)
                for j in range(3):
                    for m in range(4):
                        mm = pe.transpose(bank[j][:, m * C:(m + 1) * C], raw[:, 4 * j + m, :], g.ident[:, :])
                    mm.then_inc(S["rawT"], 1)
                wait("lacd", n + 1)
                for i in range(2):
                    b = bank[3 + i]
                    pe.matmul(b[:, :], g.ident[:, :], bc(g.future[:, :].unsqueeze(1), [P, 4, C]), start=True, stop=False)
                    for hh in range(4):
                        h = 2 * hh + i
                        mm = pe.matmul(b[:, hh * C:(hh + 1) * C], bc(lac[:, h:h + 1], [P, C]), g.upto[:, :],
                                       start=False, stop=(hh == 3))
                    mm.then_inc(S["gb"], 1)
                for j, (src, ready) in enumerate(((qn, "qnd"), (kn, "knd"), (kb, "kbd"))):
                    wait(ready, n + 1)
                    wait("vbd", n + 1)
                    for m in range(4):
                        mm = pe.transpose(bank[j][:, m * C:(m + 1) * C],
                                          src[:, 2 * m:2 * m + 2, :].rearrange("p h d -> p (h d)"), g.ident[:, :])
                    mm.then_inc(S["tT"], 1)
                wait("kTd", n + 1)
                wait("kbTd", n + 1)
                wait("decd", n * 2 + 2)
                for i in range(2):
                    for hh in range(4):
                        h = 2 * hh + i
                        mm = pe.matmul(bank[3 + i][:, hh * C:(hh + 1) * C], kT[part(h), h // 2, :], kbT[part(h), h // 2, :],
                                       start=True, stop=True)
                    mm.then_inc(S["ltm"], 1)
                wait("qTd", n + 1)
                for i in range(2):
                    for hh in range(4):
                        h = 2 * hh + i
                        mm = pe.matmul(bank[6 + i][:, hh * C:(hh + 1) * C], kT[part(h), h // 2, :], qT[part(h), h // 2, :],
                                       start=True, stop=True)
                    mm.then_inc(S["atm"], 1)
                for s_ in range(LEVELS):
                    for i in range(2):
                        wait("lmd", n * (2 * LEVELS) + 2 * s_ + i + 1)
                        wait("ltd", n * 2 + 2)
                        if s_:
                            wait("tmd", n * (2 * LEVELS - 2) + 2 * (s_ - 1) + i + 1)
                        for hh in range(4):
                            rhs = Tm[i][:, hh, :] if s_ else g.ident[:, :]
                            mm = pe.matmul(bank[i][:, hh * C:(hh + 1) * C], LM[i][s_ % 2][:, hh, :], rhs,
                                           start=True, stop=True)
                        mm.then_inc(S["pm"], 1)
                    if s_ == 0:
                        continue
                    for i in range(2):
                        wait("smd", n * (2 * LEVELS) + 2 * (s_ - 1) + i + 1)
                        wait("pd", n * (2 * LEVELS - 2) + 2 * (s_ - 1) + i + 1)
                        if s_ < LEVELS - 1:
                            for hh in range(4):
                                pe.matmul(bank[2 + i][:, hh * C:(hh + 1) * C], Sm[i][:, hh, :], Pm[i][:, hh, :],
                                          start=True, stop=True)
                        for hh in range(4):
                            mm = pe.matmul(bank[4 + i][:, hh * C:(hh + 1) * C], Pm[i][:, hh, :], Sm[i][:, hh, :],
                                           start=True, stop=True)
                        mm.then_inc(S["wm"], 1)
                wait("smd", n * (2 * LEVELS) + 2 * LEVELS)
                wait("kbgd", n + 1)
                for h in range(H):
                    mm = pe.matmul(bank[0][part(h), (h // 2) * C:(h // 2 + 1) * C], kbg[:, h, :],
                                   Sm[h % 2][:, h // 2, :], start=True, stop=True, skip_group_check=True)
                mm.then_inc(S["wTm"], 1)
                wait("atd", n * 2 + 2)
                for h in range(H):
                    pe.matmul(bank[1 + h % 2][:, h // 2 * GD:(h // 2 + 1) * GD], Sm[h % 2][:, h // 2, :], vb[:, h, :],
                              start=(h < 2), stop=False, skip_group_check=True)
                wait("wTd", n + 1)
                for h in range(H):
                    mm = pe.matmul(bank[1 + h % 2][:, h // 2 * GD:(h // 2 + 1) * GD], wT[part(h), h // 2, :],
                                   state[part(h), h // 2, :], start=False, stop=True, skip_group_check=True)
                mm.then_inc(S["vnm"], 1)
                for h in range(H):
                    mm = pe.matmul(bank[3 + 3 * (h % 2)][:, h // 2 * GD:(h // 2 + 1) * GD], qT[part(h), h // 2, :],
                                   state[part(h), h // 2, :], start=True, stop=True)
                wait("vn0", n + 1)
                wait("vnd", n + 1)
                for h in range(H):
                    mm = pe.matmul(bank[4 + 3 * (h % 2)][:, h // 2 * GD:(h // 2 + 1) * GD], AT[h % 2][:, h // 2, :],
                                   vn[:, h, :], start=True, stop=True)
                mm.then_inc(S["om"], 1)
                wait("kdecd", n * 2 + 2)
                for h in range(H):
                    mm = pe.matmul(bank[5][part(h), (h // 2) * GD:(h // 2 + 1) * GD], kdec[:, h, :], vn[:, h, :],
                                   start=True, stop=True, skip_group_check=True)
                mm.then_inc(S["kvm"], 1)
                wait("yd", n * 2 + 2)
                for m in range(4):
                    mm = pe.transpose(bank[0][:, m * C:(m + 1) * C],
                                      osb[:, 2 * m:2 * m + 2, :].rearrange("p h d -> p (h d)"), g.ident[:, :])
                mm.then_inc(S["yT"], 1)

        @block.scalar
        def _(act):
            wait = lambda name, v: act.wait_ge(S[name], v)
            ch = Chain(act, S["pre_a"])
            wait("pre_b", 1)
            ch.do(act.activation(sp2[:, :, :], sp2[:, :, :], ACT.Exp))
            ch.do(act.activation(beta[:, :, :], beta[:, :, :], ACT.Exp))
            ch.do(act.activation(alog[:, :], alog[:, :], ACT.Exp))
            ch.do(act.activation(sp3[:, :, :], sp2[:, :, :], ACT.Ln, bias=1.0))
            with act.Fori(0, NT) as n:
                for j in range(2):
                    wait("rawT", n * 3 + j + 1)
                    wait("ssqd", n)
                    act.activation(sq[:, j * W:(j + 1) * W], bank[j][:, :], ACT.Square).then_inc(S["sqd"], 1)
                wait("ssqd", n + 1)
                act.activation(rn[:, :], ssq[:, :], ACT.Ln).then_inc(S["lnr"], 1)
                wait("lnr", n + 1)
                act.activation(rn[:, :], rn[:, :], ACT.Exp, scale=-0.5).then_inc(S["rnd"], 1)
                wait("gcold", n * 2 + 2)
                act.activation(eg[:, :], gcol[:, :], ACT.Exp).then_inc(S["egd"], 1)
                wait("std", n)
                for i in range(2):
                    half = slice(64 * i, 64 * i + 64)
                    act.activation(egl[half, :], m4(bank[3 + i][half, :])[:, :, C - 1], ACT.Exp).then_inc(S["egld"], 1)
                for i in range(2):
                    wait("gsub", n * 2 + i + 1)
                    act.activation(dec[i][:, :, :], gtmp[i][:, :, :], ACT.Exp).then_inc(S["decd"], 1)
                for j, (dst, done) in enumerate(((qT, "qTd"), (kT, "kTd"), (kbT, "kbTd"))):
                    wait("tT", n * 3 + j + 1)
                    act.copy(dst[:, :, :].rearrange("p m c -> p (m c)"), bank[j][:, :]).then_inc(S[done], 1)
                for s_ in range(1, LEVELS):
                    for i in range(2):
                        wait("pm", n * (2 * LEVELS) + 2 * s_ + i + 1)
                        act.copy(Pm[i][:, :, :].rearrange("p m c -> p (m c)"), bank[i][:, :]).then_inc(S["pd"], 1)
                wait("wTm", n + 1)
                act.mul(wT[:, :, :].rearrange("p m c -> p (m c)"), bank[0][:, :], -1.0).then_inc(S["wTd"], 1)
                wait("vnm", n + 1)
                act.copy(vn[:, 0::2, :], w4(bank[1][:, 0:W // 2])).then_inc(S["vn0"], 1)
                act.copy(vn[:, 1::2, :], w4(bank[2][:, 0:W // 2])).then_inc(S["vnd"], 1)
                wait("od", n * 2 + 2)
                act.activation(sq[:, 0:W], osb[:, :, :].rearrange("p h d -> p (h d)"), ACT.Square).then_inc(S["osq"], 1)
                wait("ossd", n + 1)
                act.activation(ors[:, :], oss[:, :], ACT.Ln).then_inc(S["ors1"], 1)
                wait("ors1", n + 1)
                act.activation(ors[:, :], ors[:, :], ACT.Exp, scale=-0.5).then_inc(S["ors2"], 1)
                wait("yT", n + 1)
                act.copy(o.mixT[:, 4:8, bass.ds(n * C, C)], m4(bank[0][:, :])).then_inc(S["mixd"], 1)

        @block.vector
        def _(dve):
            wait = lambda name, v: dve.wait_ge(S[name], v)
            wait("vec_in", 48)
            ch = Chain(dve, S["pre_c"])
            a, b = o.ab[:, :, 0:H], o.ab[:, :, H:2 * H]
            ch.do(dve.tensor_tensor(sp1[:, :, :], a, bc(dtb[:, :].unsqueeze(1), [P, NT, H]), ALU.add))
            ch.do(dve.tensor_scalar(sp2[:, :, :], sp1[:, :, :], -1.0, None, ALU.mult))
            ch.do(dve.tensor_tensor(sp2[:, :, :], sp2[:, :, :], sp1[:, :, :], ALU.min))
            ch.do(dve.tensor_scalar(sp1[:, :, :], sp1[:, :, :], 0.0, None, ALU.max))
            dve.tensor_scalar(beta[:, :, :], b, -1.0, 80.0, ALU.mult, ALU.min).then_inc(S["pre_b"], 1)
            wait("pre_a", 4)
            ch.do(dve.tensor_scalar(la[:, :, :], sp2[:, :, :], 1.0, None, ALU.add))
            ch.do(dve.tensor_scalar(la[:, :, :], la[:, :, :], -1.0, 1e-30, ALU.add, ALU.max))
            ch.do(dve.reciprocal(la[:, :, :], la[:, :, :]))
            ch.do(dve.tensor_tensor(la[:, :, :], la[:, :, :], sp2[:, :, :], ALU.mult))
            ch.do(dve.tensor_tensor(la[:, :, :], la[:, :, :], sp3[:, :, :], ALU.mult))
            ch.do(dve.tensor_tensor(la[:, :, :], la[:, :, :], sp1[:, :, :], ALU.add))
            ch.do(dve.scalar_tensor_tensor(out=la[:, :, :], in0=la[:, :, :], scalar=-1.0,
                                           in1=bc(alog[:, :].unsqueeze(1), [P, NT, H]), op0=ALU.mult, op1=ALU.mult))
            ch.do(dve.tensor_scalar(beta[:, :, :], beta[:, :, :], 1.0, None, ALU.add))
            dve.reciprocal(beta[:, :, :], beta[:, :, :]).then_inc(S["pre_d"], 1)
            wait("pre_d", 1)
            with dve.Fori(0, NT) as n:
                bcol = bc(beta[:, bass.ds(n, 1), :].rearrange("p a h -> p (a h)").unsqueeze(2), [P, H, GD])
                wait("sqd", n * 2 + 2)
                dve.tensor_reduce(ssq[:, :], w4(sq[:, :]), AX.X, ALU.add).then_inc(S["tmp1"], 1)
                wait("tmp1", n * 3 + 1)
                dve.tensor_scalar(ssq[:, :], ssq[:, :], RMS_EPS, None, ALU.add).then_inc(S["ssqd"], 1)
                wait("rnd", n + 1)
                dve.tensor_scalar(rn[:, 0:H], rn[:, 0:H], GD ** -0.5, None, ALU.mult).then_inc(S["tmp1"], 1)
                wait("tmp1", n * 3 + 2)
                wait("tT", n * 3)
                dve.tensor_tensor(qn[:, :, :], w4(bank[0][:, :]), col(rn[:, 0:H], H, GD), ALU.mult).then_inc(S["qnd"], 1)
                dve.tensor_tensor(kn[:, :, :], w4(bank[1][:, :]), col(rn[:, H:2 * H], H, GD), ALU.mult)\
                    .then_inc(S["knd"], 1)
                wait("rawT", n * 3 + 3)
                dve.tensor_tensor(vb[:, :, :], w4(bank[2][:, :]), bcol, ALU.mult).then_inc(S["vbd"], 1)
                wait("knd", n + 1)
                dve.tensor_tensor(kb[:, :, :], kn[:, :, :], bcol, ALU.mult).then_inc(S["kbd"], 1)
                for i in range(2):
                    wait("gb", n * 2 + i + 1)
                    dve.tensor_tensor(gtmp[i][:, :, :], m4(bank[3 + i][:, :]), bc(g.ident[:, :].unsqueeze(1), [P, 4, C]),
                                      ALU.mult).then_inc(S["gdiag"], 1)
                    wait("gdiag", n * 2 + i + 1)
                    dve.tensor_reduce(gcol[:, i::2], gtmp[i][:, :, :], AX.X, ALU.add).then_inc(S["gcold"], 1)
                for i in range(2):
                    wait("gcold", n * 2 + 2)
                    wait("egld", n * 2 + 2)
                    dve.tensor_tensor(gtmp[i][:, :, :], m4(bank[3 + i][:, :]), col(gcol[:, i::2], 4, C),
                                      ALU.subtract).then_inc(S["gsub"], 1)
                for i in range(2):
                    wait("ltm", n * 2 + i + 1)
                    dve.tensor_tensor(LT[i][:, :, :], m4(bank[3 + i][:, :]), dec[i][:, :, :], ALU.mult)\
                        .then_inc(S["ltd"], 1)
                for i in range(2):
                    wait("atm", n * 2 + i + 1)
                    dve.tensor_tensor(AT[i][:, :, :], m4(bank[6 + i][:, :]), dec[i][:, :, :], ALU.mult)\
                        .then_inc(S["atd"], 1)
                idb = bc(g.ident[:, :].unsqueeze(1), [P, 4, C])
                for i in range(2):
                    wait("lmd", n * (2 * LEVELS) + i + 1)
                    wait("pm", n * (2 * LEVELS) + i + 1)
                    dve.tensor_tensor(Sm[i][:, :, :], idb, LM[i][0][:, :, :], ALU.subtract).then_inc(S["smd"], 1)
                    dve.tensor_tensor(Tm[i][:, :, :], idb, m4(bank[i][:, :]), ALU.subtract).then_inc(S["tmd"], 1)
                for s_ in range(1, LEVELS):
                    for i in range(2):
                        wait("wm", n * (2 * LEVELS - 2) + 2 * (s_ - 1) + i + 1)
                        dve.tensor_tensor(Sm[i][:, :, :], Sm[i][:, :, :], m4(bank[4 + i][:, :]), ALU.subtract)\
                            .then_inc(S["smd"], 1)
                        if s_ < LEVELS - 1:
                            dve.tensor_tensor(Tm[i][:, :, :], Tm[i][:, :, :], m4(bank[2 + i][:, :]), ALU.subtract)\
                                .then_inc(S["tmd"], 1)
                wait("om", n + 1)
                for i in range(2):
                    dve.tensor_tensor(osb[:, i::2, :], w4(bank[3 + 3 * i][:, 0:W // 2]), col(eg[:, i::2], H // 2, GD),
                                      ALU.mult).then_inc(S["oq"], 1)
                for i in range(2):
                    wait("oq", n * 2 + i + 1)
                    dve.tensor_tensor(osb[:, i::2, :], osb[:, i::2, :], w4(bank[4 + 3 * i][:, 0:W // 2]), ALU.add)\
                        .then_inc(S["od"], 1)
                wait("kvm", n + 1)
                wait("ones_state", n + 1)
                dve.tensor_tensor(state[:, :, :], state[:, :, :], w4(bank[5][:, 0:H // 2 * GD]), ALU.add)\
                    .then_inc(S["std"], 1)
                wait("osq", n + 1)
                dve.tensor_reduce(oss[:, :], w4(sq[:, 0:W]), AX.X, ALU.add).then_inc(S["tmp1"], 1)
                wait("tmp1", n * 3 + 3)
                dve.tensor_scalar(oss[:, :], oss[:, :], 1.0 / GD, RMS_EPS, ALU.mult, ALU.add).then_inc(S["ossd"], 1)
                wait("ors2", n + 1)
                dve.tensor_tensor(osb[:, :, :], osb[:, :, :], col(ors[:, :], H, GD), ALU.mult).then_inc(S["yd"], 1)
                wait("yd", n * 2 + 1)
                gate = w4(o.gate[:, bass.ds(n, 1), :].rearrange("p a w -> p (a w)"))
                dve.tensor_tensor(osb[:, :, :], osb[:, :, :], gate, ALU.mult).then_inc(S["yd"], 1)


class Hybrid:

    def __init__(self, g, ctx):
        self.mixT = g.sb(ctx, "mixT0", [P, KD, T])
        self.ab = g.sb(ctx, "gdn_ab", [P, NT, 2 * HEADS])
        self.gate = g.sb(ctx, "gdn_gate", [P, NT, HEADS * GD])

    def attention_inputs(self, g, ctx):
        self.latT = g.sb(ctx, "latT", [P, 3, T])
        self.krT = g.sb(ctx, "krT", [ROPE, T])
        self.v = g.sb(ctx, "mla_v", [P, NT, HEADS * VD])
        self.q = g.sb(ctx, "mla_q", [P, NT, HEADS, QD])


class ResidualNorm:

    def __init__(self, g, ctx, tag, x_dram, out_dram, layer, gate, gain, bias):
        self.g, self.x_dram, self.out_dram = g, x_dram, out_dram
        self.gain_row, self.bias_row = gain, bias
        self.gate = g.mod[:, layer, gate, :]
        sb = lambda name, shape: g.sb(ctx, f"{tag}_{name}", shape)
        self.gate_b = sb("gate_b", [P, D])
        self.gain_b = sb("gain_b", [P, D])
        self.bias_b = sb("bias_b", [P, D])
        self.diag = sb("diag", [P, KD, P])
        self.x = [sb(f"x{i}", [P, D]) for i in range(2)]
        self.z = [sb(f"z{i}", [P, D]) for i in range(3)]
        self.stats = sb("stats", [P, NT, 2, 6])
        self.mv = sb("mv", [P, NT, 2])
        self.rstd = sb("rstd", [P, NT])
        self.nmr = sb("nmr", [P, NT])
        names = "rows diagd gated gatec zmul zsum stat moments lnd rstdd nmrd normed gained done stored".split()
        self.S = dict(zip(names, g.sems(ctx, tag, *names)))
        self.x_in = g.sems(ctx, tag, "x_in0", "x_in1")

    def load_rows(self, sp):
        sp.dma_start(self.gain_b[:, :], self.gain_row.partition_broadcast(P)).then_inc(self.S["rows"], 16)
        sp.dma_start(self.bias_b[:, :], self.bias_row.partition_broadcast(P)).then_inc(self.S["rows"], 16)

    def load_x(self, sp, t):
        if t >= 2:
            sp.wait_ge(self.S["zsum"], t - 1)
        sp.dma_start(self.x[t % 2][:, :], self.x_dram[t * P:(t + 1) * P, :]).then_inc(self.x_in[t % 2], 16)

    def store(self, sp, t):
        sp.wait_ge(self.S["done"], t + 1)
        sp.dma_start(self.out_dram[t * P:(t + 1) * P, :], self.z[t % 3][:, :]).then_inc(self.S["stored"], 16)

    def gate_diag(self, dve):
        for kk in range(KD):
            dve.tensor_scalar(self.diag[:, kk, :], self.g.ident[:, :], self.gate[:, kk:kk + 1], None, ALU.mult)\
                .then_inc(self.S["diagd"], 1)

    def gate_rows(self, pe, banks):
        pe.wait_ge(self.S["diagd"], KD)
        for half in range(2):
            mm = pe.matmul(banks[:, half * 512:(half + 1) * 512], self.g.ones[:, :],
                           self.diag[:, 4 * half:4 * half + 4, :], start=True, stop=True)
        mm.then_inc(self.S["gated"], 1)

    def gate_copy(self, act, banks):
        act.wait_ge(self.S["gated"], 1)
        act.copy(self.gate_b[:, :], banks[:, :]).then_inc(self.S["gatec"], 1)

    def vector(self, dve, t, y):
        S, z = self.S, self.z[t % 3]
        if t == 0:
            dve.wait_ge(S["gatec"], 1)
        if t >= 3:
            dve.wait_ge(S["stored"], 16 * (t - 2))
        dve.tensor_tensor(z[:, :], y, self.gate_b[:, :], ALU.mult).then_inc(S["zmul"], 1)
        dve.wait_ge(S["zmul"], t + 1)
        dve.wait_ge(self.x_in[t % 2], 16 * (t // 2 + 1))
        dve.scalar_tensor_tensor(out=z[:, :], in0=self.x[t % 2][:, :], scalar=ALPHA, in1=z[:, :], op0=ALU.mult,
                                 op1=ALU.add).then_inc(S["zsum"], 1)
        dve.wait_ge(S["zsum"], t + 1)
        for half in range(2):
            dve.bn_stats(self.stats[:, t, half, :], z[:, half * 512:(half + 1) * 512]).then_inc(S["stat"], 1)
        dve.wait_ge(S["stat"], 2 * t + 2)
        dve.bn_aggr(self.mv[:, t, :], self.stats[:, t, :, :].rearrange("p a b -> p (a b)")).then_inc(S["moments"], 1)
        dve.wait_ge(S["moments"], 2 * t + 1)
        dve.tensor_scalar(self.rstd[:, t:t + 1], self.mv[:, t, 1:2], LN_EPS, None, ALU.add).then_inc(S["moments"], 1)
        dve.wait_ge(S["rstdd"], t + 1)
        dve.scalar_tensor_tensor(out=self.nmr[:, t:t + 1], in0=self.mv[:, t, 0:1], scalar=-1.0,
                                 in1=self.rstd[:, t:t + 1], op0=ALU.mult, op1=ALU.mult).then_inc(S["nmrd"], 1)

    def scalar(self, act, t):
        S, r, z = self.S, self.rstd[:, t:t + 1], self.z[t % 3]
        act.wait_ge(S["moments"], 2 * t + 2)
        act.activation(r, r, ACT.Ln).then_inc(S["lnd"], 1)
        act.wait_ge(S["lnd"], t + 1)
        act.activation(r, r, ACT.Exp, scale=-0.5).then_inc(S["rstdd"], 1)
        act.wait_ge(S["nmrd"], t + 1)
        act.activation(z[:, :], z[:, :], ACT.Identity, bias=self.nmr[:, t:t + 1], scale=r).then_inc(S["normed"], 1)

    def pool(self, pool, t):
        S, z = self.S, self.z[t % 3]
        if t == 0:
            pool.wait_ge(S["rows"], 32)
        pool.wait_ge(S["normed"], t + 1)
        pool.tensor_tensor(z[:, :], z[:, :], self.gain_b[:, :], ALU.mult).then_inc(S["gained"], 1)
        pool.wait_ge(S["gained"], t + 1)
        pool.tensor_tensor(z[:, :], z[:, :], self.bias_b[:, :], ALU.add).then_inc(S["done"], 1)


def mix_out(g, tag, mixT, nk, w, x_dram, out_dram, layer):
    nc, io = g.nc, g.io
    with ExitStack() as ctx:
        rn = ResidualNorm(g, ctx, tag, x_dram, out_dram, layer, 2, io["ln_mix_g"][layer], io["ln_mix_b"][layer])
        ws = g.sb(ctx, f"{tag}_w", [P, nk, D])
        py = [g.ps(ctx, f"{tag}_py{i}", [P, D]) for i in range(3)]
        proj, = g.sems(ctx, tag, "proj")
        w_in = g.sems(ctx, tag, *[f"w_in{i}" for i in range(nk // 4)])
        block = ctx.enter_context(nc.Block())
        wr = w.rearrange("(k p) n -> p k n", p=P)

        @block.sync
        def _(sp):
            for c in range(nk // 4):
                sp.dma_start(ws[:, 4 * c:4 * c + 4, :], wr[:, 4 * c:4 * c + 4, :]).then_inc(w_in[c], 16)
            rn.load_rows(sp)
            for t in range(NT + 1):
                if t < NT:
                    rn.load_x(sp, t)
                if t >= 1:
                    rn.store(sp, t - 1)
            sp.wait_ge(rn.S["stored"], 16 * NT)

        @block.tensor
        def _(pe):
            rn.gate_rows(pe, py[2])
            for t in range(NT):
                if t == 2:
                    pe.wait_ge(rn.S["gatec"], 1)
                if t >= 3:
                    pe.wait_ge(rn.S["zmul"], t - 2)
                for half in range(2):
                    for kk in range(nk):
                        if t == 0 and kk % 4 == 0:
                            pe.wait_ge(w_in[kk // 4], 16)
                        mm = pe.matmul(py[t % 3][:, half * 512:(half + 1) * 512], mixT[:, kk, t * P:(t + 1) * P],
                                       ws[:, kk, half * 512:(half + 1) * 512], start=(kk == 0), stop=(kk == nk - 1))
                mm.then_inc(proj, 1)

        @block.vector
        def _(dve):
            rn.gate_diag(dve)
            for t in range(NT):
                dve.wait_ge(proj, t + 1)
                rn.vector(dve, t, py[t % 3][:, :])

        @block.scalar
        def _(act):
            rn.gate_copy(act, py[2])
            for t in range(NT):
                rn.scalar(act, t)

        @block.gpsimd
        def _(pool):
            for t in range(NT):
                rn.pool(pool, t)


def retention(g, mixT):
    nc, io = g.nc, g.io
    STEPS = 2 * NT
    HK = RDK // 2
    QK = 2 * RDK
    W = QK + 2 * RDV
    lg = [math.log(1.0 - 2.0 ** (-5.0 - h)) for h in range(HEADS)]
    with ExitStack() as ctx:
        sb = lambda name, shape, dt=F32: g.sb(ctx, f"ret_{name}", shape, dt)
        w = [sb(f"w{u}", [P, KD, W]) for u in range(2)]
        gain = sb("gain", [P, HEADS, RDV])
        bias = sb("bias", [P, HEADS, RDV])
        place_i = sb("place_i", [P, 1], I32)
        place = sb("place", [P, 1])
        rate = sb("rate", [P, 2, HEADS])
        decay = sb("decay", [P, 2, HEADS])
        chunk_decay = sb("chunk_decay", [P, HEADS])
        qk = [sb(f"qk{i}", [P, 2, RDK]) for i in range(2)]
        tmp = [sb(f"tmp{i}", [P, 2, HK]) for i in range(2)]
        qkr = [sb(f"qkr{i}", [P, 2, RDK]) for i in range(4)]
        v = [sb(f"v{i}", [P, RDV]) for i in range(4)]
        gate = [sb(f"gate{i}", [P, RDV]) for i in range(4)]
        qkT = [sb(f"qkT{i}", [P, 2, P]) for i in range(2)]
        scores = [sb(f"scores{i}", [P, P]) for i in range(2)]
        state = [sb(f"state{i}", [P, RDV]) for i in range(2)]
        z = [sb(f"z{i}", [P, RDV]) for i in range(4)]
        stats = [sb(f"stats{i}", [P, 6]) for i in range(2)]
        mv = [sb(f"mv{i}", [P, 2]) for i in range(2)]
        rstd = [sb(f"rstd{i}", [P, 1]) for i in range(2)]
        head_gain = [sb(f"head_gain{u}", [P, RDV]) for u in range(2)]
        head_bias = [sb(f"head_bias{u}", [P, RDV]) for u in range(2)]
        p_qkv = [g.ps(ctx, f"ret_pqkv{i}", [P, 512]) for i in range(2)]
        p_gate = [g.ps(ctx, f"ret_pgate{i}", [P, 512]) for i in range(2)]
        p_turn = g.ps(ctx, "ret_pturn", [P, 512])
        p_scores = g.ps(ctx, "ret_pscores", [P, 512])
        p_out = g.ps(ctx, "ret_pout", [P, 512])
        p_back = g.ps(ctx, "ret_pback", [P, 512])
        names = ("rows placed rates exps qkv gates taken gated roped turned turnc scored masked out moments logs roots norms rowsc "
                 "gained back backc").split()
        S = dict(zip(names, g.sems(ctx, "ret", *names)))
        w_in = g.sems(ctx, "ret", "w_in0", "w_in1")
        block = ctx.enter_context(nc.Block())
        w_dram = io["ret_w_in"][0].rearrange("(k p) n -> p k n", p=P)
        parts = []
        at = off = 0
        for width in (RDK, RDK, RDV, RDV):
            cols = w_dram[:, :, at:at + HEADS * width].rearrange("p k (m u n) -> p k m u n", u=2, n=width)
            parts.append((off, width, cols))
            at += HEADS * width
            off += width
        pairs = HEADS // 2
        before = lambda m, s: m * STEPS + max(s, 0)
        after = lambda m, s: m * STEPS + s + 1

        @block.sync
        def _(sp):
            def panel(m, u):
                for off, width, cols in parts:
                    sp.dma_start(w[u][:, :, off:off + width], cols[:, :, bass.ds(m, 1), u, :]
                                 .rearrange("p k a n -> p k (a n)")).then_inc(w_in[u], 16)

            with sp.Fori(0, pairs) as m:
                for u in range(2):
                    sp.wait_ge(S["gates"], m * STEPS)
                    panel(m, u)

        @block.gpsimd
        def _(pool):
            pool.iota(place_i[:, :], [[1, 1]], base=1, channel_multiplier=1).then_inc(S["placed"], 1)
            for h in range(HEADS):
                pool.memset(rate[:, 0, h:h + 1], lg[h]).then_inc(S["placed"], 1)
                pool.memset(rate[:, 1, h:h + 1], -lg[h]).then_inc(S["placed"], 1)
                pool.memset(chunk_decay[:, h:h + 1], math.exp(RDK * lg[h])).then_inc(S["placed"], 1)
            pool.wait_ge(S["rows"], 32)
            gp = gain[:, :, :].rearrange("p (m u) n -> p m u n", u=2)
            bp = bias[:, :, :].rearrange("p (m u) n -> p m u n", u=2)
            with pool.Fori(0, pairs) as m:
                for u in range(2):
                    row = lambda t: t[:, bass.ds(m, 1), u, :].rearrange("p a n -> p (a n)")
                    pool.tensor_copy(head_gain[u][:, :], row(gp)).then_inc(S["rowsc"], 1)
                    pool.tensor_copy(head_bias[u][:, :], row(bp)).then_inc(S["rowsc"], 1)
                for s in range(STEPS):
                    u, zb = s // NT, z[s % 4][:, :]
                    pool.wait_ge(S["norms"], after(m, s))
                    pool.wait_ge(S["rowsc"], m * 4 + 4)
                    pool.tensor_tensor(zb, zb, head_gain[u][:, :], ALU.mult).then_inc(S["gained"], 1)
                    pool.wait_ge(S["gained"], m * 3 * STEPS + 3 * s + 1)
                    pool.tensor_tensor(zb, zb, head_bias[u][:, :], ALU.add).then_inc(S["gained"], 1)
                    pool.wait_ge(S["gained"], m * 3 * STEPS + 3 * s + 2)
                    pool.tensor_tensor(zb, zb, gate[s % 4][:, :], ALU.mult).then_inc(S["gained"], 1)

        @block.tensor
        def _(pe):
            with pe.Fori(0, pairs) as m:
                def project(s):
                    u, t = s // NT, s % NT
                    if t == 0:
                        pe.wait_ge(w_in[u], m * 64 + 64)
                    pe.wait_ge(S["taken"], before(m, s - 1))
                    for kk in range(KD):
                        mm = pe.matmul(p_qkv[s % 2][:, :], g.hT[:, kk, t * P:(t + 1) * P], w[u][:, kk, 0:512],
                                       start=(kk == 0), stop=(kk == KD - 1))
                    mm.then_inc(S["qkv"], 1)

                def project_gate(s):
                    u, t = s // NT, s % NT
                    pe.wait_ge(S["gated"], before(m, s - 1))
                    for kk in range(KD):
                        mm = pe.matmul(p_gate[s % 2][:, 0:RDV], g.hT[:, kk, t * P:(t + 1) * P], w[u][:, kk, 512:W],
                                       start=(kk == 0), stop=(kk == KD - 1))
                    mm.then_inc(S["gates"], 1)

                def turn(s):
                    pe.wait_ge(S["roped"], m * 6 * STEPS + 6 * s + 6)
                    pe.wait_ge(S["turnc"], before(m, s))
                    for i in range(2):
                        mm = pe.transpose(p_turn[:, i * P:(i + 1) * P], qkr[s % 4][:, i, :], g.ident[:, :])
                    mm.then_inc(S["turned"], 1)

                def score(s):
                    pe.wait_ge(S["turnc"], after(m, s))
                    pe.wait_ge(S["masked"], before(m, s))
                    pe.matmul(p_scores[:, 0:P], qkT[s % 2][:, 1, :], qkT[s % 2][:, 0, :], start=True, stop=True)\
                        .then_inc(S["scored"], 1)

                def output(s):
                    t = s % NT
                    pe.wait_ge(S["masked"], after(m, s))
                    pe.wait_ge(S["norms"], before(m, s))
                    pe.matmul(p_out[:, 0:RDV], scores[s % 2][:, :], v[s % 4][:, :], start=True, stop=(t == 0))
                    if t:
                        pe.matmul(p_out[:, 0:RDV], qkT[s % 2][:, 0, :], state[(s - 1) % 2][:, :], start=False, stop=True)
                    pe.matmul(p_out[:, RDV:2 * RDV], qkr[s % 4][:, 1, :], v[s % 4][:, :], start=True, stop=True)\
                        .then_inc(S["out"], 1)

                def turn_back(s):
                    pe.wait_ge(S["gained"], m * 3 * STEPS + 3 * s + 3)
                    pe.wait_ge(S["backc"], before(m, s))
                    for i in range(2):
                        mm = pe.transpose(p_back[:, i * P:(i + 1) * P], z[s % 4][:, i * P:(i + 1) * P], g.ident[:, :])
                    mm.then_inc(S["back"], 1)

                for s in range(STEPS + 3):
                    if s < STEPS:
                        project(s)
                    if 0 <= s - 2 < STEPS:
                        output(s - 2)
                    if 0 <= s - 1 < STEPS:
                        turn(s - 1)
                    if s < STEPS:
                        project_gate(s)
                    if 0 <= s - 1 < STEPS:
                        score(s - 1)
                    if 0 <= s - 3 < STEPS:
                        turn_back(s - 3)

        @block.scalar
        def _(act):
            act.dma_start(gain[:, :, :].rearrange("p h n -> p (h n)"), io["ret_gn_g"][0].partition_broadcast(P))\
                .then_inc(S["rows"], 16)
            act.dma_start(bias[:, :, :].rearrange("p h n -> p (h n)"), io["ret_gn_b"][0].partition_broadcast(P))\
                .then_inc(S["rows"], 16)
            act.wait_ge(S["rates"], 3)
            act.activation(decay[:, :, :], rate[:, :, :], ACT.Exp).then_inc(S["exps"], 1)
            act.wait_ge(S["exps"], 2)
            dp = decay[:, :, :].rearrange("p i (m u) -> p i m u", u=2)
            mp = mixT[:, :, :].rearrange("p (m k) t -> p m k t", k=4)
            with act.Fori(0, pairs) as m:
                def take(s):
                    u, b = s // NT, s % 4
                    act.wait_ge(S["qkv"], after(m, s))
                    act.wait_ge(S["roped"], m * 6 * STEPS + max(6 * (s - 1), 0))
                    act.wait_ge(S["out"], before(m, s - 3))
                    act.copy(v[b][:, :], p_qkv[s % 2][:, QK:512])
                    for i in range(2):
                        ins = act.activation(qk[s % 2][:, i, :], p_qkv[s % 2][:, i * RDK:(i + 1) * RDK], ACT.Copy,
                                             scale=dp[:, i, bass.ds(m, 1), u])
                    ins.then_inc(S["taken"], 1)

                def take_gate(s):
                    act.wait_ge(S["gates"], after(m, s))
                    act.wait_ge(S["gained"], m * 3 * STEPS + max(3 * (s - 3), 0))
                    act.activation(gate[s % 4][:, :], p_gate[s % 2][:, 0:RDV], ACT.Silu).then_inc(S["gated"], 1)

                def root(s):
                    act.wait_ge(S["moments"], m * 5 * STEPS + 5 * s + 5)
                    act.wait_ge(S["norms"], before(m, s - 1))
                    act.activation(rstd[s % 2][:, :], mv[s % 2][:, 1:2], ACT.Ln).then_inc(S["logs"], 1)
                    act.wait_ge(S["logs"], after(m, s))
                    act.activation(rstd[s % 2][:, :], rstd[s % 2][:, :], ACT.Exp, scale=-0.5).then_inc(S["roots"], 1)

                def take_turned(s):
                    act.wait_ge(S["turned"], after(m, s))
                    act.wait_ge(S["out"], before(m, s - 1))
                    act.copy(qkT[s % 2][:, :, :].rearrange("p a t -> p (a t)"), p_turn[:, 0:2 * P])\
                        .then_inc(S["turnc"], 1)

                def take_back(s):
                    u, t = s // NT, s % NT
                    act.wait_ge(S["back"], after(m, s))
                    act.copy(mp[:, bass.ds(m, 1), 2 * u:2 * u + 2, t * P:(t + 1) * P].rearrange("p a k t -> p (a k) t"),
                             p_back[:, 0:2 * P].rearrange("p (k t) -> p k t", k=2)).then_inc(S["backc"], 1)

                for s in range(STEPS + 3):
                    if s < STEPS:
                        take(s)
                    if 0 <= s - 2 < STEPS:
                        root(s - 2)
                    if 0 <= s - 1 < STEPS:
                        take_turned(s - 1)
                    if s < STEPS:
                        take_gate(s)
                    if 0 <= s - 3 < STEPS:
                        take_back(s - 3)

        @block.vector
        def _(dve):
            dve.wait_ge(S["placed"], 1 + 3 * HEADS)
            ch = Chain(dve, S["rates"])
            ch.do(dve.tensor_copy(place[:, :], place_i[:, :]))
            for i in range(2):
                ch.mark(dve.tensor_scalar(rate[:, i, :], rate[:, i, :], place[:, 0:1], None, ALU.mult))
            dve.wait_ge(S["exps"], 1)
            dve.tensor_scalar(decay[:, 0, :], decay[:, 0, :], RDK ** -0.5, None, ALU.mult).then_inc(S["exps"], 1)
            cd = chunk_decay[:, :].rearrange("p (m u) -> p m u", u=2)
            with dve.Fori(0, pairs) as m:
                def rope(s):
                    t, x, out = s % NT, qk[s % 2], qkr[s % 4]
                    dve.wait_ge(S["taken"], after(m, s))
                    dve.wait_ge(S["out"], before(m, s - 3))
                    ch = Chain(dve, S["roped"], m * 6 * STEPS + 6 * s)
                    cos = bc(g.cos[:, t, :].unsqueeze(1), [P, 2, HK])
                    sin = bc(g.sin[:, t, :].unsqueeze(1), [P, 2, HK])
                    x1, x2 = x[:, :, 0:HK], x[:, :, HK:RDK]
                    ta, tb = tmp[0][:, :, :], tmp[1][:, :, :]
                    ch.mark(dve.tensor_tensor(ta, x1, cos, ALU.mult))
                    ch.do(dve.tensor_tensor(tb, x2, sin, ALU.mult))
                    ch.do(dve.tensor_tensor(out[:, :, 0:HK], ta, tb, ALU.subtract))
                    ch.mark(dve.tensor_tensor(ta, x1, sin, ALU.mult))
                    ch.do(dve.tensor_tensor(tb, x2, cos, ALU.mult))
                    ch.do(dve.tensor_tensor(out[:, :, HK:RDK], ta, tb, ALU.add))

                def mask(s):
                    dve.wait_ge(S["scored"], after(m, s))
                    dve.wait_ge(S["out"], before(m, s - 1))
                    dve.tensor_tensor(scores[s % 2][:, :], p_scores[:, 0:P], g.upto[:, :], ALU.mult)\
                        .then_inc(S["masked"], 1)

                def finish(s):
                    u, t, st = s // NT, s % NT, state[s % 2]
                    dve.wait_ge(S["out"], after(m, s))
                    ch = Chain(dve, S["moments"], m * 5 * STEPS + 5 * s)
                    if t:
                        ch.mark(dve.tensor_tensor(st[:, :], state[(s - 1) % 2][:, :], p_out[:, RDV:2 * RDV], ALU.add))
                    else:
                        ch.mark(dve.tensor_copy(st[:, :], p_out[:, RDV:2 * RDV]))
                    ch.do(dve.bn_stats(stats[s % 2][:, :], p_out[:, 0:RDV]))
                    ch.mark(dve.tensor_scalar(st[:, :], st[:, :], cd[:, bass.ds(m, 1), u], None, ALU.mult))
                    ch.do(dve.bn_aggr(mv[s % 2][:, :], stats[s % 2][:, :]))
                    ch.mark(dve.tensor_scalar(mv[s % 2][:, 1:2], mv[s % 2][:, 1:2], LN_EPS, None, ALU.add))

                def centre(s):
                    dve.wait_ge(S["roots"], after(m, s))
                    dve.wait_ge(S["back"], before(m, s - 3))
                    dve.tensor_scalar(z[s % 4][:, :], p_out[:, 0:RDV], mv[s % 2][:, 0:1], rstd[s % 2][:, 0:1],
                                      ALU.subtract, ALU.mult).then_inc(S["norms"], 1)

                for s in range(STEPS + 2):
                    if 0 <= s - 2 < STEPS:
                        finish(s - 2)
                    if s < STEPS:
                        rope(s)
                    if 0 <= s - 2 < STEPS:
                        centre(s - 2)
                    if 0 <= s - 1 < STEPS:
                        mask(s - 1)


class Routing:

    def __init__(self, g, ctx, tag):
        self.weight = g.sb(ctx, f"{tag}_weight", [P, NT, 2])
        self.slot = g.sb(ctx, f"{tag}_slot", [P, NT, 2], I32)
        self.token = g.sb(ctx, f"{tag}_token", [P, NBLK], I32)
        self.expert = g.sb(ctx, f"{tag}_expert", [1, NBLK], I32)
        self.used = g.sb(ctx, f"{tag}_used", [1, 1], I32)


def route(g, tag, r, layer, y_dram=None):
    nc, io = g.nc, g.io
    spare = range(PAIRS // P, NBLK) if y_dram is not None else ()
    NR = NG + NE
    BIG = 99.0
    with ExitStack() as ctx:
        sb = lambda name, shape, dt=F32: g.sb(ctx, f"{tag}_{name}", shape, dt)
        w = sb("w", [P, KD, NR])
        bias = sb("bias", [P, NR])
        L = sb("L", [P, NT, NR])
        iota_i = sb("iota_i", [P, P], I32)
        tok_i = sb("tok_i", [P, NT], I32)
        iota = sb("iota", [P, P])
        tok = sb("tok", [P, NT])
        gm, gs, gi, m1, m2, i1, i2, ex, tw = (sb(n, [P, NT]) for n in "gm gs gi m1 m2 i1 i2 ex tw".split())
        t4, g1h = sb("t4", [P, NT, NG]), sb("g1h", [P, NT, NG])
        t32 = sb("t32", [P, NT, NG, EPG])
        es, t8 = sb("es", [P, NT, EPG]), sb("t8", [P, NT, EPG])
        O = [sb(f"O{i}", [P, NT, NE]) for i in range(2)]
        C = sb("C", [P, NT, NE])
        Cp = sb("Cp", [P, NT + 1, NE])
        cnt, nb, cum, zero = (sb(n, [P, NE]) for n in "cnt nb cum zero".split())
        rank = sb("rank", [P, NT, NE])
        st = sb("st", [P, NT, NE])
        slotf = sb("slotf", [P, NT, 2])
        lo_i, hi_i = sb("lo_i", [P, NT, 2], I32), sb("hi_i", [P, NT, 2], I32)
        lo, hi = sb("lo", [P, NT, 2]), sb("hi", [P, NT, 2])
        A = [sb(f"A{i}", [P, P]) for i in range(2)]
        B = [sb(f"B{i}", [P, NBLK]) for i in range(2)]
        be = sb("be", [1, NBLK, NE])
        bes = sb("bes", [1, NBLK])
        usf = sb("usf", [1, 2])
        pl = g.ps(ctx, f"{tag}_pl", [P, 512])
        pr = g.ps(ctx, f"{tag}_pr", [P, 512])
        pk = g.ps(ctx, f"{tag}_pk", [P, 512])
        blank = sb("blank", [P, D])
        names = "w_in b_in blanked cleared iotas logits steps grp gexp diff dexp onehot ranked hit placed".split()
        S = dict(zip(names, g.sems(ctx, tag, *names)))
        block = ctx.enter_context(nc.Block())

        @block.sync
        def _(sp):
            sp.dma_start(bias[:, 0:NG], io["moe_b_group"][layer].partition_broadcast(P)).then_inc(S["b_in"], 16)
            sp.dma_start(bias[:, NG:NR], io["moe_b_expert"][layer].partition_broadcast(P)).then_inc(S["b_in"], 16)
            with nc.allow_non_contiguous_dma(reason="the group logits' weights, 16 bytes a row"):
                sp.dma_start(w[:, :, 0:NG], io["moe_w_group"][layer].rearrange("(k p) n -> p k n", p=P))\
                    .then_inc(S["w_in"], 16)
                sp.dma_start(w[:, :, NG:NR], io["moe_w_expert"][layer].rearrange("(k p) n -> p k n", p=P))\
                    .then_inc(S["w_in"], 16)
            sp.wait_ge(S["blanked"], 1)
            for i in spare:
                sp.dma_start(y_dram[i * P:(i + 1) * P, :], blank[:, :]).then_inc(S["cleared"], 16)
            if len(spare):
                sp.wait_ge(S["cleared"], 16 * len(spare))

        @block.gpsimd
        def _(pool):
            pool.iota(iota_i[:, :], [[1, P]], base=0, channel_multiplier=0).then_inc(S["iotas"], 1)
            pool.iota(tok_i[:, :], [[P, NT]], base=0, channel_multiplier=1).then_inc(S["iotas"], 1)
            pool.memset(blank[:, :], 0.0).then_inc(S["blanked"], 1)

        @block.tensor
        def _(pe):
            pe.wait_ge(S["w_in"], 32)
            for t in range(NT):
                for kk in range(KD):
                    mm = pe.matmul(pl[:, t * NR:(t + 1) * NR], g.hT[:, kk, t * P:(t + 1) * P], w[:, kk, :],
                                   start=(kk == 0), stop=(kk == KD - 1))
            mm.then_inc(S["logits"], 1)
            pe.wait_ge(S["onehot"], 1)
            pe.matmul(pr[:, 0:NT * NE], g.before[:, :], C[:, :, :], start=True, stop=False)
            pe.matmul(pr[:, 0:NT * NE], g.ones[:, :], Cp[:, 0:NT, :], start=False, stop=True)
            pe.matmul(pr[:, NT * NE:(NT + 1) * NE], g.ones[:, :], Cp[:, NT, :], start=True, stop=True)\
                .then_inc(S["ranked"], 1)
            for n in range(2 * NT):
                pe.wait_ge(S["hit"], 2 * n + 2)
                pe.matmul(pk[:, 0:NBLK], A[n % 2][:, :], B[n % 2][:, :], start=(n == 0), stop=(n == 2 * NT - 1))\
                    .then_inc(S["placed"], 1)

        @block.scalar
        def _(act):
            act.wait_ge(S["grp"], 1)
            act.activation(t4[:, :, :], t4[:, :, :], ACT.Exp).then_inc(S["gexp"], 1)
            act.wait_ge(S["diff"], 1)
            act.activation(ex[:, :], ex[:, :], ACT.Exp).then_inc(S["dexp"], 1)

        @block.vector
        def _(dve):
            ch = Chain(dve, S["steps"])
            tt = lambda out, a, b, op: ch.do(dve.tensor_tensor(out, a, b, op))
            ts = lambda out, a, s1, s2, op0, op1=None: ch.do(
                dve.tensor_scalar(out, a, s1, s2, op0, op1) if op1 is not None else dve.tensor_scalar(out, a, s1, s2, op0))
            red = lambda out, a, op: ch.do(dve.tensor_reduce(out, a, AX.X, op))
            c3 = lambda ap, n: bc(ap.unsqueeze(2), [P, NT, n])

            def first_of(idx, v, top, n, t):
                tt(t, v, c3(top, n), ALU.is_lt)
                ch.do(dve.scalar_tensor_tensor(out=t, in0=t, scalar=BIG, in1=bc(iota[:, 0:n].unsqueeze(1), [P, NT, n]),
                                               op0=ALU.mult, op1=ALU.add))
                red(idx, t, ALU.min)

            dve.wait_ge(S["iotas"], 2)
            ch.do(dve.tensor_copy(iota[:, :], iota_i[:, :]))
            ch.do(dve.tensor_copy(tok[:, :], tok_i[:, :]))
            ch.do(dve.memset(zero[:, :], 0.0))
            ch.do(dve.memset(Cp[:, 0, :], 0.0))
            dve.wait_ge(S["b_in"], 32)
            dve.wait_ge(S["logits"], 1)
            tt(L[:, :, :], pl[:, 0:NT * NR].rearrange("p (t n) -> p t n", n=NR), bc(bias[:, :].unsqueeze(1), [P, NT, NR]),
               ALU.add)
            G = L[:, :, 0:NG]
            E = L[:, :, NG:NR].rearrange("p t (g e) -> p t g e", e=EPG)
            red(gm[:, :], G, ALU.max)
            first_of(gi[:, :], G, gm[:, :], NG, g1h[:, :, :])
            dve.tensor_tensor(t4[:, :, :], G, c3(gm[:, :], NG), ALU.subtract).then_inc(S["grp"], 1)
            tt(g1h[:, :, :], bc(iota[:, 0:NG].unsqueeze(1), [P, NT, NG]), c3(gi[:, :], NG), ALU.is_equal)
            for q in range(NG):
                tt(t32[:, :, q, :], E[:, :, q, :], bc(g1h[:, :, q:q + 1], [P, NT, EPG]), ALU.mult)
            red(es[:, :, :], t32[:, :, :, :].rearrange("p t g e -> p t e g"), ALU.add)
            red(m1[:, :], es[:, :, :], ALU.max)
            first_of(i1[:, :], es[:, :, :], m1[:, :], EPG, t8[:, :, :])
            tt(t8[:, :, :], bc(iota[:, 0:EPG].unsqueeze(1), [P, NT, EPG]), c3(i1[:, :], EPG), ALU.is_equal)
            ch.do(dve.scalar_tensor_tensor(out=es[:, :, :], in0=t8[:, :, :], scalar=NEG, in1=es[:, :, :],
                                           op0=ALU.mult, op1=ALU.add))
            red(m2[:, :], es[:, :, :], ALU.max)
            first_of(i2[:, :], es[:, :, :], m2[:, :], EPG, t8[:, :, :])
            dve.tensor_tensor(ex[:, :], m2[:, :], m1[:, :], ALU.subtract).then_inc(S["diff"], 1)
            dve.wait_ge(S["gexp"], 1)
            red(gs[:, :], t4[:, :, :], ALU.add)
            ch.do(dve.reciprocal(gs[:, :], gs[:, :]))
            dve.wait_ge(S["dexp"], 1)
            ts(tw[:, :], ex[:, :], 1.0, None, ALU.add)
            ch.do(dve.reciprocal(tw[:, :], tw[:, :]))
            tt(r.weight[:, :, 0], gs[:, :], tw[:, :], ALU.mult)
            tt(r.weight[:, :, 1], r.weight[:, :, 0], ex[:, :], ALU.mult)
            for k, idx in enumerate((i1, i2)):
                ch.do(dve.scalar_tensor_tensor(out=idx[:, :], in0=gi[:, :], scalar=float(EPG), in1=idx[:, :],
                                               op0=ALU.mult, op1=ALU.add))
                tt(O[k][:, :, :], bc(iota[:, 0:NE].unsqueeze(1), [P, NT, NE]), c3(idx[:, :], NE), ALU.is_equal)
            tt(C[:, :, :], O[0][:, :, :], O[1][:, :, :], ALU.add)
            for t in range(NT):
                tt(Cp[:, t + 1, :], Cp[:, t, :], C[:, t, :], ALU.add)
            dve.sem_inc(S["onehot"], 1)
            dve.wait_ge(S["ranked"], 1)
            ch.do(dve.tensor_copy(rank[:, :, :].rearrange("p t e -> p (t e)"), pr[:, 0:NT * NE]))
            ch.do(dve.tensor_copy(cnt[:, :], pr[:, NT * NE:(NT + 1) * NE]))
            ts(nb[:, :], cnt[:, :], 0.5, None, ALU.is_gt)
            for m in range(1, T // P):
                ch.do(dve.scalar_tensor_tensor(out=nb[:, :], in0=cnt[:, :], scalar=m * P + 0.5, in1=nb[:, :],
                                               op0=ALU.is_gt, op1=ALU.add))
            ch.do(dve.tensor_tensor_scan(cum[:, :], nb[:, :], zero[:, :], 0.0, ALU.add, ALU.add))
            tt(cnt[:, :], cum[:, :], nb[:, :], ALU.subtract)
            ts(cnt[:, :], cnt[:, :], float(P), None, ALU.mult)
            tt(rank[:, :, :], rank[:, :, :], bc(cnt[:, :].unsqueeze(1), [P, NT, NE]), ALU.add)
            for k in range(2):
                tt(st[:, :, :], rank[:, :, :], O[k][:, :, :], ALU.mult)
                red(slotf[:, :, k], st[:, :, :], ALU.add)
            ch.do(dve.tensor_copy(r.slot[:, :, :], slotf[:, :, :]))
            ts(lo_i[:, :, :], r.slot[:, :, :], P - 1, None, ALU.bitwise_and)
            ts(hi_i[:, :, :], r.slot[:, :, :], 7, None, ALU.arith_shift_right)
            ch.do(dve.tensor_copy(lo[:, :, :], lo_i[:, :, :]))
            ch.do(dve.tensor_copy(hi[:, :, :], hi_i[:, :, :]))
            for n in range(2 * NT):
                t, k = n // 2, n % 2
                if n >= 2:
                    dve.wait_ge(S["placed"], n - 1)
                dve.tensor_scalar(A[n % 2][:, :], iota[:, :], lo[:, t, k:k + 1], tok[:, t:t + 1], ALU.is_equal,
                                  ALU.mult).then_inc(S["hit"], 1)
                dve.tensor_scalar(B[n % 2][:, :], iota[:, 0:NBLK], hi[:, t, k:k + 1], None, ALU.is_equal)\
                    .then_inc(S["hit"], 1)
            tt(be[:, :, :], bc(iota[0:1, 0:NBLK].unsqueeze(2), [1, NBLK, NE]), bc(cum[0:1, :].unsqueeze(1), [1, NBLK, NE]),
               ALU.is_ge)
            red(bes[:, :], be[:, :, :], ALU.add)
            ts(bes[:, :], bes[:, :], float(NE - 1), None, ALU.min)
            ch.do(dve.tensor_copy(r.expert[:, :], bes[:, :]))
            ts(usf[:, 0:1], cum[0:1, NE - 1:NE], 0.5, 0.25, ALU.mult, ALU.add)
            ch.do(dve.tensor_copy(r.used[:, :], usf[:, 0:1]))
            dve.wait_ge(S["placed"], 2 * NT)
            ch.do(dve.tensor_copy(r.token[:, :], pk[:, 0:NBLK]))


def experts(g, tag, r, x_dram, y_dram, layer):
    nc, io = g.nc, g.io
    KF = FF // P
    PAIRS_OF_BLOCKS = NBLK // 2
    shift, scale = g.mod[:, layer, 3, :], g.mod[:, layer, 4, :]
    with ExitStack() as ctx:
        sb = lambda name, shape, dt=F32: g.sb(ctx, f"{tag}_{name}", shape, dt)
        wg, wu = ([sb(f"{n}{u}", [P, KD, FF]) for u in range(2)] for n in ("wg", "wu"))
        wd = [sb(f"wd{u}", [P, KF, D]) for u in range(2)]
        idx = [sb(f"idx{u}", [P, 1], I32) for u in range(2)]
        xg = [sb(f"xg{u}", [P, D]) for u in range(2)]
        xT = [sb(f"xT{u}", [P, KD, P]) for u in range(2)]
        hs = [sb(f"hs{u}", [P, FF]) for u in range(2)]
        hid = [sb(f"hid{u}", [P, FF]) for u in range(2)]
        hidT = [sb(f"hidT{u}", [P, KF, P]) for u in range(2)]
        y = [sb(f"y{u}", [P, D]) for u in range(2)]
        px = [g.ps(ctx, f"{tag}_px{u}", [P, 512]) for u in range(2)]
        pg = [g.ps(ctx, f"{tag}_pg{u}", [P, 512]) for u in range(2)]
        pu = [g.ps(ctx, f"{tag}_pu{u}", [P, 512]) for u in range(2)]
        pd = [g.ps(ctx, f"{tag}_pd{u}", [P, 512]) for u in range(2)]
        names = "xt xa xd gu silu hidd ht hTd down ya yd asked left".split()
        S = dict(zip(names, g.sems(ctx, tag, *names)))
        pairs = {n: g.sems(ctx, tag, n + "0", n + "1") for n in "idxd x_in gu_in d_in stored".split()}
        block = ctx.enter_context(nc.Block())
        gate_w = io["moe_w_gate"][layer].rearrange("e (k p) f -> e p k f", p=P)
        up_w = io["moe_w_up"][layer].rearrange("e (k p) f -> e p k f", p=P)
        down_w = io["moe_w_down"][layer].rearrange("e (k p) n -> e p k n", p=P)
        one = lambda ap: ap.rearrange("a p k n -> (a p) k n")

        def pairs_used(eng):
            return eng.value_load(r.used[0:1, 0:1], min_val=1, max_val=PAIRS_OF_BLOCKS)

        @block.sync
        def _(sp):
            ex = r.expert[:, :].rearrange("a (m u) -> a m u", u=2)
            with sp.Fori(0, pairs_used(sp)) as m:
                e = [sp.value_load(ex[0:1, bass.ds(m, 1), u], min_val=0, max_val=NE - 1) for u in range(2)]
                for u in range(2):
                    sp.wait_ge(S["gu"], m * 2)
                    sp.dma_start(wg[u][:, :, :], one(gate_w[bass.ds(e[u], 1)])).then_inc(pairs["gu_in"][u], 16)
                    sp.dma_start(wu[u][:, :, :], one(up_w[bass.ds(e[u], 1)])).then_inc(pairs["gu_in"][u], 16)
                for u in range(2):
                    sp.wait_ge(S["down"], m * 4)
                    sp.dma_start(wd[u][:, :, :], one(down_w[bass.ds(e[u], 1)])).then_inc(pairs["d_in"][u], 16)

        @block.gpsimd
        def _(pool):
            tk = r.token[:, :].rearrange("p (m u) -> p m u", u=2)
            with pool.Fori(0, pairs_used(pool)) as m:
                for u in range(2):
                    pool.wait_ge(pairs["x_in"][u], m * 16)
                    pool.wait_ge(S["xt"], m * 4)
                    pool.tensor_copy(idx[u][:, :], tk[:, bass.ds(m, 1), u]).then_inc(pairs["idxd"][u], 1)
                    pool.wait_ge(pairs["idxd"][u], m + 1)
                    pool.sem_inc(S["asked"], 1)
                    pool.indirect_dma_start(out=xg[u][:, :], out_offset=None, in_=x_dram,
                                            in_offset=bass.IndirectOffsetOnAxis(ap=idx[u][:, :], axis=0))\
                        .then_inc(pairs["x_in"][u], 16)

        @block.tensor
        def _(pe):
            with pe.Fori(0, pairs_used(pe)) as m:
                for u in range(2):
                    pe.wait_ge(pairs["x_in"][u], m * 16 + 16)
                    for half in range(2):
                        pe.wait_ge(S["xd" if half else "xa"], m * 2 + u)
                        if half == 0 and u == 0:
                            pe.wait_ge(S["hTd"], m * 2)
                        for j in range(4):
                            kk = 4 * half + j
                            mm = pe.transpose(px[half][:, j * P:(j + 1) * P], xg[u][:, kk * P:(kk + 1) * P], g.ident[:, :])
                        mm.then_inc(S["xt"], 1)
                    pe.wait_ge(pairs["gu_in"][u], m * 32 + 32)
                    pe.wait_ge(S["silu"], m * 2)
                    pe.wait_ge(S["hidd"], m * 2)
                    pe.wait_ge(S["xa"], m * 2 + u + 1)
                    pe.wait_ge(S["xd"], m * 2 + u + 1)
                    for dst, wt in ((pg[u], wg[u]), (pu[u], wu[u])):
                        for kk in range(KD):
                            mm = pe.matmul(dst[:, :], xT[u][:, kk, :], wt[:, kk, :], start=(kk == 0), stop=(kk == KD - 1))
                    mm.then_inc(S["gu"], 1)
                for u in range(2):
                    pe.wait_ge(S["hidd"], m * 2 + u + 1)
                    pe.wait_ge(S["hTd"], m * 2 + u)
                    for j in range(KF):
                        mm = pe.transpose(px[0][:, j * P:(j + 1) * P], hid[u][:, j * P:(j + 1) * P], g.ident[:, :])
                    mm.then_inc(S["ht"], 1)
                    pe.wait_ge(pairs["d_in"][u], m * 16 + 16)
                    pe.wait_ge(S["hTd"], m * 2 + u + 1)
                    for half in range(2):
                        pe.wait_ge(S["yd" if half else "ya"], m * 2 + u)
                        for kk in range(KF):
                            mm = pe.matmul(pd[half][:, :], hidT[u][:, kk, :], wd[u][:, kk, half * 512:(half + 1) * 512],
                                           start=(kk == 0), stop=(kk == KF - 1))
                        mm.then_inc(S["down"], 1)

        @block.scalar
        def _(act):
            yd = y_dram.rearrange("(m u p) n -> m u p n", u=2, p=P)
            with act.Fori(0, pairs_used(act)) as m:
                for u in range(2):
                    act.wait_ge(S["xt"], m * 4 + 2 * u + 1)
                    act.wait_ge(S["gu"], m * 2)
                    for j in range(4):
                        ins = act.activation(xT[u][:, j, :], px[0][:, j * P:(j + 1) * P], ACT.Identity,
                                             bias=shift[:, j:j + 1], scale=scale[:, j:j + 1])
                    ins.then_inc(S["xa"], 1)
                    act.wait_ge(S["gu"], m * 2 + u + 1)
                    act.wait_ge(S["hidd"], m * 2)
                    act.activation(hs[u][:, :], pg[u][:, :], ACT.Silu).then_inc(S["silu"], 1)
                for u in range(2):
                    act.wait_ge(S["down"], m * 4 + 2 * u + 1)
                    act.wait_ge(pairs["stored"][u], m * 16)
                    act.copy(y[u][:, 0:512], pd[0][:, :]).then_inc(S["ya"], 1)
                    act.wait_ge(S["ya"], m * 2 + u + 1)
                    act.wait_ge(S["yd"], m * 2 + u + 1)
                    act.dma_start(yd[bass.ds(m, 1), u].rearrange("a p n -> (a p) n"), y[u][:, :])\
                        .then_inc(pairs["stored"][u], 16)
            n = pairs_used(act)
            for u in range(2):
                act.wait_ge(pairs["stored"][u], n * 16)
            act.sem_inc(S["left"], 1)

        @block.vector
        def _(dve):
            with dve.Fori(0, pairs_used(dve)) as m:
                for u in range(2):
                    dve.wait_ge(S["xt"], m * 4 + 2 * u + 2)
                    dve.wait_ge(S["gu"], m * 2)
                    for j in range(4):
                        ins = dve.tensor_scalar(xT[u][:, 4 + j, :], px[1][:, j * P:(j + 1) * P], scale[:, 4 + j:5 + j],
                                                shift[:, 4 + j:5 + j], ALU.mult, ALU.add)
                    ins.then_inc(S["xd"], 1)
                    dve.wait_ge(S["silu"], m * 2 + u + 1)
                    dve.wait_ge(S["ht"], m * 2)
                    dve.tensor_tensor(hid[u][:, :], hs[u][:, :], pu[u][:, :], ALU.mult).then_inc(S["hidd"], 1)
                for u in range(2):
                    dve.wait_ge(S["ht"], m * 2 + u + 1)
                    dve.wait_ge(S["down"], m * 4)
                    dve.tensor_copy(hidT[u][:, :, :].rearrange("p k t -> p (k t)"), px[0][:, :]).then_inc(S["hTd"], 1)
                    dve.wait_ge(S["down"], m * 4 + 2 * u + 2)
                    dve.wait_ge(pairs["stored"][u], m * 16)
                    dve.tensor_copy(y[u][:, 512:D], pd[1][:, :]).then_inc(S["yd"], 1)


def combine(g, tag, r, y_dram, x_dram, out_dram, layer):
    nc, io = g.nc, g.io
    with ExitStack() as ctx:
        rn = ResidualNorm(g, ctx, tag, x_dram, out_dram, layer, 5, io["ln_ffn_g"][layer], io["ln_ffn_b"][layer])
        rows = [[g.sb(ctx, f"{tag}_r{k}_{b}", [P, D]) for b in range(2)] for k in range(2)]
        pb = g.ps(ctx, f"{tag}_pb", [P, D])
        sc1, sum2 = g.sems(ctx, tag, "sc1", "sum2")
        r_in = [g.sems(ctx, tag, f"r_in{k}_0", f"r_in{k}_1") for k in range(2)]
        block = ctx.enter_context(nc.Block())

        @block.sync
        def _(sp):
            rn.load_rows(sp)
            for t in range(NT + 1):
                if t < NT:
                    rn.load_x(sp, t)
                if t >= 1:
                    rn.store(sp, t - 1)
            sp.wait_ge(rn.S["stored"], 16 * NT)

        @block.gpsimd
        def _(pool):
            def gather(t):
                if t >= 2:
                    pool.wait_ge(rn.S["zmul"], t - 1)
                for k in range(2):
                    pool.indirect_dma_start(out=rows[k][t % 2][:, :], out_offset=None, in_=y_dram,
                                            in_offset=bass.IndirectOffsetOnAxis(ap=r.slot[:, t, k:k + 1], axis=0))\
                        .then_inc(r_in[k][t % 2], 16)

            gather(0)
            for t in range(NT):
                if t + 1 < NT:
                    gather(t + 1)
                rn.pool(pool, t)

        @block.tensor
        def _(pe):
            rn.gate_rows(pe, pb)

        @block.vector
        def _(dve):
            rn.gate_diag(dve)
            for t in range(NT):
                a, b = rows[0][t % 2], rows[1][t % 2]
                for k in range(2):
                    dve.wait_ge(r_in[k][t % 2], 16 * (t // 2 + 1))
                dve.tensor_scalar(a[:, :], a[:, :], r.weight[:, t, 0:1], None, ALU.mult).then_inc(sc1, 1)
                dve.wait_ge(sc1, t + 1)
                dve.scalar_tensor_tensor(out=a[:, :], in0=b[:, :], scalar=r.weight[:, t, 1:2], in1=a[:, :],
                                         op0=ALU.mult, op1=ALU.add).then_inc(sum2, 1)
                dve.wait_ge(sum2, t + 1)
                rn.vector(dve, t, a[:, :])

        @block.scalar
        def _(act):
            rn.gate_copy(act, pb)
            for t in range(NT):
                rn.scalar(act, t)


def moe(g, tag, x_dram, out_dram, layer):
    first = layer == 0
    if first:
        g.y_dram = g.nc.dram_tensor("expert_rows", [NBLK * P, D], F32).ap()
    with ExitStack() as ctx:
        r = Routing(g, ctx, tag)
        with ExitStack() as hctx:
            modulated(g, hctx, f"{tag}h")
            modulate(g, f"{tag}m", x_dram, layer, 1)
            route(g, f"{tag}r", r, layer, g.y_dram if first else None)
        experts(g, f"{tag}e", r, x_dram, g.y_dram, layer)
        combine(g, f"{tag}c", r, g.y_dram, x_dram, out_dram, layer)


def modulated(g, ctx, tag):
    g.hT = ctx.enter_context(g.nc.sbuf_tensor(f"hT_{tag}", [P, KD, T], F32, side="right"))


def layer_1(g, x2, out):
    nc, io = g.nc, g.io
    x3 = nc.dram_tensor("x3", [T, D], F32).ap()
    with ExitStack() as mixer:
        mixT = g.sb(mixer, "mixT1", [P, RET_MIX // P, T])
        with ExitStack() as hctx:
            modulated(g, hctx, "mix1")
            modulate(g, "m1", x2, 1, 0)
            retention(g, mixT)
        mix_out(g, "mo1", mixT, RET_MIX // P, io["ret_w_out"][0], x2, x3, 1)
    moe(g, "f1", x3, out.rearrange("b s d -> (b s) d"), 1)


def build(nc, io, out, stop=None):
    g = Program(nc, io)
    x = io["x"].rearrange("b s d -> (b s) d")
    with g.keep:
        constants(g)
        with ExitStack() as mixer:
            hctx = ExitStack()
            modulated(g, hctx, "mix0")
            modulate(g, "m0", x, 0, 0)
            o = Hybrid(g, mixer)
            with ExitStack() as ctx:
                o.attention_inputs(g, ctx)
                hybrid_inputs(g, o)
                if stop == "inputs":
                    return
                attention(g, o)
                if stop == "attention":
                    return
            with ExitStack() as ctx:
                qkvT = g.sb(ctx, "qkvT", [P, CT, T])
                gdn_convolve(g, qkvT)
                hctx.close()
                if stop == "conv":
                    return
                delta_rule(g, o, qkvT)
                if stop == "delta":
                    return
            x1 = nc.dram_tensor("x1", [T, D], F32).ap()
            mix_out(g, "mo0", o.mixT, KD, io["hy_w_out"][0], x, x1, 0)
        x2 = nc.dram_tensor("x2", [T, D], F32).ap()
        moe(g, "f0", x1, x2, 0)
        layer_1(g, x2, out)


_INS = ["x", "c", "positions", "ada_w", "ada_b", "ln_mix_g", "ln_mix_b", "ln_ffn_g", "ln_ffn_b", "hy_w_in",
        "mla_q_norm", "mla_w_uq", "mla_kv_norm", "mla_w_ukv", "gdn_conv_w", "gdn_a_log", "gdn_dt_bias", "gdn_norm",
        "hy_w_out", "ret_w_in", "ret_gn_g", "ret_gn_b", "ret_w_out", "moe_w_group", "moe_b_group", "moe_w_expert",
        "moe_b_expert", "moe_w_gate", "moe_w_up", "moe_w_down"]


def kernel(**inputs):
    import numpy as _np
    import concourse.bacc as _bacc
    from concourse import mybir as _mybir
    from concourse.bass_utils import run_bass_kernel_spmd as _run

    nc = _bacc.Bacc("TRN2", target_bir_lowering=False, num_devices=1)
    arrays, io = {}, {}
    for name in _INS:
        a = _np.ascontiguousarray(inputs[name])
        arrays[f"in_{name}_dram"] = a
        io[name] = nc.dram_tensor(f"in_{name}_dram", a.shape, _mybir.dt.from_np(a.dtype), kind="ExternalInput").ap()
    out = nc.dram_tensor("out_0_dram", (1, T, D), _mybir.dt.float32, kind="ExternalOutput").ap()
    build(nc, io, out)
    r = _run(nc, [arrays], core_ids=[0])
    return r.results[0]["out_0_dram"]
```

```python
import math
from contextlib import ExitStack

import numpy as np

import concourse.bass as bass
from concourse import mybir
from concourse.alu_op_type import AluOpType as ALU

P = 128
D = 1024
T = 1024
NT = T // P
KD = D // P
DEPTH = 2
NMOD = 6
ALPHA = (2.0 * DEPTH) ** 0.25
LN_EPS = 1e-5
RMS_EPS = 1e-6
NEG = -1.0e30

HEADS = 8
QR, KVR, ROPE, NOPE, VD = 256, 128, 32, 64, 64
QD = NOPE + ROPE
MLA_COLS = QR + KVR + ROPE
MLA_SCALE = QD ** -0.5
GD = 64
CONV = 4
QKV = HEADS * 3 * GD
CT = QKV // P
HY_IN = MLA_COLS + QKV + 2 * HEADS + HEADS * GD

RDK, RDV = 128, 256
RET_MIX = HEADS * RDV

NG, EPG = 4, 8
NE = NG * EPG
FF = 512
PAIRS = 2 * T
NBLK = PAIRS // P + NE
NFREQ = RDK // 2
PE_BANKS = 5
DVE_BANKS = NMOD * D // 512 - PE_BANKS
DVE_COLS = DVE_BANKS * 512

F32 = mybir.dt.float32
I32 = mybir.dt.int32
U32 = mybir.dt.uint32
ACT = mybir.ActivationFunctionType
AX = mybir.AxisListType


class Chain:

    def __init__(self, eng, sem, base=0):
        self.eng, self.sem, self.base, self.n = eng, sem, base, 0

    def mark(self, ins):
        ins.then_inc(self.sem, 1)
        self.n += 1

    def do(self, ins):
        self.mark(ins)
        self.eng.wait_ge(self.sem, self.base + self.n)


class Program:
    def __init__(self, nc, io):
        self.nc, self.io = nc, io
        self.keep = ExitStack()

    def sb(self, ctx, name, shape, dt=F32):
        return ctx.enter_context(self.nc.sbuf_tensor(name, shape, dt))

    def ps(self, ctx, name, shape, dt=F32):
        return ctx.enter_context(self.nc.psum_tensor(name, shape, dt))

    def sems(self, ctx, tag, *names):
        got = [self.nc.alloc_semaphore(f"{tag}_{n}") for n in names]

        def release():
            self.nc.clear_and_free_semaphores(got)
            self.nc.all_engine_barrier()

        ctx.callback(release)
        return got


def constants(g):
    nc, io = g.nc, g.io
    k = g.keep
    g.ident = g.sb(k, "ident", [P, P])
    g.ones = g.sb(k, "ones", [P, P])
    g.upto = g.sb(k, "upto", [P, P])
    g.before = g.sb(k, "before", [P, P])
    g.future = g.sb(k, "future", [P, P])
    g.futureT = g.sb(k, "futureT", [P, P])
    g.cos = g.sb(k, "cos", [P, NT, NFREQ])
    g.sin = g.sb(k, "sin", [P, NT, NFREQ])
    g.cols = g.sb(k, "cols", [P, P])
    g.convw = g.sb(k, "convw", [P, CONV, CT])
    g.mod = g.sb(k, "mod", [P, DEPTH, NMOD, KD])
    NV = DEPTH * NMOD * KD
    with ExitStack() as ctx:
        rows = g.sb(ctx, "rows", [P, P])
        crow = g.sb(ctx, "crow", [CONV * CT, P])
        pos_i = g.sb(ctx, "pos_i", [P, NT], I32)
        pos = g.sb(ctx, "pos", [P, NT])
        freq = g.sb(ctx, "freq", [P, NFREQ])
        ang = g.sb(ctx, "ang", [P, NT, NFREQ])
        turn = g.sb(ctx, "turn", [P, NT, NFREQ])
        turn_i = g.sb(ctx, "turn_i", [P, NT, NFREQ], I32)
        cact = g.sb(ctx, "cact", [P, KD])
        wada = [g.sb(ctx, f"wada{i}", [P, NMOD * D]) for i in range(4)]
        modrow = g.sb(ctx, "modrow", [1, NMOD * D])
        modrows = g.sb(ctx, "modrows", [DEPTH * NMOD * KD, P])
        part = g.sb(ctx, "part", [P, DVE_COLS])
        pv = g.ps(ctx, "pv", [P, 512])
        pm = [g.ps(ctx, f"pm{i}", [1, 512]) for i in range(max(PE_BANKS, DVE_BANKS))]
        (vec_in, pos_in, consts, posf, angs, rope_arg, ropes, turned, colsok, cactok, made, added,
         freqs, parts, summed, taken, mod_out, mod_in, modT) = g.sems(
            ctx, "c", "vec_in", "pos_in", "consts", "posf", "angs", "rope_arg", "ropes", "turned", "colsok", "cactok",
            "made", "added", "freqs", "parts", "summed", "taken", "mod_out", "mod_in", "modT")
        w_in = g.sems(ctx, "c", *[f"w_in{i}" for i in range(4)])
        mod_dram = nc.dram_tensor("mod_dram", [DEPTH * NMOD * KD, P], F32).ap()
        block = ctx.enter_context(nc.Block())
        ada_rows = io["ada_w"].rearrange("l (k p) n -> (l k) p n", p=P)

        @block.sync
        def _(sp):
            sp.dma_start(rows[0:NV, :], io["ada_b"].rearrange("l (n p) -> (l n) p", p=P)).then_inc(vec_in, 16)
            sp.dma_start(rows[NV:NV + KD, :], io["c"].rearrange("b (k p) -> (b k) p", p=P)).then_inc(vec_in, 16)
            sp.dma_start(rows[NV + KD:NV + KD + 2, :],
                         io["mla_q_norm"].rearrange("a (k p) -> (a k) p", p=P)).then_inc(vec_in, 16)
            sp.dma_start(rows[NV + KD + 2:NV + KD + 3, :], io["mla_kv_norm"]).then_inc(vec_in, 16)
            sp.dma_start(crow[:, :], io["gdn_conv_w"].rearrange("a j (m p) -> (a j m) p", p=P)).then_inc(vec_in, 16)
            for i in range(DEPTH * KD):
                if i >= 4:
                    sp.wait_ge(made, i - 3)
                    sp.wait_ge(parts, i - 3)
                sp.dma_start(wada[i % 4][:, :], ada_rows[i]).then_inc(w_in[i % 4], 16)

        @block.gpsimd
        def _(pool):
            with nc.allow_non_contiguous_dma(reason="1024 positions, once"):
                pool.dma_start(pos_i[:, :], io["positions"].rearrange("b (t p) -> p (b t)", p=P)).then_inc(pos_in, 16)
            ch = Chain(pool, consts)
            ch.mark(pool.memset(g.ident[:, :], 0.0))
            ch.mark(pool.memset(g.ones[:, :], 1.0))
            ch.mark(pool.memset(g.future[:, :], 0.0))
            ch.do(pool.memset(g.futureT[:, :], 0.0))
            ch.mark(pool.affine_select(out=g.ident[:, :], in_=g.ident[:, :], compare_op=ALU.not_equal, fill=1.0,
                                       base=0, pattern=[[-1, P]], channel_multiplier=1))
            ch.mark(pool.affine_select(out=g.upto[:, :], in_=g.ones[:, :], compare_op=ALU.is_ge, fill=0.0,
                                       base=0, pattern=[[1, P]], channel_multiplier=-1))
            ch.mark(pool.affine_select(out=g.before[:, :], in_=g.ones[:, :], compare_op=ALU.is_gt, fill=0.0,
                                       base=0, pattern=[[1, P]], channel_multiplier=-1))
            ch.mark(pool.affine_select(out=g.future[:, :], in_=g.future[:, :], compare_op=ALU.is_ge, fill=NEG,
                                       base=0, pattern=[[1, P]], channel_multiplier=-1))
            ch.do(pool.affine_select(out=g.futureT[:, :], in_=g.futureT[:, :], compare_op=ALU.is_ge, fill=NEG,
                                     base=0, pattern=[[-1, P]], channel_multiplier=1))
            inv = 1.0 / (np.float32(10000.0) ** (np.arange(NFREQ, dtype=np.float32) / np.float32(NFREQ)))
            for i in range(NFREQ):
                pool.memset(freq[:, i:i + 1], float(inv[i])).then_inc(freqs, 1)

        @block.tensor
        def _(pe):
            pe.wait_ge(consts, 9)
            pe.wait_ge(vec_in, 5 * 16)
            pe.transpose(pv[:, 0:NV + KD + 3], rows[0:NV + KD + 3, :], g.ident[0:NV + KD + 3, 0:NV + KD + 3])\
                .then_inc(turned, 1)
            pe.transpose(pv[:, P:P + CONV * CT], crow[:, :], g.ident[0:CONV * CT, 0:CONV * CT]).then_inc(turned, 1)
            pe.wait_ge(cactok, 1)
            for i in range(DEPTH * KD):
                layer, kk = i // KD, i % KD
                pe.wait_ge(w_in[i % 4], 16 * (i // 4 + 1))
                if i == KD:
                    pe.wait_ge(taken, PE_BANKS + DVE_BANKS)
                for n in range(PE_BANKS):
                    mm = pe.matmul(pm[n][:, :], cact[:, kk:kk + 1], wada[i % 4][:, n * 512:(n + 1) * 512],
                                   start=(kk == 0), stop=(kk == KD - 1))
                mm.then_inc(made, 1)
                if kk == KD - 1:
                    pe.wait_ge(parts, i + 1)
                    for n in range(DVE_BANKS):
                        pe.wait_ge(taken, layer * (PE_BANKS + DVE_BANKS) + PE_BANKS)
                        mm = pe.matmul(pm[n][:, :], g.ones[:, 0:1], part[:, n * 512:(n + 1) * 512],
                                       start=True, stop=True)
                    mm.then_inc(summed, 1)
            pe.wait_ge(mod_in, 16)
            pe.transpose(pv[:, 256:256 + NV], modrows[:, :], g.ident[0:NV, 0:NV]).then_inc(modT, 1)

        TWO_PI = 2.0 * math.pi
        C1 = 6.28125
        C2 = float(np.float32(TWO_PI - C1))
        C3 = float(TWO_PI - C1 - C2)

        @block.vector
        def _(dve):
            dve.wait_ge(turned, 2)
            dve.tensor_copy(g.cols[:, 0:NV + KD + 3], pv[:, 0:NV + KD + 3]).then_inc(colsok, 1)
            dve.tensor_copy(g.convw[:, :, :], pv[:, P:P + CONV * CT]).then_inc(colsok, 1)
            dve.wait_ge(pos_in, 16)
            ch = Chain(dve, angs)
            ch.do(dve.tensor_copy(pos[:, :], pos_i[:, :]))
            dve.wait_ge(freqs, NFREQ)
            for t in range(NT):
                ch.mark(dve.tensor_scalar(ang[:, t, :], freq[:, :], pos[:, t:t + 1], None, ALU.mult))
            dve.wait_ge(angs, ch.n)
            for out, quarter, n in ((g.sin, 0.0, 0), (g.cos, 0.25, 1)):
                ch.do(dve.tensor_scalar(turn[:, :, :], ang[:, :, :], 1.0 / TWO_PI, quarter, ALU.mult, ALU.add))
                ch.do(dve.tensor_copy(turn_i[:, :, :], turn[:, :, :]))
                ch.do(dve.tensor_copy(turn[:, :, :], turn_i[:, :, :]))
                ch.do(dve.scalar_tensor_tensor(out=out[:, :, :], in0=turn[:, :, :], scalar=-C1, in1=ang[:, :, :],
                                               op0=ALU.mult, op1=ALU.add))
                for less in (C2, C3):
                    ch.do(dve.scalar_tensor_tensor(out=out[:, :, :], in0=turn[:, :, :], scalar=-less,
                                                   in1=out[:, :, :], op0=ALU.mult, op1=ALU.add))
                ch.do(dve.tensor_scalar(out[:, :, :], out[:, :, :], math.pi / 2 * n, 3.1415925, ALU.add, ALU.min))
                dve.tensor_scalar(out[:, :, :], out[:, :, :], -3.1415925, None, ALU.max).then_inc(rope_arg, 1)
            ch = Chain(dve, parts)
            dve.wait_ge(cactok, 1)
            at = PE_BANKS * 512
            for i in range(DEPTH * KD):
                layer, kk = i // KD, i % KD
                dve.wait_ge(w_in[i % 4], 16 * (i // 4 + 1))
                if kk == 0:
                    if layer:
                        dve.wait_ge(summed, layer)
                    ch.do(dve.tensor_scalar(part[:, :], wada[i % 4][:, at:], cact[:, kk:kk + 1], None, ALU.mult))
                else:
                    ch.do(dve.scalar_tensor_tensor(out=part[:, :], in0=wada[i % 4][:, at:],
                                                   scalar=cact[:, kk:kk + 1], in1=part[:, :],
                                                   op0=ALU.mult, op1=ALU.add))
            dve.wait_ge(modT, 1)
            dve.wait_ge(colsok, 2)
            dve.tensor_tensor(g.mod[:, :, :, :].rearrange("p l m k -> p (l m k)"), pv[:, 256:256 + NV],
                              g.cols[:, 0:NV], ALU.add).then_inc(added, 1)
            dve.wait_ge(added, 1)
            for m in (1, 2, 4, 5):
                dve.tensor_scalar(g.mod[:, :, m, :], g.mod[:, :, m, :], 1.0, None, ALU.add).then_inc(added, 1)

        @block.scalar
        def _(act):
            act.wait_ge(colsok, 1)
            act.activation(cact[:, :], g.cols[:, NV:NV + KD], ACT.Silu).then_inc(cactok, 1)
            for n, table in enumerate((g.sin, g.cos)):
                act.wait_ge(rope_arg, n + 1)
                act.activation(table[:, :, :], table[:, :, :], ACT.Sin).then_inc(ropes, 1)
            for layer in range(DEPTH):
                act.wait_ge(made, KD * (layer + 1))
                if layer:
                    act.wait_ge(mod_out, 16 * layer)
                for n in range(PE_BANKS):
                    act.copy(modrow[:, n * 512:(n + 1) * 512], pm[n][:, :]).then_inc(taken, 1)
                act.wait_ge(summed, layer + 1)
                for n in range(DVE_BANKS):
                    m = PE_BANKS + n
                    act.copy(modrow[:, m * 512:(m + 1) * 512], pm[n][:, :]).then_inc(taken, 1)
                act.wait_ge(taken, (layer + 1) * (PE_BANKS + DVE_BANKS))
                act.dma_start(mod_dram[layer * NMOD * KD:(layer + 1) * NMOD * KD, :],
                              modrow[:, :].rearrange("a (n p) -> a n p", p=P)).then_inc(mod_out, 16)
            act.wait_ge(mod_out, 16 * DEPTH)
            act.dma_start(modrows[:, :], mod_dram).then_inc(mod_in, 16)
    g.qnorm = g.cols[:, NV + KD:NV + KD + 2]
    g.kvnorm = g.cols[:, NV + KD + 2:NV + KD + 3]


def modulate(g, tag, x_dram, layer, which):
    nc = g.nc
    with ExitStack() as ctx:
        xin = g.sb(ctx, f"{tag}_xin", [P, 4, D])
        pt = [g.ps(ctx, f"{tag}_pt{i}", [P, 512]) for i in range(4)]
        turned, *outs = g.sems(ctx, tag, "turned", "act_out", "dve_out")
        x_in = g.sems(ctx, tag, *[f"x_in{i}" for i in range(4)])
        block = ctx.enter_context(nc.Block())
        shift, scale = g.mod[:, layer, 3 * which, :], g.mod[:, layer, 3 * which + 1, :]

        @block.sync
        def _(sp):
            for t in range(NT):
                if t >= 4:
                    sp.wait_ge(turned, 2 * (t - 4) + 2)
                sp.dma_start(xin[:, t % 4, :], x_dram[t * P:(t + 1) * P, :]).then_inc(x_in[t % 4], 16)

        @block.tensor
        def _(pe):
            for t in range(NT):
                pe.wait_ge(x_in[t % 4], 16 * (t // 4 + 1))
                for half in range(2):
                    n = 2 * t + half
                    if n >= 4:
                        pe.wait_ge(outs[half], t - 1)
                    for j in range(4):
                        kk = 4 * half + j
                        mm = pe.transpose(pt[n % 4][:, j * P:(j + 1) * P], xin[:, t % 4, kk * P:(kk + 1) * P],
                                          g.ident[:, :])
                    mm.then_inc(turned, 1)

        def take(eng, half, out):
            for t in range(NT):
                n = 2 * t + half
                eng.wait_ge(turned, n + 1)
                for j in range(4):
                    kk = 4 * half + j
                    dst, src = g.hT[:, kk, t * P:(t + 1) * P], pt[n % 4][:, j * P:(j + 1) * P]
                    if half == 0:
                        ins = eng.activation(dst, src, ACT.Identity, bias=shift[:, kk:kk + 1],
                                             scale=scale[:, kk:kk + 1])
                    else:
                        ins = eng.tensor_scalar(dst, src, scale[:, kk:kk + 1], shift[:, kk:kk + 1],
                                                ALU.mult, ALU.add)
                ins.then_inc(out, 1)

        @block.scalar
        def _(act):
            take(nc.scalar, 0, outs[0])

        @block.vector
        def _(dve):
            take(nc.vector, 1, outs[1])



def bc(ap, shape):
    return ap.to_broadcast(list(shape))


def gdn_convolve(g, qkvT):
    nc, io = g.nc, g.io
    w_dram = io["hy_w_in"][0].rearrange("(k p) n -> p k n", p=P)
    with ExitStack() as ctx:
        w = [g.sb(ctx, f"gc_w{u}", [P, KD, P]) for u in range(2)]
        acc = [g.sb(ctx, f"gc_acc{u}", [P, T]) for u in range(2)]
        pq = [g.ps(ctx, f"gc_pq{u}", [P, T]) for u in range(2)]
        proj, taps = g.sems(ctx, "gc", "proj", "taps")
        convd = g.sems(ctx, "gc", "convd0", "convd1")
        silud = g.sems(ctx, "gc", "silud0", "silud1")
        w_in = g.sems(ctx, "gc", "w_in0", "w_in1")
        block = ctx.enter_context(nc.Block())

        @block.sync
        def _(sp):
            for u in range(2):
                sp.dma_start(w[u][:, :, :], w_dram[:, :, MLA_COLS + u * P:MLA_COLS + (u + 1) * P]).then_inc(w_in[u], 16)
            with sp.Fori(0, CT // 2 - 1) as i:
                for u in range(2):
                    sp.wait_ge(proj, i * 2 + (u + 1))
                    sp.dma_start(w[u][:, :, :], w_dram[:, :, bass.ds(i * (2 * P) + (MLA_COLS + (u + 2) * P), P)])\
                        .then_inc(w_in[u], 16)

        @block.tensor
        def _(pe):
            with pe.Fori(0, CT // 2) as i:
                for u in range(2):
                    pe.wait_ge(w_in[u], i * 16 + 16)
                    pe.wait_ge(convd[u], i)
                    for half in range(2):
                        for kk in range(KD):
                            mm = pe.matmul(pq[u][:, half * 512:(half + 1) * 512], w[u][:, kk, :],
                                           g.hT[:, kk, half * 512:(half + 1) * 512],
                                           start=(kk == 0), stop=(kk == KD - 1))
                    mm.then_inc(proj, 1)

        convw = g.convw[:, :, :].rearrange("p j (m u) -> p j m u", u=2)

        @block.vector
        def _(dve):
            with dve.Fori(0, CT // 2) as i:
                ch = Chain(dve, taps, i * (2 * (CONV - 1)))
                for u in range(2):
                    dve.wait_ge(proj, i * 2 + (u + 1))
                    dve.wait_ge(silud[u], i)
                    x, a = pq[u], acc[u]
                    ch.do(dve.tensor_scalar(a[:, :], x[:, :], convw[:, CONV - 1, bass.ds(i, 1), u], None, ALU.mult))
                    for back in range(1, CONV):
                        ins = dve.scalar_tensor_tensor(out=a[:, back:], in0=x[:, 0:T - back],
                                                       scalar=convw[:, CONV - 1 - back, bass.ds(i, 1), u],
                                                       in1=a[:, back:], op0=ALU.mult, op1=ALU.add)
                        if back < CONV - 1:
                            ch.do(ins)
                        else:
                            ins.then_inc(convd[u], 1)

        @block.scalar
        def _(act):
            with act.Fori(0, CT // 2) as i:
                for u in range(2):
                    act.wait_ge(convd[u], i + 1)
                    act.activation(qkvT[:, bass.ds(i * 2 + u, 1), 0:T].rearrange("p a t -> p (a t)"), acc[u][:, :],
                                   ACT.Silu).then_inc(silud[u], 1)


def hybrid_inputs(g, o):
    nc, io = g.nc, g.io
    w_dram = io["hy_w_in"][0].rearrange("(k p) n -> p k n", p=P)
    ab0 = MLA_COLS + QKV
    gate0 = ab0 + 2 * HEADS
    NA = MLA_COLS + 2 * HEADS
    GW = HEADS * GD
    HR = ROPE // 2
    with ExitStack() as ctx:
        wa = g.sb(ctx, "hi_wa", [P, KD, NA])
        wg = g.sb(ctx, "hi_wg", [P, KD, GW])
        wq = g.sb(ctx, "hi_wq", [P, 2, HEADS * QD])
        wv = g.sb(ctx, "hi_wv", [P, HEADS, NOPE + VD])
        lat = g.sb(ctx, "hi_lat", [P, NT, NA])
        latT = o.latT
        junk = g.sb(ctx, "hi_junk", [P, QR])
        ss = g.sb(ctx, "hi_ss", [P, NT, 2])
        rs = g.sb(ctx, "hi_rs", [P, NT, 2])
        kr = g.sb(ctx, "hi_kr", [P, NT, ROPE])
        tmp = [g.sb(ctx, f"hi_tmp{i}", [P, NT, HR]) for i in range(2)]
        qt = [g.sb(ctx, f"hi_qt{i}", [P, HEADS, HR]) for i in range(2)]
        pa = [g.ps(ctx, f"hi_pa{i}", [P, 512]) for i in range(2)]
        pg = [g.ps(ctx, f"hi_pg{i}", [P, 512]) for i in range(2)]
        pq = [g.ps(ctx, f"hi_pq{i}", [P, 1024]) for i in range(2)]
        (w_in, gate_w_in, w2_in, proj, gated, copied, squared, msd, rsd, lnd, scaled, roped, latTd, latTok, krTd, krTok, vd, vok,
         qd, qrope) = g.sems(
            ctx, "hi", "w_in", "gate_w_in", "w2_in", "proj", "gated", "copied", "squared", "msd", "rsd", "lnd", "scaled", "roped",
            "latTd", "latTok", "krTd", "krTok", "vd", "vok", "qd", "qrope")
        block = ctx.enter_context(nc.Block())
        GROUPS = [(part, half) for half in range(2) for part in range(3)]

        @block.sync
        def _(sp):
            sp.dma_start(wa[:, :, 0:MLA_COLS], w_dram[:, :, 0:MLA_COLS]).then_inc(w_in, 16)
            sp.dma_start(wa[:, :, MLA_COLS:NA], w_dram[:, :, ab0:gate0]).then_inc(w_in, 16)
            sp.dma_start(wg[:, :, :], w_dram[:, :, gate0:HY_IN]).then_inc(gate_w_in, 16)
            sp.dma_start(wq[:, :, :], io["mla_w_uq"][0].rearrange("(k p) n -> p k n", p=P)).then_inc(w2_in, 16)
            sp.dma_start(wv[:, :, :], io["mla_w_ukv"][0].rearrange("p (h n) -> p h n", h=HEADS)).then_inc(w2_in, 16)

        @block.tensor
        def _(pe):
            pe.wait_ge(w_in, 2 * 16)
            for t in range(NT):
                b = t % 2
                if t >= 2:
                    pe.wait_ge(copied, t - 1)
                    pe.wait_ge(gated, t - 1)
                for kk in range(KD):
                    pe.matmul(pa[b][:, 0:NA], g.hT[:, kk, t * P:(t + 1) * P], wa[:, kk, :],
                              start=(kk == 0), stop=(kk == KD - 1))
                if t == 0:
                    pe.wait_ge(gate_w_in, 16)
                for kk in range(KD):
                    mm = pe.matmul(pg[b][:, :], g.hT[:, kk, t * P:(t + 1) * P], wg[:, kk, :],
                                   start=(kk == 0), stop=(kk == KD - 1))
                mm.then_inc(proj, 1)
            pe.wait_ge(copied, NT)
            pe.wait_ge(gated, NT)
            for n, (part, half) in enumerate(GROUPS):
                pe.wait_ge(scaled, 2 * NT)
                if n >= 2:
                    pe.wait_ge(latTok, n - 1)
                for j in range(4):
                    t = 4 * half + j
                    mm = pe.transpose(pa[n % 2][:, j * P:(j + 1) * P], lat[:, t, part * P:(part + 1) * P], g.ident[:, :])
                mm.then_inc(latTd, 1)
            pe.wait_ge(roped, 6)
            for half in range(2):
                for j in range(4):
                    t = 4 * half + j
                    mm = pe.transpose(pg[half][0:ROPE, j * P:(j + 1) * P], kr[:, t, :], g.ident[:, :])
                mm.then_inc(krTd, 1)
            pe.wait_ge(latTok, len(GROUPS))
            pe.wait_ge(krTok, 2)
            pe.wait_ge(w2_in, 2 * 16)
            for t in range(NT):
                b = t % 2
                if t >= 2:
                    pe.wait_ge(vok, t - 1)
                    pe.wait_ge(qrope, 14 * (t - 1))
                pe.matmul(pa[b][:, :], latT[:, 2, t * P:(t + 1) * P], wv[:, :, NOPE:NOPE + VD],
                          start=True, stop=True).then_inc(vd, 1)
                for c0, c1 in ((0, 480), (480, 768)):
                    at = 0 if c0 == 0 else 512
                    for kk in range(2):
                        mm = pe.matmul(pq[b][:, at:at + c1 - c0], latT[:, kk, t * P:(t + 1) * P], wq[:, kk, c0:c1],
                                       start=(kk == 0), stop=(kk == 1))
                mm.then_inc(qd, 1)

        @block.scalar
        def _(act):
            for t in range(NT):
                act.wait_ge(proj, t + 1)
                act.activation(o.gate[:, t, :], pg[t % 2][:, :], ACT.Silu).then_inc(gated, 1)
            for t in range(NT):
                act.wait_ge(copied, t + 1)
                for j, (a, b) in enumerate(((0, QR), (QR, QR + KVR))):
                    if j or t:
                        act.wait_ge(squared, 2 * t + j)
                    act.activation(junk[:, 0:b - a], lat[:, t, a:b], ACT.Square,
                                   accum_out=ss[:, t, j:j + 1]).then_inc(squared, 1)
            act.wait_ge(msd, 2)
            act.activation(rs[:, :, :], ss[:, :, :], ACT.Ln).then_inc(lnd, 1)
            act.wait_ge(lnd, 1)
            act.activation(rs[:, :, :], rs[:, :, :], ACT.Exp, scale=-0.5).then_inc(rsd, 1)
            for n, (part, half) in enumerate(GROUPS):
                act.wait_ge(latTd, n + 1)
                gain = g.qnorm[:, part:part + 1] if part < 2 else g.kvnorm
                act.activation(latT[:, part, half * 512:(half + 1) * 512], pa[n % 2][:, :], ACT.Copy,
                               scale=gain).then_inc(latTok, 1)
            for half in range(2):
                act.wait_ge(krTd, half + 1)
                act.copy(o.krT[:, half * 512:(half + 1) * 512], pg[half][0:ROPE, :]).then_inc(krTok, 1)
            for t in range(NT):
                act.wait_ge(vd, t + 1)
                act.copy(o.v[:, t, :], pa[t % 2][:, :]).then_inc(vok, 1)

        @block.vector
        def _(dve):
            for t in range(NT):
                dve.wait_ge(proj, t + 1)
                dve.tensor_copy(lat[:, t, :], pa[t % 2][:, 0:NA]).then_inc(copied, 1)
            dve.wait_ge(copied, NT)
            dve.tensor_copy(o.ab[:, :, :], lat[:, :, MLA_COLS:NA])
            dve.wait_ge(squared, 2 * NT)
            for j, n in enumerate((QR, KVR)):
                dve.tensor_scalar(ss[:, :, j], ss[:, :, j], 1.0 / n, RMS_EPS, ALU.mult, ALU.add).then_inc(msd, 1)

            def rope(ch, out1, out2, x1, x2, cos, sin, ta, tb):
                ch.mark(dve.tensor_tensor(ta, x1, cos, ALU.mult))
                ch.do(dve.tensor_tensor(tb, x2, sin, ALU.mult))
                ch.do(dve.tensor_tensor(out1, ta, tb, ALU.subtract))
                ch.mark(dve.tensor_tensor(ta, x1, sin, ALU.mult))
                ch.do(dve.tensor_tensor(tb, x2, cos, ALU.mult))
                ch.do(dve.tensor_tensor(out2, ta, tb, ALU.add))

            k0 = QR + KVR
            rope(Chain(dve, roped), kr[:, :, 0:HR], kr[:, :, HR:ROPE], lat[:, :, k0:k0 + HR],
                 lat[:, :, k0 + HR:k0 + ROPE], g.cos[:, :, 0:NFREQ:4], g.sin[:, :, 0:NFREQ:4],
                 tmp[0][:, :, :], tmp[1][:, :, :])
            dve.wait_ge(rsd, 1)
            for t in range(NT):
                for j, (a, b) in enumerate(((0, QR), (QR, QR + KVR))):
                    dve.tensor_scalar(lat[:, t, a:b], lat[:, t, a:b], rs[:, t, j:j + 1], None, ALU.mult)\
                        .then_inc(scaled, 1)
            ch = Chain(dve, qrope)
            for t in range(NT):
                dve.wait_ge(qd, t + 1)
                for c0, heads in ((0, range(0, 5)), (512, range(5, 8))):
                    n = len(heads)
                    src = pq[t % 2][:, c0:c0 + n * QD].rearrange("p (h d) -> p h d", d=QD)
                    dst = o.q[:, t, heads[0]:heads[0] + n, :]
                    cos = bc(g.cos[:, t, 0:NFREQ:4].unsqueeze(1), [P, n, HR])
                    sin = bc(g.sin[:, t, 0:NFREQ:4].unsqueeze(1), [P, n, HR])
                    last = Chain(dve, qrope, ch.n)
                    rope(last, dst[:, :, NOPE:NOPE + HR], dst[:, :, NOPE + HR:QD], src[:, :, NOPE:NOPE + HR],
                         src[:, :, NOPE + HR:QD], cos, sin, qt[0][:, 0:n, :], qt[1][:, 0:n, :])
                    ch.n += last.n
                    ch.do(dve.tensor_copy(dst[:, :, 0:NOPE], src[:, :, 0:NOPE]))


def attention(g, o):
    nc, io = g.nc, g.io
    NB = T // P
    ITEMS = [(u, i) for u in range(2) for i in range(NB)]
    HALVES = [(n, b) for n, (u, i) in enumerate(ITEMS) for b in range(i // 4 + 1)]
    NI, NH = len(ITEMS), len(HALVES)
    upto_item = [sum(1 for m, _ in HALVES if m <= n) for n in range(NI)]
    with ExitStack() as ctx:
        wk_all = g.sb(ctx, "at_wk_all", [P, HEADS, NOPE])
        wk = [g.sb(ctx, f"at_wk{u}", [P, NOPE]) for u in range(2)]
        qs = [g.sb(ctx, f"at_qs{u}", [P, NT, QD]) for u in range(2)]
        qT = [g.sb(ctx, f"at_qT{u}", [QD, T]) for u in range(2)]
        kT = [g.sb(ctx, f"at_kT{u}", [QD, T]) for u in range(2)]
        p = [g.sb(ctx, f"at_p{u}", [P, T]) for u in range(2)]
        pT = [g.sb(ctx, f"at_pT{u}", [P, NB, P]) for u in range(2)]
        otok = g.sb(ctx, "at_o", [P, NT, 2 * VD])
        nmax = g.sb(ctx, "at_nmax", [P, NI])
        tot = g.sb(ctx, "at_tot", [P, NI])
        inv = g.sb(ctx, "at_inv", [P, NI])
        sc = [g.ps(ctx, f"at_s{u}", [P, T]) for u in range(2)]
        pt = [g.ps(ctx, f"at_pt{u}", [P, 512]) for u in range(2)]
        po = [g.ps(ctx, f"at_po{u}", [P, 512]) for u in range(2)]
        (w_in, krok, staged, kd, qd, kok, qok, scored, maxed, probs, turned, pTok, pv, topd, invd, normed, oTd, oTok) = g.sems(
            ctx, "at", "w_in", "krok", "staged", "kd", "qd", "kok", "qok", "scored", "maxed", "probs", "turned", "pTok",
            "pv", "topd", "invd", "normed", "oTd", "oTok")
        block = ctx.enter_context(nc.Block())
        PAIR = HEADS // 2

        @block.sync
        def _(sp):
            sp.dma_start(wk_all[:, :, :], io["mla_w_ukv"][0].rearrange("p (h n) -> p h n", h=HEADS)[:, :, 0:NOPE])\
                .then_inc(w_in, 16)

        @block.gpsimd
        def _(pool):
            pool.wait_ge(w_in, 16)
            with pool.Fori(0, PAIR) as m:
                for u in range(2):
                    pool.wait_ge(kd, m * 2)
                    pool.wait_ge(qd, m * 2)
                    qp = o.q[:, :, :, :].rearrange("p t (m u) d -> p t m u d", u=2)
                    wp = wk_all[:, :, :].rearrange("p (m u) d -> p m u d", u=2)
                    pool.tensor_copy(qs[u][:, :, :], qp[:, :, bass.ds(m, 1), u, :].rearrange("p t a d -> p t (a d)"))\
                        .then_inc(staged, 1)
                    pool.tensor_copy(wk[u][:, :], wp[:, bass.ds(m, 1), u, :].rearrange("p a d -> p (a d)"))\
                        .then_inc(staged, 1)

        @block.tensor
        def _(pe):
            def scores(m, n):
                u, i = ITEMS[n]
                s = sc[n % 2]
                pe.wait_ge(probs, m * NI + max(n - 1, 0))
                end = (i + 1) * P
                for c0 in range(0, end, 512):
                    c1 = min(c0 + 512, end)
                    pe.matmul(s[:, c0:c1], qT[u][:, i * P:end], kT[u][:, c0:c1], start=True, stop=(c1 < end))
                pe.matmul(s[:, i * P:end], g.ident[:, :], g.futureT[:, :], start=False, stop=True).then_inc(scored, 1)

            def values(m, n):
                u, i = ITEMS[n]
                for b in range(i // 4 + 1):
                    h = HALVES.index((n, b))
                    pe.wait_ge(probs, m * NI + n + 1)
                    pe.wait_ge(pTok, m * NH + max(h - 1, 0))
                    for j in range(4 * b, min(4 * b + 4, i + 1)):
                        mm = pe.transpose(pt[h % 2][:, (j - 4 * b) * P:(j - 4 * b + 1) * P],
                                          p[n % 2][:, j * P:(j + 1) * P], g.ident[:, :])
                    mm.then_inc(turned, 1)
                if n + 2 < NI:
                    scores(m, n + 2)
                pe.wait_ge(normed, m * NI + max(n - 1, 0))
                pe.wait_ge(pTok, m * NH + upto_item[n])
                for j in range(i + 1):
                    mm = pe.matmul(po[n % 2][:, 0:VD], pT[n % 2][:, j, :], o.v[:, j, bass.ds(m * (2 * VD) + u * VD, VD)],
                                   start=(j == 0), stop=(j == i))
                mm.then_inc(pv, 1)

            pe.wait_ge(krok, 2)
            with pe.Fori(0, PAIR) as m:
                for u in range(2):
                    pe.wait_ge(staged, m * 4 + (2 * u + 2))
                    pe.wait_ge(probs, m * NI)
                    pe.wait_ge(oTok, m)
                    pe.wait_ge(kok, m * 2 + u)
                    for c in range(2):
                        mm = pe.matmul(sc[0][0:NOPE, c * 512:(c + 1) * 512], wk[u][:, :],
                                       o.latT[:, 2, c * 512:(c + 1) * 512], start=True, stop=True)
                    mm.then_inc(kd, 1)
                    pe.wait_ge(qok, m * 2 + u)
                    for t in range(NT):
                        mm = pe.transpose(sc[1][0:QD, t * P:(t + 1) * P], qs[u][:, t, :], g.ident[:, :])
                    mm.then_inc(qd, 1)
                pe.wait_ge(kok, m * 2 + 2)
                pe.wait_ge(qok, m * 2 + 2)
                scores(m, 0)
                scores(m, 1)
                for n in range(NI):
                    values(m, n)
                pe.wait_ge(normed, m * NI + NI)
                for t in range(NT):
                    mm = pe.transpose(sc[0][:, t * P:(t + 1) * P], otok[:, t, :], g.ident[:, :])
                mm.then_inc(oTd, 1)

        @block.scalar
        def _(act):
            for u in range(2):
                act.copy(kT[u][NOPE:QD, :], o.krT[:, :]).then_inc(krok, 1)
            with act.Fori(0, PAIR) as m:
                for u in range(2):
                    act.wait_ge(kd, m * 2 + (u + 1))
                    act.copy(kT[u][0:NOPE, :], sc[0][0:NOPE, :]).then_inc(kok, 1)
                for n, (u, i) in enumerate(ITEMS):
                    act.wait_ge(maxed, m * NI + n + 1)
                    act.wait_ge(turned, m * NH + (upto_item[n - 2] if n >= 2 else 0))
                    act.activation(p[n % 2][:, 0:(i + 1) * P], sc[n % 2][:, 0:(i + 1) * P], ACT.Exp,
                                   bias=nmax[:, n:n + 1], scale=MLA_SCALE, accum_out=tot[:, n:n + 1]).then_inc(probs, 1)
                act.wait_ge(oTd, m + 1)
                act.copy(o.mixT[:, bass.ds(m, 1), :].rearrange("p a t -> p (a t)"), sc[0][:, :]).then_inc(oTok, 1)

        @block.vector
        def _(dve):
            def top(m, n):
                u, i = ITEMS[n]
                dve.wait_ge(scored, m * NI + n + 1)
                dve.tensor_reduce(tot[:, n:n + 1], sc[n % 2][:, 0:(i + 1) * P], AX.X, ALU.max).then_inc(topd, 1)
                dve.wait_ge(topd, m * NI + n + 1)
                dve.tensor_scalar(nmax[:, n:n + 1], tot[:, n:n + 1], -MLA_SCALE, None, ALU.mult).then_inc(maxed, 1)

            with dve.Fori(0, PAIR) as m:
                for u in range(2):
                    dve.wait_ge(qd, m * 2 + (u + 1))
                    dve.tensor_copy(qT[u][:, :], sc[1][0:QD, :]).then_inc(qok, 1)
                top(m, 0)
                top(m, 1)
                for n, (u, i) in enumerate(ITEMS):
                    for b in range(i // 4 + 1):
                        h = HALVES.index((n, b))
                        nb = min(4, i + 1 - 4 * b)
                        dve.wait_ge(turned, m * NH + h + 1)
                        dve.wait_ge(pv, m * NI + max(n - 1, 0))
                        dve.tensor_copy(pT[n % 2][:, 4 * b:4 * b + nb, :].rearrange("p j q -> p (j q)"),
                                        pt[h % 2][:, 0:nb * P]).then_inc(pTok, 1)
                    if n + 2 < NI:
                        top(m, n + 2)
                    dve.wait_ge(probs, m * NI + n + 1)
                    dve.reciprocal(inv[:, n:n + 1], tot[:, n:n + 1]).then_inc(invd, 1)
                    dve.wait_ge(invd, m * NI + n + 1)
                    dve.wait_ge(pv, m * NI + n + 1)
                    dve.wait_ge(oTd, m)
                    dve.tensor_scalar(otok[:, i, u * VD:(u + 1) * VD], po[n % 2][:, 0:VD], inv[:, n:n + 1], None,
                                      ALU.mult).then_inc(normed, 1)


def delta_rule(g, o, qkvT):
    nc, io = g.nc, g.io
    H, C = HEADS, P
    LEVELS = 7
    PADS = 4
    W = H * GD
    with ExitStack() as ctx:
        sb = lambda name, shape, dt=F32: g.sb(ctx, "dr_" + name, shape, dt)
        dtb = sb("dtb", [P, H])
        alog = sb("alog", [P, H])
        onorm = sb("onorm", [P, GD])
        sp1 = sb("sp1", [P, NT, H])
        sp2 = sb("sp2", [P, NT, H])
        sp3 = sb("sp3", [P, NT, H])
        la_all = sb("la", [P, NT + 2, H])
        beta_all = sb("beta", [P, NT + 1, H])
        osq = sb("osq", [P, W])
        level = sb("level", [P, LEVELS, C])
        raw = sb("raw", [P, CT, C])
        lac = sb("lac", [P, H])
        sq = sb("sq", [P, 2 * W])
        ssq = sb("ssq", [P, 2 * H])
        rn = sb("rn", [P, 2 * H])
        qn, kn, kb, kbg, kdec, vb, vb_next = (
            sb(n, [P, H, GD]) for n in ("qn", "kn", "kb", "kbg", "kdec", "vb", "vb_next"))
        qT, kT, kbT = (sb(n, [P, H // 2, C]) for n in ("qT", "kT", "kbT"))
        dec = [sb(f"dec{i}", [P, 4, C]) for i in range(2)]
        gtmp = [sb(f"gtmp{i}", [P, 4, C]) for i in range(2)]
        gcol = sb("gcol", [P, H])
        eg = sb("eg", [P, H])
        egl = sb("egl", [P, H // 2])
        glast = sb("glast", [P, H // 2])
        LT = [sb(f"LT{i}", [P, 4, C]) for i in range(2)]
        AT = [sb(f"AT{i}", [P, 4, C]) for i in range(2)]
        LM = [[sb(f"LM{i}_{b}", [P, 4, C]) for b in range(2)] for i in range(2)]
        Pm = [sb(f"Pm{i}", [P, 4, C]) for i in range(2)]
        Tm = [sb(f"Tm{i}", [P, 4, C]) for i in range(2)]
        Sm = [sb(f"Sm{i}", [P, 4, C]) for i in range(2)]
        wT = sb("wT", [P, H // 2, C])
        vn = sb("vn", [P, H, GD])
        state = sb("state", [P, H // 2, GD])
        osb = sb("osb", [P, H, GD])
        oss = sb("oss", [P, H])
        ors = sb("ors", [P, H])
        la, beta = la_all[:, 0:NT, :], beta_all[:, 0:NT, :]
        bank = [g.ps(ctx, f"dr_b{i}", [P, 512]) for i in range(8)]
        names = ("vec_in masks pre_a pre_b pre_c pre_d ones_state rawc rawT sqd ssqd lnr rnd qnd knd kbd kbgd kdecd vbd lacd gb gdiag "
                 "gcold gsub decd egd egld tT qTd kTd kbTd ltm ltd atm atd lmd pm pd wm tmd smd um wTm wTd vnm vn0 vnd "
                 "om tmp1 oq od kvm std osq ossd ors1 ors2 yd yT mixd tmp2 vbc glastd free pads gained").split()
        S = dict(zip(names, g.sems(ctx, "dr", *names)))
        block = ctx.enter_context(nc.Block())

        def w4(ap):
            return ap.rearrange("p (h d) -> p h d", d=GD)

        def m4(ap):
            return ap.rearrange("p (h c) -> p h c", c=C)

        def col(ap, n, d):
            return bc(ap.unsqueeze(2), [P, n, d])

        @block.sync
        def _(sp):
            sp.dma_start(dtb[:, :], io["gdn_dt_bias"].partition_broadcast(P)).then_inc(S["vec_in"], 16)
            sp.dma_start(alog[:, :], io["gdn_a_log"].partition_broadcast(P)).then_inc(S["vec_in"], 16)
            sp.dma_start(onorm[:, :], io["gdn_norm"].partition_broadcast(P)).then_inc(S["vec_in"], 16)

        @block.gpsimd
        def _(pool):
            ch = Chain(pool, S["pads"])
            ch.do(pool.memset(state[:, :, :], 0.0))
            ch.mark(pool.memset(la_all[:, NT:, :], 0.0))
            ch.mark(pool.memset(beta_all[:, NT:, :], 0.0))
            ch.do(pool.memset(qkvT[:, :, T:], 0.0))
            pool.wait_ge(S["pre_d"], 1)

            def stage(n, first=False):
                if not first:
                    pool.wait_ge(S["rawT"], n * 3)
                    pool.wait_ge(S["gb"], n * 2)
                pool.tensor_copy(raw[:, :, :], qkvT[:, :, bass.ds(n * C, C)]).then_inc(S["rawc"], 1)
                pool.tensor_copy(lac[:, :], la_all[:, bass.ds(n, 1), :].rearrange("p a h -> p (a h)"))\
                    .then_inc(S["lacd"], 1)

            def chunk(n, first=False):
                pool.wait_ge(S["vbd"], n + 1)
                if not first:
                    pool.wait_ge(S["vnm"], n)
                    pool.sem_inc(S["free"], 1)
                pool.tensor_copy(vb[:, :, :], vb_next[:, :, :]).then_inc(S["vbc"], 1)
                pool.wait_ge(S["kbd"], n + 1)
                pool.wait_ge(S["egd"], n + 1)
                if not first:
                    pool.wait_ge(S["wTm"], n)
                pool.tensor_tensor(kbg[:, :, :], kb[:, :, :], col(eg[:, :], H, GD), ALU.mult).then_inc(S["kbgd"], 1)
                pool.wait_ge(S["decd"], n * 2 + 2)
                if not first:
                    pool.wait_ge(S["kvm"], n)
                for i in range(2):
                    pool.tensor_tensor(kdec[:, i::2, :], kn[:, i::2, :],
                                       bc(dec[i][:, :, C - 1:C], [P, 4, GD]), ALU.mult).then_inc(S["kdecd"], 1)
                for s_ in range(LEVELS):
                    for i in range(2):
                        pool.wait_ge(S["ltd"], n * 2 + i + 1)
                        if s_ >= 2:
                            pool.wait_ge(S["pm"], n * (2 * LEVELS) + 2 * (s_ - 2) + i + 1)
                            if s_ == 2:
                                pool.wait_ge(S["smd"], n * (2 * LEVELS) + i + 1)
                        elif not first:
                            pool.wait_ge(S["pm"], n * (2 * LEVELS))
                        pool.tensor_tensor(LM[i][s_ % 2][:, :, :], LT[i][:, :, :],
                                           bc(level[:, s_, :].unsqueeze(1), [P, 4, C]), ALU.mult).then_inc(S["lmd"], 1)
                stage(n + 2)
                pool.wait_ge(S["vnm"], n + 1)
                pool.wait_ge(S["om"], n + 1)
                pool.wait_ge(S["egld"], n * 2 + 2)
                if not first:
                    pool.wait_ge(S["std"], n)
                pool.tensor_tensor(state[:, :, :], state[:, :, :], col(egl[:, :], H // 2, GD), ALU.mult)\
                    .then_inc(S["ones_state"], 1)

            stage(0, first=True)
            ch = Chain(pool, S["masks"])
            for s_ in range(LEVELS):
                n = 2 ** s_
                m = level[:, s_, :].rearrange("p (b e i) -> p b e i", e=2, i=n)
                ch.do(pool.memset(level[:, s_, :], 0.0))
                ch.do(pool.memset(m[:, :, 1, :], 1.0))
                odd = m[:, :, 1, :]
                ch.do(pool.affine_select(out=odd, in_=odd, compare_op=ALU.is_ge, fill=0.0, base=0,
                                         pattern=[[-2 * n, C // (2 * n)], [0, n]], channel_multiplier=1))
                ch.do(pool.affine_select(out=odd, in_=odd, compare_op=ALU.is_gt, fill=0.0, base=n,
                                         pattern=[[2 * n, C // (2 * n)], [0, n]], channel_multiplier=-1))
            pool.wait_ge(S["vec_in"], 48)
            ch = Chain(pool, S["gained"])
            for t in range(NT):
                gt = w4(o.gate[:, t, :])
                ch.do(pool.tensor_tensor(gt, gt, bc(onorm[:, :].unsqueeze(1), [P, H, GD]), ALU.mult))
            stage(1)
            chunk(0, first=True)
            with pool.Fori(1, NT) as n:
                chunk(n)

        @block.tensor
        def _(pe):
            wait = lambda name, v: pe.wait_ge(S[name], v)

            def part(h):
                return slice(64 * (h % 2), 64 * (h % 2) + 64)

            wait("pads", PADS)
            wait("pre_d", 1)

            def raw_qk(n):
                wait("rawc", n + 1)
                for j in range(2):
                    for m in range(4):
                        mm = pe.transpose(bank[6 + j][:, m * C:(m + 1) * C], raw[:, 4 * j + m, :], g.ident[:, :])
                    mm.then_inc(S["rawT"], 1)

            def raw_v(n):
                wait("qnd", n + 1)
                for m in range(4):
                    mm = pe.transpose(bank[6][:, m * C:(m + 1) * C], raw[:, 8 + m, :], g.ident[:, :])
                mm.then_inc(S["rawT"], 1)

            def log_decays(n, i):
                wait("lacd", n + 1)
                wait("vbd" if i else "knd", n + 1)
                b = bank[7 - i]
                pe.matmul(b[:, :], g.ident[:, :], bc(g.future[:, :].unsqueeze(1), [P, 4, C]), start=True, stop=False)
                for hh in range(4):
                    h = 2 * hh + i
                    mm = pe.matmul(b[:, hh * C:(hh + 1) * C], bc(lac[:, h:h + 1], [P, C]), g.upto[:, :],
                                   start=False, stop=(hh == 3))
                mm.then_inc(S["gb"], 1)

            def chunk(n, first=False):
                for j, (src, ready) in enumerate(((qn, "qnd"), (kn, "knd"), (kb, "kbd"))):
                    wait(ready, n + 1)
                    for m in range(4):
                        mm = pe.transpose(bank[j][:, m * C:(m + 1) * C],
                                          src[:, 2 * m:2 * m + 2, :].rearrange("p h d -> p (h d)"), g.ident[:, :])
                    mm.then_inc(S["tT"], 1)
                if not first:
                    wait("od", n * 2)
                wait("kTd", n + 1)
                wait("kbTd", n + 1)
                wait("decd", n * 2 + 2)
                for i in range(2):
                    for hh in range(4):
                        h = 2 * hh + i
                        mm = pe.matmul(bank[3 + i][:, hh * C:(hh + 1) * C], kT[part(h), h // 2, :], kbT[part(h), h // 2, :],
                                       start=True, stop=True)
                    mm.then_inc(S["ltm"], 1)
                wait("qTd", n + 1)
                for i in range(2):
                    for hh in range(4):
                        h = 2 * hh + i
                        mm = pe.matmul(bank[6 + i][:, hh * C:(hh + 1) * C], kT[part(h), h // 2, :], qT[part(h), h // 2, :],
                                       start=True, stop=True)
                    mm.then_inc(S["atm"], 1)
                if not first:
                    output_turn(n - 1)
                for s_ in range(LEVELS):
                    for i in range(2):
                        wait("lmd", n * (2 * LEVELS) + 2 * s_ + i + 1)
                        wait("ltd", n * 2 + 2)
                        if s_:
                            wait("tmd", n * (2 * LEVELS - 2) + 2 * (s_ - 1) + i + 1)
                        for hh in range(4):
                            rhs = Tm[i][:, hh, :] if s_ else g.ident[:, :]
                            mm = pe.matmul(bank[i][:, hh * C:(hh + 1) * C], LM[i][s_ % 2][:, hh, :], rhs,
                                           start=True, stop=True)
                        mm.then_inc(S["pm"], 1)
                    if s_ == 0:
                        continue
                    if s_ == 1 and not first:
                        wait("mixd", n)
                    for i in range(2):
                        wait("smd", n * (2 * LEVELS) + 2 * (s_ - 1) + i + 1)
                        wait("pd", n * (2 * LEVELS - 2) + 2 * (s_ - 1) + i + 1)
                        if s_ < LEVELS - 1:
                            for hh in range(4):
                                pe.matmul(bank[2 + i][:, hh * C:(hh + 1) * C], Sm[i][:, hh, :], Pm[i][:, hh, :],
                                          start=True, stop=True)
                        for hh in range(4):
                            mm = pe.matmul(bank[4 + i][:, hh * C:(hh + 1) * C], Pm[i][:, hh, :], Sm[i][:, hh, :],
                                           start=True, stop=True)
                        mm.then_inc(S["wm"], 1)
                    if s_ == 1:
                        wait("atd", n * 2 + 2)
                        raw_qk(n + 1)
                    elif s_ == 4:
                        raw_v(n + 1)
                        log_decays(n + 1, 0)
                    elif s_ == 5:
                        log_decays(n + 1, 1)
                wait("smd", n * (2 * LEVELS) + 2 * LEVELS)
                wait("kbgd", n + 1)
                for h in range(H):
                    mm = pe.matmul(bank[0][part(h), (h // 2) * C:(h // 2 + 1) * C], kbg[:, h, :],
                                   Sm[h % 2][:, h // 2, :], start=True, stop=True, skip_group_check=True)
                mm.then_inc(S["wTm"], 1)
                wait("vbc", n + 1)
                for h in range(H):
                    pe.matmul(bank[1 + h % 2][:, h // 2 * GD:(h // 2 + 1) * GD], Sm[h % 2][:, h // 2, :], vb[:, h, :],
                              start=(h < 2), stop=False, skip_group_check=True)
                wait("wTd", n + 1)
                for h in range(H):
                    mm = pe.matmul(bank[1 + h % 2][:, h // 2 * GD:(h // 2 + 1) * GD], wT[part(h), h // 2, :],
                                   state[part(h), h // 2, :], start=False, stop=True, skip_group_check=True)
                mm.then_inc(S["vnm"], 1)
                wait("gsub", n * 2 + 4)
                for h in range(H):
                    mm = pe.matmul(bank[3 + 3 * (h % 2)][:, h // 2 * GD:(h // 2 + 1) * GD], qT[part(h), h // 2, :],
                                   state[part(h), h // 2, :], start=True, stop=True)
                wait("vn0", n + 1)
                wait("vnd", n + 1)
                for h in range(H):
                    mm = pe.matmul(bank[4 + 3 * (h % 2)][:, h // 2 * GD:(h // 2 + 1) * GD], AT[h % 2][:, h // 2, :],
                                   vn[:, h, :], start=True, stop=True)
                mm.then_inc(S["om"], 1)
                wait("kdecd", n * 2 + 2)
                for h in range(H):
                    mm = pe.matmul(bank[5][part(h), (h // 2) * GD:(h // 2 + 1) * GD], kdec[:, h, :], vn[:, h, :],
                                   start=True, stop=True, skip_group_check=True)
                mm.then_inc(S["kvm"], 1)

            def output_turn(n):
                wait("std", n + 1)
                wait("yd", n * 2 + 2)
                for m in range(4):
                    mm = pe.transpose(bank[5][:, m * C:(m + 1) * C],
                                      osb[:, 2 * m:2 * m + 2, :].rearrange("p h d -> p (h d)"), g.ident[:, :])
                mm.then_inc(S["yT"], 1)

            raw_qk(0)
            raw_v(0)
            for i in range(2):
                log_decays(0, i)
            chunk(0, first=True)
            with pe.Fori(1, NT) as n:
                chunk(n)
            output_turn(NT - 1)

        @block.scalar
        def _(act):
            wait = lambda name, v: act.wait_ge(S[name], v)
            ch = Chain(act, S["pre_a"])
            wait("pre_b", 1)
            ch.do(act.activation(sp2[:, :, :], sp2[:, :, :], ACT.Exp))
            ch.do(act.activation(beta[:, :, :], beta[:, :, :], ACT.Exp))
            ch.do(act.activation(alog[:, :], alog[:, :], ACT.Exp))
            ch.do(act.activation(sp3[:, :, :], sp2[:, :, :], ACT.Ln, bias=1.0))

            def squares(n):
                for j in range(2):
                    wait("rawT", n * 3 + j + 1)
                    wait("ssqd", n)
                    act.activation(sq[:, j * W:(j + 1) * W], bank[6 + j][:, :], ACT.Square).then_inc(S["sqd"], 1)

            def roots(n):
                wait("ssqd", n + 1)
                act.activation(rn[:, :], ssq[:, :], ACT.Ln).then_inc(S["lnr"], 1)
                wait("lnr", n + 1)
                act.activation(rn[:, :], rn[:, :], ACT.Exp, scale=-0.5).then_inc(S["rnd"], 1)

            def last_decays(n):
                for i in range(2):
                    half = slice(64 * i, 64 * i + 64)
                    wait("gcold", n * 2 + 2)
                    wait("egld", n * 2)
                    act.copy(glast[half, :], m4(bank[7 - i][half, :])[:, :, C - 1]).then_inc(S["glastd"], 1)

            def decays(n):
                wait("kdecd", n * 2)
                for i in range(2):
                    wait("gsub", n * 2 + i + 1)
                    act.activation(dec[i][:, :, :], gtmp[i][:, :, :], ACT.Exp).then_inc(S["decd"], 1)

            def output_root(n):
                wait("ossd", n + 1)
                act.activation(ors[:, :], oss[:, :], ACT.Ln).then_inc(S["ors1"], 1)
                wait("ors1", n + 1)
                act.activation(ors[:, :], ors[:, :], ACT.Exp, scale=-0.5).then_inc(S["ors2"], 1)

            def output_square(n):
                wait("od", n * 2 + 2)
                act.activation(osq[:, :], osb[:, :, :].rearrange("p h d -> p (h d)"), ACT.Square).then_inc(S["osq"], 1)

            def output_copy(n):
                wait("yT", n + 1)
                act.copy(o.mixT[:, 4:8, bass.ds(n * C, C)], m4(bank[5][:, :])).then_inc(S["mixd"], 1)

            def chunk(n, first=False):
                if not first:
                    output_square(n - 1)
                for j, (dst, done) in enumerate(((qT, "qTd"), (kT, "kTd"), (kbT, "kbTd"))):
                    wait("tT", n * 3 + j + 1)
                    act.copy(dst[:, :, :].rearrange("p m c -> p (m c)"), bank[j][:, :]).then_inc(S[done], 1)
                if not first:
                    output_root(n - 1)
                    wait("std", n)
                act.activation(eg[:, :], gcol[:, :], ACT.Exp).then_inc(S["egd"], 1)
                wait("glastd", n * 2 + 2)
                for i in range(2):
                    half = slice(64 * i, 64 * i + 64)
                    act.activation(egl[half, :], glast[half, :], ACT.Exp).then_inc(S["egld"], 1)
                if not first:
                    output_copy(n - 1)
                for s_ in range(1, LEVELS):
                    for i in range(2):
                        wait("pm", n * (2 * LEVELS) + 2 * s_ + i + 1)
                        act.copy(Pm[i][:, :, :].rearrange("p m c -> p (m c)"), bank[i][:, :]).then_inc(S["pd"], 1)
                    if s_ == 2:
                        squares(n + 1)
                    elif s_ == 3:
                        roots(n + 1)
                    elif s_ == 6:
                        last_decays(n + 1)
                wait("wTm", n + 1)
                act.mul(wT[:, :, :].rearrange("p m c -> p (m c)"), bank[0][:, :], -1.0).then_inc(S["wTd"], 1)
                wait("vnm", n + 1)
                act.copy(vn[:, 0::2, :], w4(bank[1][:, 0:W // 2])).then_inc(S["vn0"], 1)
                act.copy(vn[:, 1::2, :], w4(bank[2][:, 0:W // 2])).then_inc(S["vnd"], 1)
                decays(n + 1)

            squares(0)
            roots(0)
            last_decays(0)
            decays(0)
            chunk(0, first=True)
            with act.Fori(1, NT) as n:
                chunk(n)
            output_square(NT - 1)
            output_root(NT - 1)
            output_copy(NT - 1)

        @block.vector
        def _(dve):
            wait = lambda name, v: dve.wait_ge(S[name], v)
            wait("vec_in", 48)
            ch = Chain(dve, S["pre_c"])
            a, b = o.ab[:, :, 0:H], o.ab[:, :, H:2 * H]
            ch.do(dve.tensor_tensor(sp1[:, :, :], a, bc(dtb[:, :].unsqueeze(1), [P, NT, H]), ALU.add))
            ch.do(dve.tensor_scalar(sp2[:, :, :], sp1[:, :, :], -1.0, None, ALU.mult))
            ch.do(dve.tensor_tensor(sp2[:, :, :], sp2[:, :, :], sp1[:, :, :], ALU.min))
            ch.do(dve.tensor_scalar(sp1[:, :, :], sp1[:, :, :], 0.0, None, ALU.max))
            dve.tensor_scalar(beta[:, :, :], b, -1.0, 80.0, ALU.mult, ALU.min).then_inc(S["pre_b"], 1)
            wait("pre_a", 4)
            ch.do(dve.tensor_scalar(la[:, :, :], sp2[:, :, :], 1.0, None, ALU.add))
            ch.do(dve.tensor_scalar(la[:, :, :], la[:, :, :], -1.0, 1e-30, ALU.add, ALU.max))
            ch.do(dve.reciprocal(la[:, :, :], la[:, :, :]))
            ch.do(dve.tensor_tensor(la[:, :, :], la[:, :, :], sp2[:, :, :], ALU.mult))
            ch.do(dve.tensor_tensor(la[:, :, :], la[:, :, :], sp3[:, :, :], ALU.mult))
            ch.do(dve.tensor_tensor(la[:, :, :], la[:, :, :], sp1[:, :, :], ALU.add))
            ch.do(dve.scalar_tensor_tensor(out=la[:, :, :], in0=la[:, :, :], scalar=-1.0,
                                           in1=bc(alog[:, :].unsqueeze(1), [P, NT, H]), op0=ALU.mult, op1=ALU.mult))
            ch.do(dve.tensor_scalar(beta[:, :, :], beta[:, :, :], 1.0, None, ALU.add))
            dve.reciprocal(beta[:, :, :], beta[:, :, :]).then_inc(S["pre_d"], 1)
            wait("pre_d", 1)

            def norms(n):
                wait("sqd", n * 2 + 2)
                dve.tensor_reduce(ssq[:, :], w4(sq[:, :]), AX.X, ALU.add).then_inc(S["tmp1"], 1)
                wait("tmp1", n * 2 + 1)
                dve.tensor_scalar(ssq[:, :], ssq[:, :], RMS_EPS, None, ALU.add).then_inc(S["ssqd"], 1)

            def normed(n):
                wait("rnd", n + 1)
                dve.tensor_scalar(rn[:, 0:H], rn[:, 0:H], GD ** -0.5, None, ALU.mult).then_inc(S["tmp1"], 1)
                wait("tmp1", n * 2 + 2)
                wait("tT", n * 3)
                wait("kdecd", n * 2)
                dve.tensor_tensor(qn[:, :, :], w4(bank[6][:, :]), col(rn[:, 0:H], H, GD), ALU.mult).then_inc(S["qnd"], 1)
                dve.tensor_tensor(kn[:, :, :], w4(bank[7][:, :]), col(rn[:, H:2 * H], H, GD), ALU.mult)\
                    .then_inc(S["knd"], 1)

            def by_beta(n):
                bcol = bc(beta_all[:, bass.ds(n, 1), :].rearrange("p a h -> p (a h)").unsqueeze(2), [P, H, GD])
                wait("rawT", n * 3 + 3)
                wait("vbc", n)
                dve.tensor_tensor(vb_next[:, :, :], w4(bank[6][:, :]), bcol, ALU.mult).then_inc(S["vbd"], 1)
                wait("knd", n + 1)
                wait("kbgd", n)
                dve.tensor_tensor(kb[:, :, :], kn[:, :, :], bcol, ALU.mult).then_inc(S["kbd"], 1)

            def g_column(n, i):
                wait("gb", n * 2 + i + 1)
                wait("decd", n * 2)
                dve.tensor_tensor(gtmp[i][:, :, :], m4(bank[7 - i][:, :]), bc(g.ident[:, :].unsqueeze(1), [P, 4, C]),
                                  ALU.mult).then_inc(S["gdiag"], 1)
                wait("gdiag", n * 2 + i + 1)
                wait("egd", n)
                dve.tensor_reduce(gcol[:, i::2], gtmp[i][:, :, :], AX.X, ALU.add).then_inc(S["gcold"], 1)

            def differences(n):
                for i in range(2):
                    wait("gcold", n * 2 + 2)
                    wait("glastd", n * 2 + 2)
                    dve.tensor_tensor(gtmp[i][:, :, :], m4(bank[7 - i][:, :]), col(gcol[:, i::2], 4, C),
                                      ALU.subtract).then_inc(S["gsub"], 1)

            def output_norm(n):
                wait("ors2", n + 1)
                wait("gained", NT)
                dve.tensor_tensor(osb[:, :, :], osb[:, :, :], col(ors[:, :], H, GD), ALU.mult).then_inc(S["yd"], 1)
                wait("yd", n * 2 + 1)
                gate = w4(o.gate[:, bass.ds(n, 1), :].rearrange("p a w -> p (a w)"))
                dve.tensor_tensor(osb[:, :, :], osb[:, :, :], gate, ALU.mult).then_inc(S["yd"], 1)

            def output_sum(n):
                wait("osq", n + 1)
                dve.tensor_reduce(oss[:, :], w4(osq[:, :]), AX.X, ALU.add).then_inc(S["tmp2"], 1)
                wait("tmp2", n + 1)
                dve.tensor_scalar(oss[:, :], oss[:, :], 1.0 / GD, RMS_EPS, ALU.mult, ALU.add).then_inc(S["ossd"], 1)

            def chunk(n, first=False):
                if not first:
                    output_sum(n - 1)
                for i in range(2):
                    wait("ltm", n * 2 + i + 1)
                    dve.tensor_tensor(LT[i][:, :, :], m4(bank[3 + i][:, :]), dec[i][:, :, :], ALU.mult)\
                        .then_inc(S["ltd"], 1)
                if not first:
                    output_norm(n - 1)
                for i in range(2):
                    wait("atm", n * 2 + i + 1)
                    dve.tensor_tensor(AT[i][:, :, :], m4(bank[6 + i][:, :]), dec[i][:, :, :], ALU.mult)\
                        .then_inc(S["atd"], 1)
                idb = bc(g.ident[:, :].unsqueeze(1), [P, 4, C])
                for i in range(2):
                    wait("lmd", n * (2 * LEVELS) + i + 1)
                    wait("pm", n * (2 * LEVELS) + i + 1)
                    dve.tensor_tensor(Sm[i][:, :, :], idb, LM[i][0][:, :, :], ALU.subtract).then_inc(S["smd"], 1)
                    dve.tensor_tensor(Tm[i][:, :, :], idb, m4(bank[i][:, :]), ALU.subtract).then_inc(S["tmd"], 1)
                for s_ in range(1, LEVELS):
                    for i in range(2):
                        wait("wm", n * (2 * LEVELS - 2) + 2 * (s_ - 1) + i + 1)
                        dve.tensor_tensor(Sm[i][:, :, :], Sm[i][:, :, :], m4(bank[4 + i][:, :]), ALU.subtract)\
                            .then_inc(S["smd"], 1)
                        if s_ < LEVELS - 1:
                            dve.tensor_tensor(Tm[i][:, :, :], Tm[i][:, :, :], m4(bank[2 + i][:, :]), ALU.subtract)\
                                .then_inc(S["tmd"], 1)
                    if s_ == 2:
                        norms(n + 1)
                    elif s_ == 3:
                        normed(n + 1)
                    elif s_ == 4:
                        by_beta(n + 1)
                        g_column(n + 1, 0)
                    elif s_ == 5:
                        g_column(n + 1, 1)
                    elif s_ == 6:
                        differences(n + 1)
                wait("om", n + 1)
                for i in range(2):
                    dve.tensor_tensor(osb[:, i::2, :], w4(bank[3 + 3 * i][:, 0:W // 2]), col(eg[:, i::2], H // 2, GD),
                                      ALU.mult).then_inc(S["oq"], 1)
                for i in range(2):
                    wait("oq", n * 2 + i + 1)
                    dve.tensor_tensor(osb[:, i::2, :], osb[:, i::2, :], w4(bank[4 + 3 * i][:, 0:W // 2]), ALU.add)\
                        .then_inc(S["od"], 1)
                wait("kvm", n + 1)
                wait("ones_state", n + 1)
                dve.tensor_tensor(state[:, :, :], state[:, :, :], w4(bank[5][:, 0:H // 2 * GD]), ALU.add)\
                    .then_inc(S["std"], 1)

            wait("pads", PADS)
            norms(0)
            normed(0)
            by_beta(0)
            for i in range(2):
                g_column(0, i)
            differences(0)
            chunk(0, first=True)
            with dve.Fori(1, NT) as n:
                chunk(n)
            output_sum(NT - 1)
            output_norm(NT - 1)


class Hybrid:

    def __init__(self, g, ctx):
        self.mixT = g.sb(ctx, "mixT0", [P, KD, T])
        self.ab = g.sb(ctx, "gdn_ab", [P, NT, 2 * HEADS])
        self.gate = g.sb(ctx, "gdn_gate", [P, NT, HEADS * GD])

    def attention_inputs(self, g, ctx):
        self.latT = g.sb(ctx, "latT", [P, 3, T])
        self.krT = g.sb(ctx, "krT", [ROPE, T])
        self.v = g.sb(ctx, "mla_v", [P, NT, HEADS * VD])
        self.q = g.sb(ctx, "mla_q", [P, NT, HEADS, QD])


class ResidualNorm:

    NZ, NX = 5, 4

    def __init__(self, g, ctx, tag, x_dram, out_dram, layer, gate, gain, bias):
        self.g, self.x_dram, self.out_dram = g, x_dram, out_dram
        self.gain_row, self.bias_row = gain, bias
        self.gate = g.mod[:, layer, gate, :]
        sb = lambda name, shape: g.sb(ctx, f"{tag}_{name}", shape)
        self.gate_b = sb("gate_b", [P, D])
        self.gain_b = sb("gain_b", [P, D])
        self.bias_b = sb("bias_b", [P, D])
        self.diag = sb("diag", [P, KD, P])
        self.x = [sb(f"x{i}", [P, D]) for i in range(self.NX)]
        self.z = [sb(f"z{i}", [P, D]) for i in range(self.NZ)]
        self.stats = sb("stats", [P, NT, 2, 6])
        self.mv = sb("mv", [P, NT, 2])
        self.rstd = sb("rstd", [P, NT])
        self.nmr = sb("nmr", [P, NT])
        names = "rows diagd gated gatec zmul zsum stat moments rooted rstdd nmrd normed gained done stored".split()
        self.S = dict(zip(names, g.sems(ctx, tag, *names)))
        self.x_in = g.sems(ctx, tag, *[f"x_in{i}" for i in range(self.NX)])

    def load_rows(self, sp):
        sp.dma_start(self.gain_b[:, :], self.gain_row.partition_broadcast(P)).then_inc(self.S["rows"], 16)
        sp.dma_start(self.bias_b[:, :], self.bias_row.partition_broadcast(P)).then_inc(self.S["rows"], 16)

    def load_x(self, sp, t):
        if t >= self.NX:
            sp.wait_ge(self.S["zsum"], t - self.NX + 1)
        sp.dma_start(self.x[t % self.NX][:, :], self.x_dram[t * P:(t + 1) * P, :])\
            .then_inc(self.x_in[t % self.NX], 16)

    def store(self, sp, t):
        sp.wait_ge(self.S["done"], t + 1)
        sp.dma_start(self.out_dram[t * P:(t + 1) * P, :], self.z[t % self.NZ][:, :]).then_inc(self.S["stored"], 16)

    def traffic(self, sp):
        for t in range(NT + 3):
            if t < NT:
                self.load_x(sp, t)
            if t == 1:
                self.load_rows(sp)
            if t >= 3:
                self.store(sp, t - 3)
        sp.wait_ge(self.S["stored"], 16 * NT)

    def gate_diag(self, dve):
        for kk in range(KD):
            dve.tensor_scalar(self.diag[:, kk, :], self.g.ident[:, :], self.gate[:, kk:kk + 1], None, ALU.mult)\
                .then_inc(self.S["diagd"], 1)

    def gate_rows(self, pe, banks):
        pe.wait_ge(self.S["diagd"], KD)
        for half in range(2):
            mm = pe.matmul(banks[:, half * 512:(half + 1) * 512], self.g.ones[:, :],
                           self.diag[:, 4 * half:4 * half + 4, :], start=True, stop=True)
        mm.then_inc(self.S["gated"], 1)

    def gate_copy(self, act, banks):
        act.wait_ge(self.S["gated"], 1)
        act.copy(self.gate_b[:, :], banks[:, :]).then_inc(self.S["gatec"], 1)

    def vector(self, dve, ready, y):
        for t in range(NT + 2):
            if t < NT:
                dve.wait_ge(ready, t + 1)
                self.sum_and_moments(dve, t, y[t % len(y)][:, :])
            if 0 <= t - 1 < NT:
                self.inverse_root(dve, t - 1)
            if 0 <= t - 2 < NT:
                self.apply_gain(dve, t - 2)

    def sum_and_moments(self, dve, t, y):
        S, z = self.S, self.z[t % self.NZ]
        if t == 0:
            dve.wait_ge(S["gatec"], 1)
        if t >= self.NZ:
            dve.wait_ge(S["stored"], 16 * (t - self.NZ + 1))
        dve.tensor_tensor(z[:, :], y, self.gate_b[:, :], ALU.mult).then_inc(S["zmul"], 1)
        dve.wait_ge(S["zmul"], t + 1)
        dve.wait_ge(self.x_in[t % self.NX], 16 * (t // self.NX + 1))
        dve.scalar_tensor_tensor(out=z[:, :], in0=self.x[t % self.NX][:, :], scalar=ALPHA, in1=z[:, :], op0=ALU.mult,
                                 op1=ALU.add).then_inc(S["zsum"], 1)
        dve.wait_ge(S["zsum"], t + 1)
        for half in range(2):
            dve.bn_stats(self.stats[:, t, half, :], z[:, half * 512:(half + 1) * 512]).then_inc(S["stat"], 1)
        dve.wait_ge(S["stat"], 2 * t + 2)
        dve.bn_aggr(self.mv[:, t, :], self.stats[:, t, :, :].rearrange("p a b -> p (a b)")).then_inc(S["moments"], 1)
        dve.wait_ge(S["moments"], 2 * t + 1)
        dve.tensor_scalar(self.rstd[:, t:t + 1], self.mv[:, t, 1:2], LN_EPS, None, ALU.add).then_inc(S["moments"], 1)

    def inverse_root(self, dve, t):
        S, r = self.S, self.rstd[:, t:t + 1]
        dve.wait_ge(S["rooted"], t + 1)
        dve.reciprocal(r, r).then_inc(S["rstdd"], 1)
        dve.wait_ge(S["rstdd"], t + 1)
        dve.scalar_tensor_tensor(out=self.nmr[:, t:t + 1], in0=self.mv[:, t, 0:1], scalar=-1.0, in1=r,
                                 op0=ALU.mult, op1=ALU.mult).then_inc(S["nmrd"], 1)

    def apply_gain(self, dve, t):
        S, z = self.S, self.z[t % self.NZ]
        if t == 0:
            dve.wait_ge(S["rows"], 32)
        dve.wait_ge(S["normed"], t + 1)
        dve.tensor_tensor(z[:, :], z[:, :], self.gain_b[:, :], ALU.mult).then_inc(S["gained"], 1)

    def scalar(self, act):
        S = self.S
        for t in range(NT + 1):
            if t < NT:
                act.wait_ge(S["moments"], 2 * t + 2)
                act.activation(self.rstd[:, t:t + 1], self.rstd[:, t:t + 1], ACT.Sqrt).then_inc(S["rooted"], 1)
            if t >= 1:
                p, z = t - 1, self.z[(t - 1) % self.NZ]
                act.wait_ge(S["nmrd"], p + 1)
                act.activation(z[:, :], z[:, :], ACT.Identity, bias=self.nmr[:, p:p + 1],
                               scale=self.rstd[:, p:p + 1]).then_inc(S["normed"], 1)

    def pool(self, pool, t):
        S, z = self.S, self.z[t % self.NZ]
        if t == 0:
            pool.wait_ge(S["rows"], 32)
        pool.wait_ge(S["gained"], t + 1)
        pool.tensor_tensor(z[:, :], z[:, :], self.bias_b[:, :], ALU.add).then_inc(S["done"], 1)


def mix_out(g, tag, mixT, nk, w, x_dram, out_dram, layer):
    nc, io = g.nc, g.io
    with ExitStack() as ctx:
        rn = ResidualNorm(g, ctx, tag, x_dram, out_dram, layer, 2, io["ln_mix_g"][layer], io["ln_mix_b"][layer])
        ws = g.sb(ctx, f"{tag}_w", [P, nk, D])
        py = [g.ps(ctx, f"{tag}_py{i}", [P, D]) for i in range(3)]
        proj, = g.sems(ctx, tag, "proj")
        w_in = g.sems(ctx, tag, *[f"w_in{i}" for i in range(nk // 4)])
        block = ctx.enter_context(nc.Block())
        wr = w.rearrange("(k p) n -> p k n", p=P)

        @block.sync
        def _(sp):
            for c in range(nk // 4):
                sp.dma_start(ws[:, 4 * c:4 * c + 4, :], wr[:, 4 * c:4 * c + 4, :]).then_inc(w_in[c], 16)
            rn.traffic(sp)

        @block.tensor
        def _(pe):
            rn.gate_rows(pe, py[2])
            for t in range(NT):
                if t == 2:
                    pe.wait_ge(rn.S["gatec"], 1)
                if t >= 3:
                    pe.wait_ge(rn.S["zmul"], t - 2)
                for kk in range(nk):
                    for half in range(2):
                        if t == 0 and half == 0 and kk % 4 == 0:
                            pe.wait_ge(w_in[kk // 4], 16)
                        mm = pe.matmul(py[t % 3][:, half * 512:(half + 1) * 512], mixT[:, kk, t * P:(t + 1) * P],
                                       ws[:, kk, half * 512:(half + 1) * 512], start=(kk == 0), stop=(kk == nk - 1))
                mm.then_inc(proj, 1)

        @block.vector
        def _(dve):
            rn.gate_diag(dve)
            rn.vector(dve, proj, py)

        @block.scalar
        def _(act):
            rn.gate_copy(act, py[2])
            rn.scalar(act)

        @block.gpsimd
        def _(pool):
            for t in range(NT):
                rn.pool(pool, t)


def retention(g, mixT):
    nc, io = g.nc, g.io
    STEPS = 2 * NT
    HK = RDK // 2
    QK = 2 * RDK
    W = QK + 2 * RDV
    lg = [math.log(1.0 - 2.0 ** (-5.0 - h)) for h in range(HEADS)]
    with ExitStack() as ctx:
        sb = lambda name, shape, dt=F32: g.sb(ctx, f"ret_{name}", shape, dt)
        w = [sb(f"w{u}", [P, KD, W]) for u in range(2)]
        gain = sb("gain", [P, HEADS, RDV])
        bias = sb("bias", [P, HEADS, RDV])
        place_i = sb("place_i", [P, 1], I32)
        place = sb("place", [P, 1])
        rate = sb("rate", [P, 2, HEADS])
        decay = sb("decay", [P, 2, HEADS])
        chunk_decay = sb("chunk_decay", [P, HEADS])
        qk = [sb(f"qk{i}", [P, 2, RDK]) for i in range(2)]
        tmp = [sb(f"tmp{i}", [P, 2, HK]) for i in range(2)]
        qkr = [sb(f"qkr{i}", [P, 2, RDK]) for i in range(4)]
        v = [sb(f"v{i}", [P, RDV]) for i in range(4)]
        gate = [sb(f"gate{i}", [P, RDV]) for i in range(4)]
        qkT = [sb(f"qkT{i}", [P, 2, P]) for i in range(2)]
        scores = [sb(f"scores{i}", [P, P]) for i in range(2)]
        state = [sb(f"state{i}", [P, RDV]) for i in range(2)]
        z = [sb(f"z{i}", [P, RDV]) for i in range(4)]
        stats = [sb(f"stats{i}", [P, 6]) for i in range(2)]
        mv = [sb(f"mv{i}", [P, 2]) for i in range(2)]
        rstd = [sb(f"rstd{i}", [P, 1]) for i in range(2)]
        head_gain = [sb(f"head_gain{u}", [P, RDV]) for u in range(2)]
        head_bias = [sb(f"head_bias{u}", [P, RDV]) for u in range(2)]
        p_qkv = [g.ps(ctx, f"ret_pqkv{i}", [P, 512]) for i in range(2)]
        p_gate = [g.ps(ctx, f"ret_pgate{i}", [P, 512]) for i in range(2)]
        p_turn = g.ps(ctx, "ret_pturn", [P, 512])
        p_scores = g.ps(ctx, "ret_pscores", [P, 512])
        p_out = g.ps(ctx, "ret_pout", [P, 512])
        p_back = g.ps(ctx, "ret_pback", [P, 512])
        names = ("rows placed rates exps qkv gates taken gated roped turned turnc scored masked out moments logs roots norms rowsc "
                 "gained back backc").split()
        S = dict(zip(names, g.sems(ctx, "ret", *names)))
        w_in = g.sems(ctx, "ret", "w_in0", "w_in1")
        block = ctx.enter_context(nc.Block())
        w_dram = io["ret_w_in"][0].rearrange("(k p) n -> p k n", p=P)
        parts = []
        at = off = 0
        for width in (RDK, RDK, RDV, RDV):
            cols = w_dram[:, :, at:at + HEADS * width].rearrange("p k (m u n) -> p k m u n", u=2, n=width)
            parts.append((off, width, cols))
            at += HEADS * width
            off += width
        pairs = HEADS // 2
        before = lambda m, s: m * STEPS + max(s, 0)
        after = lambda m, s: m * STEPS + s + 1

        @block.sync
        def _(sp):
            def panel(m, u):
                for off, width, cols in parts:
                    sp.dma_start(w[u][:, :, off:off + width], cols[:, :, bass.ds(m, 1), u, :]
                                 .rearrange("p k a n -> p k (a n)")).then_inc(w_in[u], 16)

            with sp.Fori(0, pairs) as m:
                for u in range(2):
                    sp.wait_ge(S["gates"], m * STEPS)
                    panel(m, u)

        @block.gpsimd
        def _(pool):
            pool.iota(place_i[:, :], [[1, 1]], base=1, channel_multiplier=1).then_inc(S["placed"], 1)
            for h in range(HEADS):
                pool.memset(rate[:, 0, h:h + 1], lg[h]).then_inc(S["placed"], 1)
                pool.memset(rate[:, 1, h:h + 1], -lg[h]).then_inc(S["placed"], 1)
                pool.memset(chunk_decay[:, h:h + 1], math.exp(RDK * lg[h])).then_inc(S["placed"], 1)
            pool.wait_ge(S["rows"], 32)
            gp = gain[:, :, :].rearrange("p (m u) n -> p m u n", u=2)
            bp = bias[:, :, :].rearrange("p (m u) n -> p m u n", u=2)
            with pool.Fori(0, pairs) as m:
                for u in range(2):
                    row = lambda t: t[:, bass.ds(m, 1), u, :].rearrange("p a n -> p (a n)")
                    pool.tensor_copy(head_gain[u][:, :], row(gp)).then_inc(S["rowsc"], 1)
                    pool.tensor_copy(head_bias[u][:, :], row(bp)).then_inc(S["rowsc"], 1)
                for s in range(STEPS):
                    u, zb = s // NT, z[s % 4][:, :]
                    pool.wait_ge(S["norms"], after(m, s))
                    pool.wait_ge(S["rowsc"], m * 4 + 4)
                    pool.tensor_tensor(zb, zb, head_gain[u][:, :], ALU.mult).then_inc(S["gained"], 1)
                    pool.wait_ge(S["gained"], m * 3 * STEPS + 3 * s + 1)
                    pool.tensor_tensor(zb, zb, head_bias[u][:, :], ALU.add).then_inc(S["gained"], 1)
                    pool.wait_ge(S["gained"], m * 3 * STEPS + 3 * s + 2)
                    pool.tensor_tensor(zb, zb, gate[s % 4][:, :], ALU.mult).then_inc(S["gained"], 1)

        @block.tensor
        def _(pe):
            with pe.Fori(0, pairs) as m:
                def project(s):
                    u, t = s // NT, s % NT
                    if t == 0:
                        pe.wait_ge(w_in[u], m * 64 + 64)
                    pe.wait_ge(S["taken"], before(m, s - 1))
                    for kk in range(KD):
                        mm = pe.matmul(p_qkv[s % 2][:, :], g.hT[:, kk, t * P:(t + 1) * P], w[u][:, kk, 0:512],
                                       start=(kk == 0), stop=(kk == KD - 1))
                    mm.then_inc(S["qkv"], 1)

                def project_gate(s):
                    u, t = s // NT, s % NT
                    pe.wait_ge(S["gated"], before(m, s - 1))
                    for kk in range(KD):
                        mm = pe.matmul(p_gate[s % 2][:, 0:RDV], g.hT[:, kk, t * P:(t + 1) * P], w[u][:, kk, 512:W],
                                       start=(kk == 0), stop=(kk == KD - 1))
                    mm.then_inc(S["gates"], 1)

                def turn(s):
                    pe.wait_ge(S["roped"], m * 6 * STEPS + 6 * s + 6)
                    pe.wait_ge(S["turnc"], before(m, s))
                    for i in range(2):
                        mm = pe.transpose(p_turn[:, i * P:(i + 1) * P], qkr[s % 4][:, i, :], g.ident[:, :])
                    mm.then_inc(S["turned"], 1)

                def score(s):
                    pe.wait_ge(S["turnc"], after(m, s))
                    pe.wait_ge(S["masked"], before(m, s))
                    pe.matmul(p_scores[:, 0:P], qkT[s % 2][:, 1, :], qkT[s % 2][:, 0, :], start=True, stop=True)\
                        .then_inc(S["scored"], 1)

                def output(s):
                    t = s % NT
                    pe.wait_ge(S["masked"], after(m, s))
                    pe.wait_ge(S["norms"], before(m, s))
                    pe.matmul(p_out[:, 0:RDV], scores[s % 2][:, :], v[s % 4][:, :], start=True, stop=(t == 0))
                    if t:
                        pe.matmul(p_out[:, 0:RDV], qkT[s % 2][:, 0, :], state[(s - 1) % 2][:, :], start=False, stop=True)
                    pe.matmul(p_out[:, RDV:2 * RDV], qkr[s % 4][:, 1, :], v[s % 4][:, :], start=True, stop=True)\
                        .then_inc(S["out"], 1)

                def turn_back(s):
                    pe.wait_ge(S["gained"], m * 3 * STEPS + 3 * s + 3)
                    pe.wait_ge(S["backc"], before(m, s))
                    for i in range(2):
                        mm = pe.transpose(p_back[:, i * P:(i + 1) * P], z[s % 4][:, i * P:(i + 1) * P], g.ident[:, :])
                    mm.then_inc(S["back"], 1)

                for s in range(STEPS + 3):
                    if s < STEPS:
                        project(s)
                    if 0 <= s - 2 < STEPS:
                        output(s - 2)
                    if 0 <= s - 1 < STEPS:
                        turn(s - 1)
                    if s < STEPS:
                        project_gate(s)
                    if 0 <= s - 1 < STEPS:
                        score(s - 1)
                    if 0 <= s - 3 < STEPS:
                        turn_back(s - 3)

        @block.scalar
        def _(act):
            act.dma_start(gain[:, :, :].rearrange("p h n -> p (h n)"), io["ret_gn_g"][0].partition_broadcast(P))\
                .then_inc(S["rows"], 16)
            act.dma_start(bias[:, :, :].rearrange("p h n -> p (h n)"), io["ret_gn_b"][0].partition_broadcast(P))\
                .then_inc(S["rows"], 16)
            act.wait_ge(S["rates"], 3)
            act.activation(decay[:, :, :], rate[:, :, :], ACT.Exp).then_inc(S["exps"], 1)
            act.wait_ge(S["exps"], 2)
            dp = decay[:, :, :].rearrange("p i (m u) -> p i m u", u=2)
            mp = mixT[:, :, :].rearrange("p (m k) t -> p m k t", k=4)
            with act.Fori(0, pairs) as m:
                def take(s):
                    u, b = s // NT, s % 4
                    act.wait_ge(S["qkv"], after(m, s))
                    act.wait_ge(S["roped"], m * 6 * STEPS + max(6 * (s - 1), 0))
                    act.wait_ge(S["out"], before(m, s - 3))
                    act.copy(v[b][:, :], p_qkv[s % 2][:, QK:512])
                    for i in range(2):
                        ins = act.activation(qk[s % 2][:, i, :], p_qkv[s % 2][:, i * RDK:(i + 1) * RDK], ACT.Copy,
                                             scale=dp[:, i, bass.ds(m, 1), u])
                    ins.then_inc(S["taken"], 1)

                def take_gate(s):
                    act.wait_ge(S["gates"], after(m, s))
                    act.wait_ge(S["gained"], m * 3 * STEPS + max(3 * (s - 3), 0))
                    act.activation(gate[s % 4][:, :], p_gate[s % 2][:, 0:RDV], ACT.Silu).then_inc(S["gated"], 1)

                def root(s):
                    act.wait_ge(S["moments"], m * 5 * STEPS + 5 * s + 5)
                    act.wait_ge(S["norms"], before(m, s - 1))
                    act.activation(rstd[s % 2][:, :], mv[s % 2][:, 1:2], ACT.Ln).then_inc(S["logs"], 1)
                    act.wait_ge(S["logs"], after(m, s))
                    act.activation(rstd[s % 2][:, :], rstd[s % 2][:, :], ACT.Exp, scale=-0.5).then_inc(S["roots"], 1)

                def take_turned(s):
                    act.wait_ge(S["turned"], after(m, s))
                    act.wait_ge(S["out"], before(m, s - 1))
                    act.copy(qkT[s % 2][:, :, :].rearrange("p a t -> p (a t)"), p_turn[:, 0:2 * P])\
                        .then_inc(S["turnc"], 1)

                def take_back(s):
                    u, t = s // NT, s % NT
                    act.wait_ge(S["back"], after(m, s))
                    act.copy(mp[:, bass.ds(m, 1), 2 * u:2 * u + 2, t * P:(t + 1) * P].rearrange("p a k t -> p (a k) t"),
                             p_back[:, 0:2 * P].rearrange("p (k t) -> p k t", k=2)).then_inc(S["backc"], 1)

                for s in range(STEPS + 3):
                    if s < STEPS:
                        take(s)
                    if 0 <= s - 2 < STEPS:
                        root(s - 2)
                    if 0 <= s - 1 < STEPS:
                        take_turned(s - 1)
                    if s < STEPS:
                        take_gate(s)
                    if 0 <= s - 3 < STEPS:
                        take_back(s - 3)

        @block.vector
        def _(dve):
            dve.wait_ge(S["placed"], 1 + 3 * HEADS)
            ch = Chain(dve, S["rates"])
            ch.do(dve.tensor_copy(place[:, :], place_i[:, :]))
            for i in range(2):
                ch.mark(dve.tensor_scalar(rate[:, i, :], rate[:, i, :], place[:, 0:1], None, ALU.mult))
            dve.wait_ge(S["exps"], 1)
            dve.tensor_scalar(decay[:, 0, :], decay[:, 0, :], RDK ** -0.5, None, ALU.mult).then_inc(S["exps"], 1)
            cd = chunk_decay[:, :].rearrange("p (m u) -> p m u", u=2)
            with dve.Fori(0, pairs) as m:
                def rope(s):
                    t, x, out = s % NT, qk[s % 2], qkr[s % 4]
                    dve.wait_ge(S["taken"], after(m, s))
                    dve.wait_ge(S["out"], before(m, s - 3))
                    ch = Chain(dve, S["roped"], m * 6 * STEPS + 6 * s)
                    cos = bc(g.cos[:, t, :].unsqueeze(1), [P, 2, HK])
                    sin = bc(g.sin[:, t, :].unsqueeze(1), [P, 2, HK])
                    x1, x2 = x[:, :, 0:HK], x[:, :, HK:RDK]
                    ta, tb = tmp[0][:, :, :], tmp[1][:, :, :]
                    ch.mark(dve.tensor_tensor(ta, x1, cos, ALU.mult))
                    ch.do(dve.tensor_tensor(tb, x2, sin, ALU.mult))
                    ch.do(dve.tensor_tensor(out[:, :, 0:HK], ta, tb, ALU.subtract))
                    ch.mark(dve.tensor_tensor(ta, x1, sin, ALU.mult))
                    ch.do(dve.tensor_tensor(tb, x2, cos, ALU.mult))
                    ch.do(dve.tensor_tensor(out[:, :, HK:RDK], ta, tb, ALU.add))

                def mask(s):
                    dve.wait_ge(S["scored"], after(m, s))
                    dve.wait_ge(S["out"], before(m, s - 1))
                    dve.tensor_tensor(scores[s % 2][:, :], p_scores[:, 0:P], g.upto[:, :], ALU.mult)\
                        .then_inc(S["masked"], 1)

                def finish(s):
                    u, t, st = s // NT, s % NT, state[s % 2]
                    dve.wait_ge(S["out"], after(m, s))
                    ch = Chain(dve, S["moments"], m * 5 * STEPS + 5 * s)
                    if t:
                        ch.mark(dve.tensor_tensor(st[:, :], state[(s - 1) % 2][:, :], p_out[:, RDV:2 * RDV], ALU.add))
                    else:
                        ch.mark(dve.tensor_copy(st[:, :], p_out[:, RDV:2 * RDV]))
                    ch.do(dve.bn_stats(stats[s % 2][:, :], p_out[:, 0:RDV]))
                    ch.mark(dve.tensor_scalar(st[:, :], st[:, :], cd[:, bass.ds(m, 1), u], None, ALU.mult))
                    ch.do(dve.bn_aggr(mv[s % 2][:, :], stats[s % 2][:, :]))
                    ch.mark(dve.tensor_scalar(mv[s % 2][:, 1:2], mv[s % 2][:, 1:2], LN_EPS, None, ALU.add))

                def centre(s):
                    dve.wait_ge(S["roots"], after(m, s))
                    dve.wait_ge(S["back"], before(m, s - 3))
                    dve.tensor_scalar(z[s % 4][:, :], p_out[:, 0:RDV], mv[s % 2][:, 0:1], rstd[s % 2][:, 0:1],
                                      ALU.subtract, ALU.mult).then_inc(S["norms"], 1)

                for s in range(STEPS + 2):
                    if 0 <= s - 2 < STEPS:
                        finish(s - 2)
                    if s < STEPS:
                        rope(s)
                    if 0 <= s - 2 < STEPS:
                        centre(s - 2)
                    if 0 <= s - 1 < STEPS:
                        mask(s - 1)


class Routing:

    def __init__(self, g, ctx, tag):
        self.weight = g.sb(ctx, f"{tag}_weight", [P, NT, 2])
        self.slot = g.sb(ctx, f"{tag}_slot", [P, NT, 2], I32)
        self.token = g.sb(ctx, f"{tag}_token", [P, NBLK + 2], I32)
        self.full = g.sb(ctx, f"{tag}_full", [1, NBLK], I32)
        self.expert = g.sb(ctx, f"{tag}_expert", [1, NBLK], I32)
        self.used = g.sb(ctx, f"{tag}_used", [1, 1], I32)


def route(g, tag, r, layer, y_dram=None):
    nc, io = g.nc, g.io
    spare = range(PAIRS // P, NBLK) if y_dram is not None else ()
    NR = NG + NE
    BIG = 99.0
    with ExitStack() as ctx:
        sb = lambda name, shape, dt=F32: g.sb(ctx, f"{tag}_{name}", shape, dt)
        w = sb("w", [P, KD, NR])
        bias = sb("bias", [P, NR])
        L = sb("L", [P, NT, NR])
        iota_i = sb("iota_i", [P, P], I32)
        tok_i = sb("tok_i", [P, NT], I32)
        iota = sb("iota", [P, P])
        tok = sb("tok", [P, NT])
        gm, gs, gi, m1, m2, i1, i2, ex, tw = (sb(n, [P, NT]) for n in "gm gs gi m1 m2 i1 i2 ex tw".split())
        t4, g1h = sb("t4", [P, NT, NG]), sb("g1h", [P, NT, NG])
        t32 = sb("t32", [P, NT, NG, EPG])
        es, t8 = sb("es", [P, NT, EPG]), sb("t8", [P, NT, EPG])
        O = [sb(f"O{i}", [P, NT, NE]) for i in range(2)]
        C = sb("C", [P, NT, NE])
        Cp = sb("Cp", [P, NT + 1, NE])
        cnt, nb, cum, zero = (sb(n, [P, NE]) for n in "cnt nb cum zero".split())
        rank = sb("rank", [P, NT, NE])
        st = sb("st", [P, NT, NE])
        slotf = sb("slotf", [P, NT, 2])
        lo_i, hi_i = sb("lo_i", [P, NT, 2], I32), sb("hi_i", [P, NT, 2], I32)
        lo, hi = sb("lo", [P, NT, 2]), sb("hi", [P, NT, 2])
        A = [sb(f"A{i}", [P, P]) for i in range(2)]
        B = [sb(f"B{i}", [P, NBLK]) for i in range(2)]
        be = sb("be", [1, NBLK, NE])
        bes = sb("bes", [1, NBLK])
        tokf = sb("tokf", [P, NBLK + 2])
        usf = sb("usf", [1, 2])
        pl = g.ps(ctx, f"{tag}_pl", [P, 512])
        pr = g.ps(ctx, f"{tag}_pr", [P, 512])
        pk = g.ps(ctx, f"{tag}_pk", [P, 512])
        blank = sb("blank", [P, D])
        names = "w_in b_in blanked cleared iotas logits steps grp gexp diff dexp onehot ranked hit placed".split()
        S = dict(zip(names, g.sems(ctx, tag, *names)))
        block = ctx.enter_context(nc.Block())

        @block.sync
        def _(sp):
            sp.dma_start(bias[:, 0:NG], io["moe_b_group"][layer].partition_broadcast(P)).then_inc(S["b_in"], 16)
            sp.dma_start(bias[:, NG:NR], io["moe_b_expert"][layer].partition_broadcast(P)).then_inc(S["b_in"], 16)
            with nc.allow_non_contiguous_dma(reason="the group logits' weights, 16 bytes a row"):
                sp.dma_start(w[:, :, 0:NG], io["moe_w_group"][layer].rearrange("(k p) n -> p k n", p=P))\
                    .then_inc(S["w_in"], 16)
                sp.dma_start(w[:, :, NG:NR], io["moe_w_expert"][layer].rearrange("(k p) n -> p k n", p=P))\
                    .then_inc(S["w_in"], 16)
            sp.wait_ge(S["blanked"], 1)
            for i in spare:
                sp.dma_start(y_dram[i * P:(i + 1) * P, :], blank[:, :]).then_inc(S["cleared"], 16)
            if len(spare):
                sp.wait_ge(S["cleared"], 16 * len(spare))

        @block.gpsimd
        def _(pool):
            pool.iota(iota_i[:, :], [[1, P]], base=0, channel_multiplier=0).then_inc(S["iotas"], 1)
            pool.iota(tok_i[:, :], [[P, NT]], base=1, channel_multiplier=1).then_inc(S["iotas"], 1)
            pool.memset(blank[:, :], 0.0).then_inc(S["blanked"], 1)

        @block.tensor
        def _(pe):
            pe.wait_ge(S["w_in"], 32)
            for t in range(NT):
                for kk in range(KD):
                    mm = pe.matmul(pl[:, t * NR:(t + 1) * NR], g.hT[:, kk, t * P:(t + 1) * P], w[:, kk, :],
                                   start=(kk == 0), stop=(kk == KD - 1))
            mm.then_inc(S["logits"], 1)
            pe.wait_ge(S["onehot"], 1)
            pe.matmul(pr[:, 0:NT * NE], g.before[:, :], C[:, :, :], start=True, stop=False)
            pe.matmul(pr[:, 0:NT * NE], g.ones[:, :], Cp[:, 0:NT, :], start=False, stop=True)
            pe.matmul(pr[:, NT * NE:(NT + 1) * NE], g.ones[:, :], Cp[:, NT, :], start=True, stop=True)\
                .then_inc(S["ranked"], 1)
            for n in range(2 * NT):
                pe.wait_ge(S["hit"], 2 * n + 2)
                pe.matmul(pk[:, 0:NBLK], A[n % 2][:, :], B[n % 2][:, :], start=(n == 0), stop=(n == 2 * NT - 1))\
                    .then_inc(S["placed"], 1)

        @block.scalar
        def _(act):
            act.wait_ge(S["grp"], 1)
            act.activation(t4[:, :, :], t4[:, :, :], ACT.Exp).then_inc(S["gexp"], 1)
            act.wait_ge(S["diff"], 1)
            act.activation(ex[:, :], ex[:, :], ACT.Exp).then_inc(S["dexp"], 1)

        @block.vector
        def _(dve):
            ch = Chain(dve, S["steps"])
            tt = lambda out, a, b, op: ch.do(dve.tensor_tensor(out, a, b, op))
            ts = lambda out, a, s1, s2, op0, op1=None: ch.do(
                dve.tensor_scalar(out, a, s1, s2, op0, op1) if op1 is not None else dve.tensor_scalar(out, a, s1, s2, op0))
            red = lambda out, a, op: ch.do(dve.tensor_reduce(out, a, AX.X, op))
            c3 = lambda ap, n: bc(ap.unsqueeze(2), [P, NT, n])

            def first_of(idx, v, top, n, t):
                tt(t, v, c3(top, n), ALU.is_lt)
                ch.do(dve.scalar_tensor_tensor(out=t, in0=t, scalar=BIG, in1=bc(iota[:, 0:n].unsqueeze(1), [P, NT, n]),
                                               op0=ALU.mult, op1=ALU.add))
                red(idx, t, ALU.min)

            dve.wait_ge(S["iotas"], 2)
            ch.do(dve.tensor_copy(iota[:, :], iota_i[:, :]))
            ch.do(dve.tensor_copy(tok[:, :], tok_i[:, :]))
            ch.do(dve.memset(zero[:, :], 0.0))
            ch.do(dve.memset(Cp[:, 0, :], 0.0))
            dve.wait_ge(S["b_in"], 32)
            dve.wait_ge(S["logits"], 1)
            tt(L[:, :, :], pl[:, 0:NT * NR].rearrange("p (t n) -> p t n", n=NR), bc(bias[:, :].unsqueeze(1), [P, NT, NR]),
               ALU.add)
            G = L[:, :, 0:NG]
            E = L[:, :, NG:NR].rearrange("p t (g e) -> p t g e", e=EPG)
            red(gm[:, :], G, ALU.max)
            first_of(gi[:, :], G, gm[:, :], NG, g1h[:, :, :])
            dve.tensor_tensor(t4[:, :, :], G, c3(gm[:, :], NG), ALU.subtract).then_inc(S["grp"], 1)
            tt(g1h[:, :, :], bc(iota[:, 0:NG].unsqueeze(1), [P, NT, NG]), c3(gi[:, :], NG), ALU.is_equal)
            for q in range(NG):
                tt(t32[:, :, q, :], E[:, :, q, :], bc(g1h[:, :, q:q + 1], [P, NT, EPG]), ALU.mult)
            red(es[:, :, :], t32[:, :, :, :].rearrange("p t g e -> p t e g"), ALU.add)
            red(m1[:, :], es[:, :, :], ALU.max)
            first_of(i1[:, :], es[:, :, :], m1[:, :], EPG, t8[:, :, :])
            tt(t8[:, :, :], bc(iota[:, 0:EPG].unsqueeze(1), [P, NT, EPG]), c3(i1[:, :], EPG), ALU.is_equal)
            ch.do(dve.scalar_tensor_tensor(out=es[:, :, :], in0=t8[:, :, :], scalar=NEG, in1=es[:, :, :],
                                           op0=ALU.mult, op1=ALU.add))
            red(m2[:, :], es[:, :, :], ALU.max)
            first_of(i2[:, :], es[:, :, :], m2[:, :], EPG, t8[:, :, :])
            dve.tensor_tensor(ex[:, :], m2[:, :], m1[:, :], ALU.subtract).then_inc(S["diff"], 1)
            dve.wait_ge(S["gexp"], 1)
            red(gs[:, :], t4[:, :, :], ALU.add)
            ch.do(dve.reciprocal(gs[:, :], gs[:, :]))
            dve.wait_ge(S["dexp"], 1)
            ts(tw[:, :], ex[:, :], 1.0, None, ALU.add)
            ch.do(dve.reciprocal(tw[:, :], tw[:, :]))
            tt(r.weight[:, :, 0], gs[:, :], tw[:, :], ALU.mult)
            tt(r.weight[:, :, 1], r.weight[:, :, 0], ex[:, :], ALU.mult)
            for k, idx in enumerate((i1, i2)):
                ch.do(dve.scalar_tensor_tensor(out=idx[:, :], in0=gi[:, :], scalar=float(EPG), in1=idx[:, :],
                                               op0=ALU.mult, op1=ALU.add))
                tt(O[k][:, :, :], bc(iota[:, 0:NE].unsqueeze(1), [P, NT, NE]), c3(idx[:, :], NE), ALU.is_equal)
            tt(C[:, :, :], O[0][:, :, :], O[1][:, :, :], ALU.add)
            for t in range(NT):
                tt(Cp[:, t + 1, :], Cp[:, t, :], C[:, t, :], ALU.add)
            dve.sem_inc(S["onehot"], 1)
            dve.wait_ge(S["ranked"], 1)
            ch.do(dve.tensor_copy(rank[:, :, :].rearrange("p t e -> p (t e)"), pr[:, 0:NT * NE]))
            ch.do(dve.tensor_copy(cnt[:, :], pr[:, NT * NE:(NT + 1) * NE]))
            ts(nb[:, :], cnt[:, :], 0.5, None, ALU.is_gt)
            for m in range(1, T // P):
                ch.do(dve.scalar_tensor_tensor(out=nb[:, :], in0=cnt[:, :], scalar=m * P + 0.5, in1=nb[:, :],
                                               op0=ALU.is_gt, op1=ALU.add))
            ch.do(dve.tensor_tensor_scan(cum[:, :], nb[:, :], zero[:, :], 0.0, ALU.add, ALU.add))
            tt(cnt[:, :], cum[:, :], nb[:, :], ALU.subtract)
            ts(cnt[:, :], cnt[:, :], float(P), None, ALU.mult)
            tt(rank[:, :, :], rank[:, :, :], bc(cnt[:, :].unsqueeze(1), [P, NT, NE]), ALU.add)
            for k in range(2):
                tt(st[:, :, :], rank[:, :, :], O[k][:, :, :], ALU.mult)
                red(slotf[:, :, k], st[:, :, :], ALU.add)
            ch.do(dve.tensor_copy(r.slot[:, :, :], slotf[:, :, :]))
            ts(lo_i[:, :, :], r.slot[:, :, :], P - 1, None, ALU.bitwise_and)
            ts(hi_i[:, :, :], r.slot[:, :, :], 7, None, ALU.arith_shift_right)
            ch.do(dve.tensor_copy(lo[:, :, :], lo_i[:, :, :]))
            ch.do(dve.tensor_copy(hi[:, :, :], hi_i[:, :, :]))
            for n in range(2 * NT):
                t, k = n // 2, n % 2
                if n >= 2:
                    dve.wait_ge(S["placed"], n - 1)
                dve.tensor_scalar(A[n % 2][:, :], iota[:, :], lo[:, t, k:k + 1], tok[:, t:t + 1], ALU.is_equal,
                                  ALU.mult).then_inc(S["hit"], 1)
                dve.tensor_scalar(B[n % 2][:, :], iota[:, 0:NBLK], hi[:, t, k:k + 1], None, ALU.is_equal)\
                    .then_inc(S["hit"], 1)
            tt(be[:, :, :], bc(iota[0:1, 0:NBLK].unsqueeze(2), [1, NBLK, NE]), bc(cum[0:1, :].unsqueeze(1), [1, NBLK, NE]),
               ALU.is_ge)
            red(bes[:, :], be[:, :, :], ALU.add)
            ts(bes[:, :], bes[:, :], float(NE - 1), None, ALU.min)
            ch.do(dve.tensor_copy(r.expert[:, :], bes[:, :]))
            ts(usf[:, 0:1], cum[0:1, NE - 1:NE], 0.5, 0.25, ALU.mult, ALU.add)
            ch.do(dve.tensor_copy(r.used[:, :], usf[:, 0:1]))
            dve.wait_ge(S["placed"], 2 * NT)
            ts(r.full[:, :], pk[64:65, 0:NBLK], 0.5, None, ALU.is_gt)
            ch.do(dve.memset(tokf[:, :], 0.0))
            ts(tokf[:, 0:NBLK], pk[:, 0:NBLK], -1.0, 0.0, ALU.add, ALU.max)
            ch.do(dve.tensor_copy(r.token[:, :], tokf[:, :]))


def experts(g, tag, r, x_dram, y_dram, layer):
    nc, io = g.nc, g.io
    KF = FF // P
    HALF = P // 2
    FH, DH = FF // 2, D // 2
    PAIRS_OF_BLOCKS = NBLK // 2
    shift, scale = g.mod[:, layer, 3, :], g.mod[:, layer, 4, :]
    with ExitStack() as ctx:
        sb = lambda name, shape, dt=F32: g.sb(ctx, f"{tag}_{name}", shape, dt)
        wgu = [sb(f"wgu{u}", [P, KD, 2, FF]) for u in range(2)]
        wd = [sb(f"wd{u}", [P, KF, D]) for u in range(2)]
        idx = [sb(f"idx{u}", [P, 1], I32) for u in range(2)]
        xg = [sb(f"xg{u}", [P, D]) for u in range(2)]
        xT = [sb(f"xT{u}", [P, KD, P]) for u in range(2)]
        hs = [sb(f"hs{s}", [P, FH]) for s in range(2)]
        hid = [sb(f"hid{s}", [P, FH]) for s in range(2)]
        hidT = sb("hidT", [P, 2, KF // 2, 2, HALF])
        y = [sb(f"y{u}", [P, 2, DH]) for u in range(2)]
        px = [g.ps(ctx, f"{tag}_px{i}", [P, 512]) for i in range(2)]
        pgu = [g.ps(ctx, f"{tag}_pgu{s}", [P, 512]) for s in range(2)]
        ph = g.ps(ctx, f"{tag}_ph", [P, 512])
        pd = [g.ps(ctx, f"{tag}_pd{s}", [P, 512]) for s in range(2)]
        names = "xt_a xa xd silu_a silu_b hid_a hid_b ht hTd ya yb asked left".split()
        S = dict(zip(names, g.sems(ctx, tag, *names)))
        pairs = {n: g.sems(ctx, tag, n + "0", n + "1") for n in "idxd x_in gu_in d_in stored xt_b gu_a gu_b down_a down_b".split()}
        block = ctx.enter_context(nc.Block())
        gate_w = io["moe_w_gate"][layer].rearrange("e (k p) f -> e p k f", p=P)
        up_w = io["moe_w_up"][layer].rearrange("e (k p) f -> e p k f", p=P)
        down_w = io["moe_w_down"][layer].rearrange("e (k p) n -> e p k n", p=P)
        one = lambda ap: ap.rearrange("a p k n -> (a p) k n")

        def pairs_used(eng):
            return eng.value_load(r.used[0:1, 0:1], min_val=1, max_val=PAIRS_OF_BLOCKS)

        def following(m, u):
            return (m, 1) if u == 0 else (m + 1, 0)

        @block.sync
        def _(sp):
            ex = r.expert[:, :].rearrange("a (m u) -> a m u", u=2)
            with sp.Fori(0, pairs_used(sp)) as m:
                e = [sp.value_load(ex[0:1, bass.ds(m, 1), u], min_val=0, max_val=NE - 1) for u in range(2)]
                for u in range(2):
                    sp.wait_ge(pairs["gu_a"][u], m)
                    sp.wait_ge(pairs["gu_b"][u], m)
                    sp.dma_start(wgu[u][:, :, 0, :], one(gate_w[bass.ds(e[u], 1)])).then_inc(pairs["gu_in"][u], 16)
                    sp.dma_start(wgu[u][:, :, 1, :], one(up_w[bass.ds(e[u], 1)])).then_inc(pairs["gu_in"][u], 16)
                    sp.wait_ge(pairs["down_a"][u], m)
                    sp.wait_ge(pairs["down_b"][u], m)
                    sp.dma_start(wd[u][:, :, :], one(down_w[bass.ds(e[u], 1)])).then_inc(pairs["d_in"][u], 16)

        @block.gpsimd
        def _(pool):
            tk = r.token[:, :].rearrange("p (m u) -> p m u", u=2)

            def gather(m, u, col):
                pool.tensor_copy(idx[u][:, :], col).then_inc(pairs["idxd"][u], 1)
                pool.wait_ge(pairs["idxd"][u], m + 1)
                pool.sem_inc(S["asked"], 1)
                pool.indirect_dma_start(out=xg[u][:, :], out_offset=None, in_=x_dram,
                                        in_offset=bass.IndirectOffsetOnAxis(ap=idx[u][:, :], axis=0))\
                    .then_inc(pairs["x_in"][u], 16)

            gather(0, 0, tk[:, 0:1, 0])
            with pool.Fori(0, pairs_used(pool)) as m:
                for u in range(2):
                    mn, un = following(m, u)
                    pool.wait_ge(pairs["x_in"][un], mn * 16)
                    pool.wait_ge(pairs["xt_b"][un], mn)
                    gather(mn, un, tk[:, bass.ds(mn, 1), un])

        @block.tensor
        def _(pe):
            full = r.full[:, :].rearrange("a (m u) -> a m u", u=2)

            def turn(m, u, first=False):
                pe.wait_ge(pairs["x_in"][u], m * 16 + 16)
                for half in range(2):
                    if not first:
                        pe.wait_ge(S["xd" if half else "xa"], m * 2 + u)
                    for j in range(4):
                        kk = 4 * half + j
                        mm = pe.transpose(px[half][:, j * P:(j + 1) * P], xg[u][:, kk * P:(kk + 1) * P], g.ident[:, :])
                    mm.then_inc(pairs["xt_b"][u] if half else S["xt_a"], 1)

            def gate_up(u, s):
                for kk in range(KD):
                    for half in range(2):
                        mm = pe.matmul(pgu[s][half * HALF:(half + 1) * HALF, :], xT[u][:, kk, s * HALF:(s + 1) * HALF],
                                       wgu[u][:, kk, :, half * FH:(half + 1) * FH], start=(kk == 0),
                                       stop=(kk == KD - 1), skip_group_check=True)
                return mm

            def down(u, s):
                for k in range(KF):
                    for half in range(2):
                        mm = pe.matmul(pd[s][half * HALF:(half + 1) * HALF, :], hidT[:, s, k % 2, k // 2, :],
                                       wd[u][:, k, half * DH:(half + 1) * DH], start=(k == 0), stop=(k == KF - 1),
                                       skip_group_check=True)
                return mm

            for bank in (pgu[1], pd[1]):
                pe.matmul(bank[:, :], g.ident[:, :], g.cos[:, 0:8, :].rearrange("p t n -> p (t n)"), start=True, stop=True)
            turn(0, 0, first=True)
            with pe.Fori(0, pairs_used(pe)) as m:
                second = [pe.value_load(full[0:1, bass.ds(m, 1), u], min_val=0, max_val=1) for u in range(2)]
                for u in range(2):
                    n = m * 2 + u
                    pe.wait_ge(pairs["gu_in"][u], m * 32 + 32)
                    pe.wait_ge(S["xa"], n + 1)
                    pe.wait_ge(S["xd"], n + 1)
                    pe.wait_ge(S["hid_a"], n)
                    pe.wait_ge(S["hid_b"], n)
                    gate_up(u, 0).then_inc(pairs["gu_a"][u], 1)
                    with pe.If(second[u] > 0):
                        gate_up(u, 1).then_inc(pairs["gu_b"][u], 1)
                    with pe.Else():
                        pe.sem_inc(pairs["gu_b"][u], 1)
                    turn(*following(m, u))
                    pe.wait_ge(S["hid_a"], n + 1)
                    pe.wait_ge(S["hid_b"], n + 1)
                    pe.wait_ge(S["hTd"], n)
                    for s in range(2):
                        for j in range(2):
                            mm = pe.transpose(ph[:, (2 * s + j) * P:(2 * s + j + 1) * P], hid[s][:, j * P:(j + 1) * P],
                                              g.ident[:, :])
                    mm.then_inc(S["ht"], 1)
                    pe.wait_ge(pairs["d_in"][u], m * 16 + 16)
                    pe.wait_ge(S["hTd"], n + 1)
                    pe.wait_ge(S["ya"], n)
                    pe.wait_ge(S["yb"], n)
                    down(u, 0).then_inc(pairs["down_a"][u], 1)
                    with pe.If(second[u] > 0):
                        down(u, 1).then_inc(pairs["down_b"][u], 1)
                    with pe.Else():
                        pe.sem_inc(pairs["down_b"][u], 1)

        @block.scalar
        def _(act):
            yd = y_dram.rearrange("(m u s t) (c n) -> m u c t s n", u=2, s=2, t=HALF, c=2)

            def take(m, u, first=False):
                act.wait_ge(S["xt_a"], m * 2 + u + 1)
                if not first:
                    act.wait_ge(pairs["gu_b"][u], m)
                for j in range(4):
                    ins = act.activation(xT[u][:, j, :], px[0][:, j * P:(j + 1) * P], ACT.Identity,
                                         bias=shift[:, j:j + 1], scale=scale[:, j:j + 1])
                ins.then_inc(S["xa"], 1)

            take(0, 0, first=True)
            with act.Fori(0, pairs_used(act)) as m:
                for u in range(2):
                    n = m * 2 + u
                    act.wait_ge(pairs["gu_a"][u], m + 1)
                    act.wait_ge(S["hid_a"], n)
                    act.activation(hs[0][:, :], pgu[0][:, 0:FH], ACT.Silu).then_inc(S["silu_a"], 1)
                    act.wait_ge(pairs["gu_b"][u], m + 1)
                    act.wait_ge(S["hid_b"], n)
                    act.activation(hs[1][:, :], pgu[1][:, 0:FH], ACT.Silu).then_inc(S["silu_b"], 1)
                    take(*following(m, u))
                    act.wait_ge(pairs["down_a"][u], m + 1)
                    act.wait_ge(pairs["stored"][u], m * 32)
                    act.copy(y[u][:, 0, :], pd[0][:, :]).then_inc(S["ya"], 1)
                    act.wait_ge(S["ya"], n + 1)
                    act.wait_ge(S["yb"], n + 1)
                    for c in range(2):
                        act.dma_start(yd[bass.ds(m, 1), u, c].rearrange("a t s n -> (a t) s n"),
                                      y[u][c * HALF:(c + 1) * HALF, :, :]).then_inc(pairs["stored"][u], 16)
            n = pairs_used(act)
            for u in range(2):
                act.wait_ge(pairs["stored"][u], n * 32)
            act.sem_inc(S["left"], 1)

        @block.vector
        def _(dve):
            def take(m, u, first=False):
                dve.wait_ge(pairs["xt_b"][u], m + 1)
                if not first:
                    dve.wait_ge(pairs["gu_b"][u], m)
                for j in range(4):
                    ins = dve.tensor_scalar(xT[u][:, 4 + j, :], px[1][:, j * P:(j + 1) * P], scale[:, 4 + j:5 + j],
                                            shift[:, 4 + j:5 + j], ALU.mult, ALU.add)
                ins.then_inc(S["xd"], 1)

            take(0, 0, first=True)
            with dve.Fori(0, pairs_used(dve)) as m:
                for u in range(2):
                    n = m * 2 + u
                    for s, (silu, done) in enumerate((("silu_a", "hid_a"), ("silu_b", "hid_b"))):
                        dve.wait_ge(S[silu], n + 1)
                        dve.wait_ge(S["ht"], n)
                        dve.tensor_tensor(hid[s][:, :], hs[s][:, :], pgu[s][:, FH:FF], ALU.mult).then_inc(S[done], 1)
                    take(*following(m, u))
                    dve.wait_ge(S["ht"], n + 1)
                    dve.wait_ge(pairs["down_a"][1 - u], m + u)
                    dve.wait_ge(pairs["down_b"][1 - u], m + u)
                    dve.tensor_copy(hidT[:, :, :, :, :].rearrange("p s j h t -> p (s j h t)"), ph[:, :])\
                        .then_inc(S["hTd"], 1)
                    dve.wait_ge(pairs["down_b"][u], m + 1)
                    dve.wait_ge(pairs["stored"][u], m * 32)
                    dve.tensor_copy(y[u][:, 1, :], pd[1][:, :]).then_inc(S["yb"], 1)


def combine(g, tag, r, y_dram, x_dram, out_dram, layer):
    nc, io = g.nc, g.io
    NR = 4
    with ExitStack() as ctx:
        rn = ResidualNorm(g, ctx, tag, x_dram, out_dram, layer, 5, io["ln_ffn_g"][layer], io["ln_ffn_b"][layer])
        rows = [[g.sb(ctx, f"{tag}_r{k}_{b}", [P, D]) for b in range(NR)] for k in range(2)]
        weights = g.sb(ctx, f"{tag}_weights", [P, NT, 2, P])
        py = [g.ps(ctx, f"{tag}_py{i}", [P, D]) for i in range(3)]
        weighed, summed = g.sems(ctx, tag, "weighed", "summed")
        r_in = g.sems(ctx, tag, *[f"r_in{b}" for b in range(NR)])
        block = ctx.enter_context(nc.Block())

        @block.sync
        def _(sp):
            rn.traffic(sp)

        @block.gpsimd
        def _(pool):
            def gather(t):
                if t >= NR:
                    pool.wait_ge(summed, t - NR + 1)
                for k in range(2):
                    pool.indirect_dma_start(out=rows[k][t % NR][:, :], out_offset=None, in_=y_dram,
                                            in_offset=bass.IndirectOffsetOnAxis(ap=r.slot[:, t, k:k + 1], axis=0))\
                        .then_inc(r_in[t % NR], 16)

            for t in range(NR):
                gather(t)
            for t in range(NT):
                if t + NR < NT:
                    gather(t + NR)
                rn.pool(pool, t)

        @block.tensor
        def _(pe):
            rn.gate_rows(pe, py[2])
            pe.wait_ge(weighed, 2 * NT)
            for t in range(NT):
                pe.wait_ge(r_in[t % NR], 32 * (t // NR + 1))
                if t == 2:
                    pe.wait_ge(rn.S["gatec"], 1)
                if t >= 3:
                    pe.wait_ge(rn.S["zmul"], t - 2)
                for half in range(2):
                    for k in range(2):
                        mm = pe.matmul(py[t % 3][:, half * 512:(half + 1) * 512], weights[:, t, k, :],
                                       rows[k][t % NR][:, half * 512:(half + 1) * 512], start=(k == 0), stop=(k == 1))
                mm.then_inc(summed, 1)

        @block.vector
        def _(dve):
            rn.gate_diag(dve)
            for t in range(NT):
                for k in range(2):
                    dve.tensor_scalar(weights[:, t, k, :], g.ident[:, :], r.weight[:, t, k:k + 1], None, ALU.mult)\
                        .then_inc(weighed, 1)
            rn.vector(dve, summed, py)

        @block.scalar
        def _(act):
            rn.gate_copy(act, py[2])
            rn.scalar(act)


def moe(g, tag, x_dram, out_dram, layer):
    first = layer == 0
    if first:
        g.y_dram = g.nc.dram_tensor("expert_rows", [NBLK * P, D], F32).ap()
    with ExitStack() as ctx:
        r = Routing(g, ctx, tag)
        with ExitStack() as hctx:
            modulated(g, hctx, f"{tag}h")
            modulate(g, f"{tag}m", x_dram, layer, 1)
            route(g, f"{tag}r", r, layer, g.y_dram if first else None)
        experts(g, f"{tag}e", r, x_dram, g.y_dram, layer)
        combine(g, f"{tag}c", r, g.y_dram, x_dram, out_dram, layer)


def modulated(g, ctx, tag):
    g.hT = ctx.enter_context(g.nc.sbuf_tensor(f"hT_{tag}", [P, KD, T], F32, side="right"))


def layer_1(g, x2, out):
    nc, io = g.nc, g.io
    x3 = nc.dram_tensor("x3", [T, D], F32).ap()
    with ExitStack() as mixer:
        mixT = g.sb(mixer, "mixT1", [P, RET_MIX // P, T])
        with ExitStack() as hctx:
            modulated(g, hctx, "mix1")
            modulate(g, "m1", x2, 1, 0)
            retention(g, mixT)
        mix_out(g, "mo1", mixT, RET_MIX // P, io["ret_w_out"][0], x2, x3, 1)
    moe(g, "f1", x3, out.rearrange("b s d -> (b s) d"), 1)


def build(nc, io, out):
    g = Program(nc, io)
    x = io["x"].rearrange("b s d -> (b s) d")
    with g.keep:
        constants(g)
        with ExitStack() as mixer:
            hctx = ExitStack()
            modulated(g, hctx, "mix0")
            modulate(g, "m0", x, 0, 0)
            o = Hybrid(g, mixer)
            with ExitStack() as ctx:
                o.attention_inputs(g, ctx)
                hybrid_inputs(g, o)
                attention(g, o)
            with ExitStack() as ctx:
                qkvT = g.sb(ctx, "qkvT", [P, CT, T + 2 * P])
                gdn_convolve(g, qkvT)
                hctx.close()
                delta_rule(g, o, qkvT)
            x1 = nc.dram_tensor("x1", [T, D], F32).ap()
            mix_out(g, "mo0", o.mixT, KD, io["hy_w_out"][0], x, x1, 0)
        x2 = nc.dram_tensor("x2", [T, D], F32).ap()
        moe(g, "f0", x1, x2, 0)
        layer_1(g, x2, out)


_INS = ["x", "c", "positions", "ada_w", "ada_b", "ln_mix_g", "ln_mix_b", "ln_ffn_g", "ln_ffn_b", "hy_w_in",
        "mla_q_norm", "mla_w_uq", "mla_kv_norm", "mla_w_ukv", "gdn_conv_w", "gdn_a_log", "gdn_dt_bias", "gdn_norm",
        "hy_w_out", "ret_w_in", "ret_gn_g", "ret_gn_b", "ret_w_out", "moe_w_group", "moe_b_group", "moe_w_expert",
        "moe_b_expert", "moe_w_gate", "moe_w_up", "moe_w_down"]


def kernel(**inputs):
    import numpy as _np
    import concourse.bacc as _bacc
    from concourse import mybir as _mybir
    from concourse.bass_utils import run_bass_kernel_spmd as _run

    nc = _bacc.Bacc("TRN2", target_bir_lowering=False, num_devices=1)
    arrays, io = {}, {}
    for name in _INS:
        a = _np.ascontiguousarray(inputs[name])
        arrays[f"in_{name}_dram"] = a
        io[name] = nc.dram_tensor(f"in_{name}_dram", a.shape, _mybir.dt.from_np(a.dtype), kind="ExternalInput").ap()
    out = nc.dram_tensor("out_0_dram", (1, T, D), _mybir.dt.float32, kind="ExternalOutput").ap()
    build(nc, io, out)
    r = _run(nc, [arrays], core_ids=[0])
    return r.results[0]["out_0_dram"]
```
